# Optimizing a Trainium2 kernel written in Bass

```python
import jax, jax.numpy as jnp
from jax import lax
import numpy as np

D_MODEL = 1024
BATCH = 1
SEQ = 512
DEPTH = 1

D_MIX = D_MODEL
HEAD_DIM = 64
D_ATTN = D_MIX // 2
N_HEADS = D_ATTN // HEAD_DIM
D_CONV = D_MIX - D_ATTN
D_IN = 3 * D_ATTN + 2 * D_CONV
CONV_WIDTH = 31
DILATED_BRANCHES = ((128, 1), (512, 4), (2048, 16))
ATTN_BLOCK = 128
N_GROUPS = 4
EXPERTS_PER_GROUP = 8
N_EXPERTS = N_GROUPS * EXPERTS_PER_GROUP
TOP_K_INNER = 2
D_EXPERT = D_MODEL // 2
MOE_BLOCK = 256
NORM_EPS = 1e-6
N_MOD = 6


def rms_norm(x, g):
    x32 = x.astype(jnp.float32)
    y = x32 * lax.rsqrt(jnp.mean(x32 * x32, axis=-1, keepdims=True) + NORM_EPS)
    return (y * g.astype(jnp.float32)).astype(x.dtype)

def layer_norm(x, g, b):
    x32 = x.astype(jnp.float32)
    mu = jnp.mean(x32, axis=-1, keepdims=True)
    var = jnp.mean(jnp.square(x32 - mu), axis=-1, keepdims=True)
    y = (x32 - mu) * lax.rsqrt(var + NORM_EPS)
    return (y * g.astype(jnp.float32) + b.astype(jnp.float32)).astype(x.dtype)

def alibi_slopes(n_heads):
    return jnp.asarray(2.0 ** (-8.0 * np.arange(1, n_heads + 1) / n_heads), dtype=jnp.float32)

def dilated_branch(q, k, v, slopes, window, dil):
    B, H, S, Dh = q.shape
    L = S // dil
    n_back = window // dil
    nb = -(-L // ATTN_BLOCK)
    Lp = nb * ATTN_BLOCK

    def to_blocks(t):
        t = t.reshape(B, H, L, dil, Dh).transpose(0, 1, 3, 2, 4)
        t = jnp.pad(t, ((0, 0), (0, 0), (0, 0), (0, Lp - L), (0, 0)))
        return t.reshape(B, H, dil, nb, ATTN_BLOCK, Dh)

    def with_prev(t):
        prev = jnp.pad(t[:, :, :, :-1], ((0, 0), (0, 0), (0, 0), (1, 0), (0, 0), (0, 0)))
        return jnp.concatenate([prev, t], axis=4)

    qb = to_blocks(q)
    kc = with_prev(to_blocks(k))
    vc = with_prev(to_blocks(v))
    s = jnp.einsum('bhrnqd,bhrnkd->bhrnqk', qb, kc,
                   preferred_element_type=jnp.float32) * (HEAD_DIM ** -0.5)
    qi = np.arange(ATTN_BLOCK)[:, None] + ATTN_BLOCK
    ki = np.arange(2 * ATTN_BLOCK)[None, :]
    delta = qi - ki
    blk_ok = (np.arange(nb)[:, None, None] > 0) | (ki[None] >= ATTN_BLOCK)
    valid = (delta >= 0) & (delta <= n_back) & blk_ok
    bias = -slopes[:, None, None] * jnp.asarray(delta * dil, dtype=jnp.float32)
    s = s + bias[None, :, None, None]
    s = jnp.where(valid[None, None, None], s, -jnp.inf)
    m = jnp.max(s, axis=-1)
    p = jnp.exp(s - m[..., None])
    l = jnp.sum(p, axis=-1)
    o = jnp.einsum('bhrnqk,bhrnkd->bhrnqd', p, vc.astype(jnp.float32))

    def from_blocks(t, trailing):
        t = t.reshape((B, H, dil, Lp) + trailing)[:, :, :, :L]
        t = jnp.moveaxis(t, 2, 3)
        return t.reshape((B, H, S) + trailing)

    return from_blocks(o, (Dh,)), from_blocks(m, ()), from_blocks(l, ())

def dilated_attention(q, k, v, slopes):
    outs = [dilated_branch(q, k, v, slopes, w, d) for (w, d) in DILATED_BRANCHES]
    m_all = jnp.stack([m for (_, m, _) in outs])
    m_max = jnp.max(m_all, axis=0)
    num = 0.0
    den = 0.0
    for (o, m, l) in outs:
        a = jnp.exp(m - m_max)
        num = num + a[..., None] * o
        den = den + a * l
    return num / den[..., None]

def conformer_conv(a, b, conv_w, conv_b, ln_g, ln_b):
    u = a * jax.nn.sigmoid(b)
    y = lax.conv_general_dilated(u, conv_w[:, None, :].astype(u.dtype), window_strides=(1,),
                                 padding=[(CONV_WIDTH - 1, 0)],
                                 dimension_numbers=('NWC', 'WIO', 'NWC'),
                                 feature_group_count=D_CONV) + conv_b
    return jax.nn.silu(layer_norm(y, ln_g, ln_b))

def hier_moe(h, w_rg, b_rg, w_re, b_re, w_gate, w_up, w_down):
    B, S, D = h.shape
    T = B * S
    hf = h.reshape(T, D)
    tix = jnp.arange(T)
    g_logits = (hf @ w_rg + b_rg).astype(jnp.float32)
    g_prob = jax.nn.softmax(g_logits, axis=-1)
    grp = jnp.argmax(g_logits, axis=-1)
    p_grp = g_prob[tix, grp]
    e_logits = (hf @ w_re + b_re).astype(jnp.float32).reshape(T, N_GROUPS, EXPERTS_PER_GROUP)
    e_logits = e_logits[tix, grp]
    top_val, top_idx = lax.top_k(e_logits, TOP_K_INNER)
    top_w = jax.nn.softmax(top_val, axis=-1) * p_grp[:, None]

    A = T * TOP_K_INNER
    eid = (grp[:, None] * EXPERTS_PER_GROUP + top_idx).reshape(A).astype(jnp.int32)
    tok = jnp.repeat(tix, TOP_K_INNER).astype(jnp.int32)
    wts = top_w.reshape(A)
    order = jnp.argsort(eid)
    s_eid, s_tok, s_w = eid[order], tok[order], wts[order]
    counts = jnp.bincount(eid, length=N_EXPERTS)
    start = jnp.cumsum(counts) - counts
    padded = ((counts + MOE_BLOCK - 1) // MOE_BLOCK) * MOE_BLOCK
    pad_end = jnp.cumsum(padded)
    pad_start = pad_end - padded
    dest = pad_start[s_eid] + (jnp.arange(A) - start[s_eid])
    P = (-(-A // MOE_BLOCK)) * MOE_BLOCK + N_EXPERTS * MOE_BLOCK
    nblk = P // MOE_BLOCK
    buf_tok = jnp.full((P,), T, dtype=jnp.int32).at[dest].set(s_tok)
    buf_w = jnp.zeros((P,), dtype=jnp.float32).at[dest].set(s_w)
    blk_eid = jnp.clip(jnp.searchsorted(pad_end, jnp.arange(nblk) * MOE_BLOCK, side='right'),
                       0, N_EXPERTS - 1)
    x_pad = jnp.concatenate([hf, jnp.zeros((1, D), hf.dtype)], axis=0)
    xb = x_pad[buf_tok].reshape(nblk, MOE_BLOCK, D)

    def expert_block(args):
        xblk, e = args
        return (jax.nn.silu(xblk @ w_gate[e]) * (xblk @ w_up[e])) @ w_down[e]

    yb = lax.map(expert_block, (xb, blk_eid)).reshape(P, D)
    out = jnp.zeros((T + 1, D), yb.dtype).at[buf_tok].add(yb * buf_w[:, None].astype(yb.dtype))[:T]
    return out.reshape(B, S, D).astype(h.dtype)

def first_inputs(seed: int = 0) -> dict:
    key = jax.random.key(seed)
    ks = jax.random.split(key, 24)
    f32 = jnp.float32
    nrm = lambda k, shape, s: jax.random.normal(k, shape, f32) * s
    L = DEPTH
    return {
        "x": nrm(ks[0], (BATCH, SEQ, D_MODEL), 1.0),
        "c": nrm(ks[1], (BATCH, D_MODEL), 1.0),
        "w_mod": nrm(ks[2], (L, D_MODEL, N_MOD * D_MODEL), 0.5 * D_MODEL ** -0.5),
        "b_mod": nrm(ks[3], (L, N_MOD * D_MODEL), 0.01),
        "g_norm1": 1.0 + nrm(ks[4], (L, D_MODEL), 0.02),
        "w_in": nrm(ks[5], (L, D_MODEL, D_IN), D_MODEL ** -0.5),
        "conv_w": nrm(ks[6], (L, CONV_WIDTH, D_CONV), CONV_WIDTH ** -0.5),
        "conv_b": nrm(ks[7], (L, D_CONV), 0.01),
        "conv_ln_g": 1.0 + nrm(ks[8], (L, D_CONV), 0.02),
        "conv_ln_b": nrm(ks[9], (L, D_CONV), 0.01),
        "w_out": nrm(ks[10], (L, D_MIX, D_MODEL), D_MIX ** -0.5),
        "g_norm2": 1.0 + nrm(ks[11], (L, D_MODEL), 0.02),
        "w_router_group": nrm(ks[12], (L, D_MODEL, N_GROUPS), D_MODEL ** -0.5),
        "b_router_group": nrm(ks[13], (L, N_GROUPS), 0.01),
        "w_router_expert": nrm(ks[14], (L, D_MODEL, N_EXPERTS), D_MODEL ** -0.5),
        "b_router_expert": nrm(ks[15], (L, N_EXPERTS), 0.01),
        "w_exp_gate": nrm(ks[16], (L, N_EXPERTS, D_MODEL, D_EXPERT), D_MODEL ** -0.5),
        "w_exp_up": nrm(ks[17], (L, N_EXPERTS, D_MODEL, D_EXPERT), D_MODEL ** -0.5),
        "w_exp_down": nrm(ks[18], (L, N_EXPERTS, D_EXPERT, D_MODEL), D_EXPERT ** -0.5),
        "g_final": 1.0 + nrm(ks[19], (D_MODEL,), 0.02),
    }

def first_block(x, c, w_mod, b_mod, g_norm1, w_in, conv_w, conv_b, conv_ln_g, conv_ln_b, w_out,
              g_norm2, w_router_group, b_router_group, w_router_expert, b_router_expert,
              w_exp_gate, w_exp_up, w_exp_down, g_final):
    B, S, D = x.shape
    slopes = alibi_slopes(N_HEADS)
    c_act = jax.nn.silu(c)

    def split_heads(t):
        return t.reshape(B, S, N_HEADS, HEAD_DIM).transpose(0, 2, 1, 3)

    for l in range(DEPTH):
        mod = c_act @ w_mod[l] + b_mod[l]
        sh1, sc1, gt1, sh2, sc2, gt2 = jnp.split(mod[:, None, :], N_MOD, axis=-1)

        h = rms_norm(x, g_norm1[l]) * (1.0 + sc1) + sh1
        u = h @ w_in[l]
        q, k, v, ga, gb = jnp.split(
            u, [D_ATTN, 2 * D_ATTN, 3 * D_ATTN, 3 * D_ATTN + D_CONV], axis=-1)
        attn = dilated_attention(split_heads(q), split_heads(k), split_heads(v), slopes)
        attn = attn.transpose(0, 2, 1, 3).reshape(B, S, D_ATTN).astype(x.dtype)
        conv = conformer_conv(ga, gb, conv_w[l], conv_b[l], conv_ln_g[l], conv_ln_b[l])
        mix = jnp.concatenate([attn, conv], axis=-1) @ w_out[l]
        x = x + gt1 * mix

        h2 = rms_norm(x, g_norm2[l]) * (1.0 + sc2) + sh2
        x = x + gt2 * hier_moe(h2, w_router_group[l], b_router_group[l], w_router_expert[l],
                               b_router_expert[l], w_exp_gate[l], w_exp_up[l], w_exp_down[l])

    return rms_norm(x, g_final)


CHUNK = 64
Q_BLOCK = 128
N_META = 16
SB_HEADS = 8
SB_HEAD_DIM = 64
GLA_HEADS = 4
GLA_HEAD_DK = 128
GLA_HEAD_DV = 256
GATE_RANK = 16
GATE_TAU = 16.0
D_FF = 2816
CONV_W = 3
N_BRANCHES = 2
EPS = 1e-6

SB_WIDTH = SB_HEADS * SB_HEAD_DIM
GLA_K_WIDTH = GLA_HEADS * GLA_HEAD_DK
GLA_V_WIDTH = GLA_HEADS * GLA_HEAD_DV
IN_WIDTHS = (SB_WIDTH, SB_WIDTH, SB_WIDTH, GLA_K_WIDTH, GLA_K_WIDTH, GLA_V_WIDTH, GLA_V_WIDTH, GATE_RANK, N_BRANCHES * D_MODEL)
IN_TOTAL = 3 * SB_WIDTH + 2 * GLA_K_WIDTH + 2 * GLA_V_WIDTH + GATE_RANK + N_BRANCHES * D_MODEL


def _rmsnorm(x, g):
    xf = x.astype(jnp.float32)
    y = xf * lax.rsqrt(jnp.mean(xf * xf, axis=-1, keepdims=True) + EPS)
    return (y * g.astype(jnp.float32)).astype(x.dtype)

def _split_cols(a, widths):
    outs, start = [], 0
    for w in widths:
        outs.append(a[..., start:start + w])
        start += w
    return outs

def _heads(a, n_heads):
    b, l, _ = a.shape
    return a.reshape(b, l, n_heads, -1).transpose(0, 2, 1, 3)

def _stick_breaking(q, k, v):
    b, h, lp, dh = q.shape
    nb = lp // Q_BLOCK
    scale = dh ** -0.5
    kpos = jnp.arange(lp)
    qb = q.reshape(b, h, nb, Q_BLOCK, dh).transpose(2, 0, 1, 3, 4)

    def block(args):
        qi, i = args
        z = jnp.einsum('bhqd,bhkd->bhqk', qi, k).astype(jnp.float32) * scale
        qpos = i * Q_BLOCK + jnp.arange(Q_BLOCK)
        strict = kpos[None, :] < qpos[:, None]
        u = jnp.where(strict, jax.nn.log_sigmoid(-z), 0.0)
        tail = lax.cumsum(u, axis=3, reverse=True) - u
        w = jnp.where(strict, jnp.exp(jax.nn.log_sigmoid(z) + tail), 0.0)
        return jnp.einsum('bhqk,bhkd->bhqd', w.astype(v.dtype), v)

    out = lax.map(block, (qb, jnp.arange(nb)))
    return out.transpose(1, 2, 0, 3, 4).reshape(b, h, lp, dh)

def _gla(q, k, v, g):
    b, h, lp, dk = q.shape
    dv = v.shape[-1]
    nc = lp // CHUNK

    def to_chunks(a):
        return a.reshape(b, h, nc, CHUNK, a.shape[-1]).transpose(2, 0, 1, 3, 4)

    qc, kc, vc, gc = to_chunks(q), to_chunks(k), to_chunks(v), to_chunks(g)
    causal = jnp.tril(jnp.ones((CHUNK, CHUNK), dtype=bool))

    def step(state, inp):
        qi, ki, vi, gi = inp
        cum = jnp.cumsum(gi, axis=2)
        diff = cum[:, :, :, None, :] - cum[:, :, None, :, :]
        decay = jnp.exp(jnp.where(causal[None, None, :, :, None], diff, -jnp.inf))
        att = jnp.einsum('bhtd,bhsd,bhtsd->bhts', qi, ki, decay)
        o = jnp.einsum('bhts,bhsv->bhtv', att, vi) + jnp.einsum('bhtd,bhdv->bhtv', qi * jnp.exp(cum), state)
        last = cum[:, :, -1:, :]
        state = jnp.exp(last[:, :, 0, :])[..., None] * state + jnp.einsum('bhsd,bhsv->bhdv', ki * jnp.exp(last - cum), vi)
        return state, o

    state0 = jnp.zeros((b, h, dk, dv), jnp.float32)
    _, oc = lax.scan(step, state0, (qc, kc, vc, gc))
    return oc.transpose(1, 2, 0, 3, 4).reshape(b, h, lp, dv)

def _causal_dwconv(a, w, bias):
    a_p = jnp.pad(a, ((0, 0), (CONV_W - 1, 0), (0, 0)))
    y = lax.conv_general_dilated(a_p, w[:, None, :].astype(a.dtype), window_strides=(1,), padding='VALID',
                                 dimension_numbers=('NWC', 'WIO', 'NWC'), feature_group_count=a.shape[-1])
    return y + bias.astype(a.dtype)

def second_inputs(seed: int = 0) -> dict:
    key = jax.random.key(seed)
    ks = jax.random.split(key, 20)
    f32 = jnp.float32

    def nrm(k, shape, scale):
        return jax.random.normal(k, shape, f32) * scale

    def gain(k, n):
        return 1.0 + 0.02 * jax.random.normal(k, (DEPTH, n), f32)

    return {
        "x": nrm(ks[0], (BATCH, SEQ, D_MODEL), 1.0),
        "meta_tokens": nrm(ks[1], (N_META, D_MODEL), 1.0),
        "norm_mix_pre": gain(ks[2], D_MODEL),
        "w_in": nrm(ks[3], (DEPTH, D_MODEL, IN_TOTAL), D_MODEL ** -0.5),
        "w_gk_up": nrm(ks[4], (DEPTH, GATE_RANK, GLA_K_WIDTH), GATE_RANK ** -0.5),
        "b_gk": nrm(ks[5], (DEPTH, GLA_K_WIDTH), 0.1),
        "gla_head_norm": gain(ks[6], GLA_HEAD_DV),
        "w_sb_out": nrm(ks[7], (DEPTH, SB_WIDTH, D_MODEL), SB_WIDTH ** -0.5),
        "w_gla_out": nrm(ks[8], (DEPTH, GLA_V_WIDTH, D_MODEL), GLA_V_WIDTH ** -0.5),
        "w_o": nrm(ks[9], (DEPTH, D_MODEL, D_MODEL), D_MODEL ** -0.5),
        "norm_mix_post": gain(ks[10], D_MODEL),
        "norm_ffn_pre": gain(ks[11], D_MODEL),
        "w_ffn_up": nrm(ks[12], (DEPTH, D_MODEL, D_FF), D_MODEL ** -0.5),
        "w_ffn_gate": nrm(ks[13], (DEPTH, D_MODEL, D_FF), D_MODEL ** -0.5),
        "conv_w": nrm(ks[14], (DEPTH, CONV_W, D_FF), CONV_W ** -0.5),
        "conv_b": nrm(ks[15], (DEPTH, D_FF), 0.02),
        "w_ffn_down": nrm(ks[16], (DEPTH, D_FF, D_MODEL), D_FF ** -0.5),
        "norm_ffn_post": gain(ks[17], D_MODEL),
    }

def second_block(x, meta_tokens, norm_mix_pre, w_in, w_gk_up, b_gk, gla_head_norm, w_sb_out, w_gla_out, w_o,
              norm_mix_post, norm_ffn_pre, w_ffn_up, w_ffn_gate, conv_w, conv_b, w_ffn_down, norm_ffn_post):
    b, s, _ = x.shape
    L = s + N_META
    Lp = -(-L // Q_BLOCK) * Q_BLOCK
    meta = jnp.broadcast_to(meta_tokens[None].astype(x.dtype), (b, N_META, D_MODEL))
    h = jnp.concatenate([meta, x], axis=1)

    for l in range(DEPTH):
        hn = _rmsnorm(h, norm_mix_pre[l])
        hn_p = jnp.pad(hn, ((0, 0), (0, Lp - L), (0, 0)))
        proj = hn_p @ w_in[l]
        sb_q, sb_k, sb_v, g_q, g_k, g_v, g_r, g_lr, merge = _split_cols(proj, IN_WIDTHS)

        sb = _stick_breaking(_heads(sb_q, SB_HEADS), _heads(sb_k, SB_HEADS), _heads(sb_v, SB_HEADS))
        sb = sb.transpose(0, 2, 1, 3).reshape(b, Lp, SB_WIDTH)[:, :L]

        glog = jax.nn.log_sigmoid((g_lr @ w_gk_up[l] + b_gk[l]).astype(jnp.float32)) / GATE_TAU
        gq = _heads(g_q, GLA_HEADS).astype(jnp.float32) * (GLA_HEAD_DK ** -0.5)
        gk = _heads(g_k, GLA_HEADS).astype(jnp.float32)
        gv = _heads(g_v, GLA_HEADS).astype(jnp.float32)
        o = _gla(gq, gk, gv, _heads(glog, GLA_HEADS))
        o = _rmsnorm(o, gla_head_norm[l])
        o = o.transpose(0, 2, 1, 3).reshape(b, Lp, GLA_V_WIDTH)[:, :L].astype(h.dtype)
        o = o * jax.nn.silu(g_r[:, :L])

        gates = jax.nn.sigmoid(merge[:, :L])
        gate_sb, gate_gla = gates[..., :D_MODEL], gates[..., D_MODEL:]
        mix = (gate_sb * (sb @ w_sb_out[l]) + gate_gla * (o @ w_gla_out[l])) @ w_o[l]
        h = h + _rmsnorm(mix, norm_mix_post[l])

        hn = _rmsnorm(h, norm_ffn_pre[l])
        up = hn @ w_ffn_up[l]
        act = jax.nn.gelu(_causal_dwconv(up, conv_w[l], conv_b[l]), approximate=True)
        ffn = (act * (hn @ w_ffn_gate[l])) @ w_ffn_down[l]
        h = h + _rmsnorm(ffn, norm_ffn_post[l])

    return h[:, N_META:]


def setup_inputs(seed=0):
    out = dict(first_inputs(seed))
    for name, value in second_inputs(seed + 1).items():
        if name != "x":
            out[name + "_2"] = value
    return out


def reference(
    x, c, w_mod, b_mod, g_norm1, w_in, conv_w, conv_b, conv_ln_g, conv_ln_b, w_out, g_norm2,
    w_router_group, b_router_group, w_router_expert, b_router_expert, w_exp_gate, w_exp_up,
    w_exp_down, g_final, meta_tokens_2, norm_mix_pre_2, w_in_2, w_gk_up_2, b_gk_2,
    gla_head_norm_2, w_sb_out_2, w_gla_out_2, w_o_2, norm_mix_post_2, norm_ffn_pre_2,
    w_ffn_up_2, w_ffn_gate_2, conv_w_2, conv_b_2, w_ffn_down_2, norm_ffn_post_2,
):
    x = first_block(
        x, c, w_mod, b_mod, g_norm1, w_in, conv_w, conv_b, conv_ln_g, conv_ln_b, w_out, g_norm2,
        w_router_group, b_router_group, w_router_expert, b_router_expert, w_exp_gate, w_exp_up,
        w_exp_down, g_final,
    )
    return second_block(
        x, meta_tokens_2, norm_mix_pre_2, w_in_2, w_gk_up_2, b_gk_2, gla_head_norm_2,
        w_sb_out_2, w_gla_out_2, w_o_2, norm_mix_post_2, norm_ffn_pre_2, w_ffn_up_2,
        w_ffn_gate_2, conv_w_2, conv_b_2, w_ffn_down_2, norm_ffn_post_2,
    )


_drawn_inputs = setup_inputs


def setup_inputs(seed=0):
    import zlib

    import numpy as np

    out = dict(_drawn_inputs(seed))
    spreads = {}
    factors = {'b_mod': 2.709,
     'g_norm1': 5.246,
     'conv_b': 8.0,
     'conv_ln_g': 7.401,
     'conv_ln_b': 7.242,
     'g_norm2': 3.135,
     'b_router_group': 8.0,
     'b_router_expert': 7.546,
     'gla_head_norm_2': 4.907,
     'norm_mix_post_2': 3.483,
     'norm_ffn_pre_2': 3.2,
     'conv_b_2': 5.098,
     'norm_ffn_post_2': 4.93}
    for name, (base, spread) in spreads.items():
        noise = np.random.default_rng([zlib.crc32(name.encode()), seed]).standard_normal(out[name].shape)
        drawn = base * np.exp(spread * noise) if base else spread * noise
        out[name] = __import__('jax').numpy.asarray(drawn.astype(out[name].dtype))
    for name, factor in factors.items():
        out[name] = (out[name] * factor).astype(out[name].dtype)
    return out
```

```python
from contextlib import ExitStack

import concourse.bass as bass
from concourse import mybir

ALU = mybir.AluOpType
ACT = mybir.ActivationFunctionType
F32 = mybir.dt.float32
I32 = mybir.dt.int32
U32 = mybir.dt.uint32
AX_X = mybir.AxisListType.X

P = 128
D = 1024
KT = D // P
SEQ = 512
TT = SEQ // P
META = 16
L2 = SEQ + META
HALF = L2 // 2
CHUNK = 4096
SLOTS = 4
EPS = 1e-6
NEG = -1.0e30

HEADS, HD = 8, 64
TAPS = 31
CM = 512 // P
PE_TAPS = 16
SLOPES = [2.0 ** (-8.0 * (h + 1) / HEADS) for h in range(HEADS)]

GROUPS, PER_GROUP, EXPERTS, FE = 4, 8, 32, 512
BLOCKS = EXPERTS + (2 * SEQ - EXPERTS) // P
BLOCKS += BLOCKS % 2
TABLE = BLOCKS + 2

GH, DK, DV = 4, 128, 256
LEVELS = 7
FF = 2816
FM = FF // P
COMPUTE_SEMAPHORES = range(140, 256)


class Steps:

    def __init__(self, eng, sem):
        self.eng, self.sem, self.n = eng, sem, 0

    def __call__(self, ins):
        self.n += 1
        ins.then_inc(self.sem, 1)
        self.eng.wait_ge(self.sem, self.n)


class Stream:

    def __init__(self, ring, arrived, chunks):
        self.ring, self.arrived, self.chunks = ring, arrived, chunks
        self.issued, self.readers, self.phase_start = 0, {}, 0

    def load_until(self, sp, n):
        while self.issued < min(n, len(self.chunks)):
            c = self.issued
            if c - SLOTS in self.readers:
                sem, value = self.readers[c - SLOTS]
                sp.wait_ge(sem, value)
            dst, src = self.chunks[c](self.ring[:, c % SLOTS, :])
            sp.dma_start(dst, src).then_inc(self.arrived[c % SLOTS], 16)
            self.issued += 1

    def use(self, eng, n):
        eng.wait_ge(self.arrived[n % SLOTS], 16 * (n // SLOTS + 1))
        return self.ring[:, n % SLOTS, :]

    def read_by(self, n, sem, value):
        self.readers[n] = (sem, value)

    def new_phase(self):
        self.readers = {}


def columns_chunk(w, c0, width=512):
    def make(slot):
        dst = slot[:, 0:KT * width].rearrange("p (k n) -> p k n", k=KT)
        return dst, w[:, c0:c0 + width].rearrange("(k p) n -> p k n", p=P)
    return make


def rows_chunk(w, r0, rows):
    def make(slot):
        k = rows // P
        dst = slot[:, 0:k * D].rearrange("p (k n) -> p k n", k=k)
        return dst, w[r0:r0 + rows, :].rearrange("(k p) n -> p k n", p=P)
    return make


def build_program(nc, a, out):
    ctx = ExitStack()
    with ctx:
        floats = 52000
        arena = ctx.enter_context(nc.sbuf_tensor("arena", [P, floats], F32))
        psum = ctx.enter_context(nc.psum_tensor("psum", [P, 8, 512], F32))
        scratch = {
            "h2": nc.dram_tensor("h2_rows", (SEQ, D), F32, kind="Internal").ap(),
            "y": nc.dram_tensor("expert_rows", ((BLOCKS + 1) * P, D), F32, kind="Internal").ap(),
            "slot_token": nc.dram_tensor("slot_token", (TABLE * P, 1), I32, kind="Internal").ap(),
        }
        place = [0]

        def region(n):
            place[0] += n
            assert place[0] <= floats, place[0]
            return arena[:, place[0] - n:place[0]]

        ring6 = region(6 * CHUNK)
        ring = ring6.rearrange("p (s n) -> p s n", s=6)
        spare = ring6[:, SLOTS * CHUNK:6 * CHUNK]
        ident = region(P)
        ones = region(P)
        before = region(P)
        upto = region(P)
        future = region(P)
        cols1 = region(72)
        convw = region(TAPS * CM)
        convw2 = region(3 * FM)
        small = region(640)
        res = region(TT * D).rearrange("p (t n) -> p t n", t=TT)
        meta = region(D)
        base = place[0]

        counter = [COMPUTE_SEMAPHORES.start]

        def semaphores(cx):
            def sem(name):
                counter[0] += 1
                return cx.enter_context(nc.semaphore(name, num=counter[0] - 1))
            return sem, lambda name: cx.enter_context(nc.semaphore(name))

        arrived = [ctx.enter_context(nc.semaphore(f"weights_arrived{i}")) for i in range(SLOTS)]
        arrived2 = [ctx.enter_context(nc.semaphore(f"later_weights_arrived{i}")) for i in range(SLOTS)]

        w_mod, w_in, w_out = a["w_mod"][0], a["w_in"][0], a["w_out"][0]
        mod = lambda c: ("mod", columns_chunk(w_mod, 512 * c))
        win = lambda c: ("win", columns_chunk(w_in, 512 * c))
        plan = [mod(0), mod(1), mod(2), mod(3), win(0), mod(4), win(1), mod(5), win(2), mod(6), mod(7), win(3),
                mod(8), mod(9), win(4), mod(10), mod(11),
                ("wout", columns_chunk(w_out, 0)), ("wout", columns_chunk(w_out, 512))]
        at = {}
        for n, (kind, _) in enumerate(plan):
            at.setdefault(kind, []).append(n)
        first = Stream(ring, arrived, [c for _, c in plan])

        w_in2 = a["w_in_2"][0]
        plan2 = [("proj", columns_chunk(w_in2, 512 * c)) for c in range(9)]
        plan2 += [("mgla", columns_chunk(w_in2, 4624 + 1024)), ("gout", columns_chunk(a["w_gla_out_2"][0], 0)),
                  ("mgla", columns_chunk(w_in2, 4624 + 1536)), ("gout", columns_chunk(a["w_gla_out_2"][0], 512)),
                  ("msb", columns_chunk(w_in2, 4624)), ("msb", columns_chunk(w_in2, 4624 + 512)),
                  ("sbout", rows_chunk(a["w_sb_out_2"][0], 0, 512)),
                  ("wo", columns_chunk(a["w_o_2"][0], 0)), ("wo", columns_chunk(a["w_o_2"][0], 512))]
        for c0 in range(0, FF, 512):
            width = min(512, FF - c0)
            plan2 += [("up", columns_chunk(a["w_ffn_up_2"][0], c0, width)),
                      ("gate", columns_chunk(a["w_ffn_gate_2"][0], c0, width))]
        for r0 in range(0, FF, 512):
            plan2 += [("down", rows_chunk(a["w_ffn_down_2"][0], r0, min(512, FF - r0)))]
        at2 = {}
        for n, (kind, _) in enumerate(plan2):
            at2.setdefault(kind, []).append(n)
        later = Stream(ring, arrived2, [c for _, c in plan2])

        g = dict(semaphores=semaphores, nc=nc, a=a, psum=psum, dram=scratch, ring=ring, spare=spare, ident=ident, ones=ones, before=before,
                 upto=upto, future=future, cols1=cols1, convw=convw, convw2=convw2, small=small, res=res, meta=meta,
                 arena=arena, base=base, first=first, later=later, at=at, at2=at2, out=out, floats=floats)
        prologue(g)
        input_projection(g)
        attention_and_conv(g)
        output_and_routing(g)
        experts(g)
        combine(g)
        nc.sync.sem_clear(COMPUTE_SEMAPHORES)
        nc.all_engine_barrier()
        counter[0] = COMPUTE_SEMAPHORES.start
        second_block(g)


COLS = [("c", 8), ("g_norm1", 8), ("conv_b", 4), ("conv_ln_g", 4), ("conv_ln_b", 4), ("b_gk_2", 4),
        ("gla_head_norm_2", 2), ("norm_mix_pre_2", 8), ("norm_ffn_pre_2", 8), ("conv_b_2", 22)]


def col(g, name):
    at = 0
    for n, k in COLS:
        if n == name:
            return g["cols1"][:, at:at + k]
        at += k


def mod_step(g, dve, step, n, chunk, slot):
    acc = g["modacc"][:, 512 * chunk:512 * chunk + 512]
    w = slot.rearrange("p (k n) -> p k n", k=KT)
    for k in range(KT):
        step(dve.scalar_tensor_tensor(out=acc, in0=w[:, k, :], scalar=g["csil"][:, k:k + 1], in1=acc,
                                      op0=ALU.mult, op1=ALU.add))
    g["first"].read_by(n, step.sem, step.n)


def prologue(g):
    nc, a, psum, base, arena = g["nc"], g["a"], g["psum"], g["base"], g["arena"]
    at, first = g["at"], g["first"]
    g["modacc"] = modacc = arena[:, base:base + 6144]
    base2 = base + 6144
    g["hT"] = hT = arena[:, base2:base2 + 4096].rearrange("p (k n) -> p k n", k=KT)
    spare, small = g["spare"], g["small"]
    rows1, rows2, rows3 = spare[:, 0:P], spare[:, P:2 * P], spare[:, 2 * P:3 * P]
    squares = spare[:, 512:512 + D]
    xn = spare[:, 2048:2048 + 4096].rearrange("p (t n) -> p t n", t=TT)
    g["csil"] = csil = small[:, 0:8]
    ss, rstd, A, modc = small[:, 8:12], small[:, 12:16], small[:, 16:24], small[:, 24:40]
    cbar, ident, ones = ExitStack(), g["ident"], g["ones"]
    res = g["res"]
    with cbar:
        sem, dma_sem = g["semaphores"](cbar)
        params, x_in, bias_in = dma_sem("params_loaded"), dma_sem("x_loaded"), dma_sem("mod_bias_loaded")
        built, zeroed = sem("constants_built"), sem("mod_sums_zeroed")
        act_step, dve_step = sem("p0_act_step"), sem("p0_dve_step")
        cols_ps, cols_sb, c_ready = sem("columns_in_psum"), sem("columns_in_sbuf"), sem("silu_c_ready")
        ssq, var, root, normed = sem("x_squares"), sem("x_variance"), sem("x_root"), sem("x_normed")
        mod_sum, mod_ps, scale_ok = sem("mod_sums_ready"), sem("mod_columns_in_psum"), sem("scale_ready")
        xT_ps, xT_sb = sem("xT_in_psum"), sem("hT_ready")
        block = cbar.enter_context(nc.Block())

        @block.gpsimd
        def _(pool):
            step = Steps(pool, built)
            step(pool.memset(g["ident"], 0.0))
            step(pool.memset(g["ones"], 1.0))
            step(pool.memset(g["future"], 0.0))
            step(pool.affine_select(out=g["ident"], in_=g["ident"], compare_op=ALU.not_equal, fill=1.0, base=0,
                                    pattern=[[-1, P]], channel_multiplier=1))
            pool.memset(modacc, 0.0).then_inc(zeroed, 1)
            step(pool.affine_select(out=g["before"], in_=g["ones"], compare_op=ALU.is_gt, fill=0.0, base=0,
                                    pattern=[[1, P]], channel_multiplier=-1))
            step(pool.affine_select(out=g["upto"], in_=g["ones"], compare_op=ALU.is_ge, fill=0.0, base=0,
                                    pattern=[[-1, P]], channel_multiplier=1))
            step(pool.affine_select(out=g["future"], in_=g["future"], compare_op=ALU.is_gt, fill=NEG, base=0,
                                    pattern=[[1, P]], channel_multiplier=-1))

        n_params = len(COLS) + 2

        @block.scalar
        def _(act):
            r = 0
            for name, k in COLS:
                src = a[name] if name in ("c",) else a[name]
                src = src.rearrange("a (k p) -> (a k) p", p=P)
                act.dma_start(rows1[r:r + k, :], src).then_inc(params, 16)
                r += k
            act.dma_start(rows2[0:TAPS * CM, :], a["conv_w"][0].rearrange("j (m p) -> (j m) p", p=P)).then_inc(params, 16)
            act.dma_start(rows3[0:3 * FM, :], a["conv_w_2"][0].rearrange("j (m p) -> (j m) p", p=P)).then_inc(params, 16)
            act.wait_ge(x_in, 16)
            for t in range(TT):
                if t:
                    act.wait_ge(ssq, t)
                act.activation(squares, res[:, t, :], ACT.Square, accum_out=ss[:, t:t + 1]).then_inc(ssq, 1)
            act.wait_ge(cols_ps, 3)
            act.activation(g["cols1"], psum[:, 0, 0:72], ACT.Copy).then_inc(cols_sb, 1)
            act.activation(csil, psum[:, 0, 0:8], ACT.Silu).then_inc(c_ready, 1)
            act.activation(g["convw"], psum[:, 1, 0:TAPS * CM], ACT.Copy).then_inc(cols_sb, 1)
            act.activation(g["convw2"], psum[:, 2, 0:3 * FM], ACT.Copy).then_inc(cols_sb, 1)
            act.wait_ge(var, 1)
            act.activation(rstd, rstd, ACT.Sqrt).then_inc(root, 1)
            act.wait_ge(scale_ok, 2)
            for k in range(KT):
                act.wait_ge(xT_ps, k + 1)
                act.activation(hT[:, k, :], psum[:, 4 + k % 4, :], ACT.Identity, bias=modc[:, k:k + 1],
                               scale=A[:, k:k + 1]).then_inc(xT_sb, 1)

        @block.vector
        def _(dve):
            step = Steps(dve, dve_step)
            dve.wait_ge(ssq, TT)
            dve.tensor_scalar(rstd, ss, 1.0 / D, EPS, ALU.mult, ALU.add).then_inc(var, 1)
            dve.wait_ge(root, 1)
            step(dve.reciprocal(rstd, rstd))
            for t in range(TT):
                dve.tensor_scalar(xn[:, t, :], res[:, t, :], rstd[:, t:t + 1], None, ALU.mult).then_inc(normed, 1)
            dve.wait_ge(zeroed, 1)
            dve.wait_ge(bias_in, 16)
            dve.wait_ge(c_ready, 1)
            for c in range(4):
                n = at["mod"][c]
                slot = first.use(dve, n)
                mod_step(g, dve, step, n, c, slot)
            dve.engine_nop().then_inc(mod_sum, 1)
            dve.wait_ge(mod_ps, 1)
            dve.wait_ge(cols_sb, 1)
            dve.tensor_copy(modc, psum[:, 3, 0:16]).then_inc(scale_ok, 1)
            dve.wait_ge(scale_ok, 1)
            dve.scalar_tensor_tensor(out=A, in0=modc[:, 8:16], scalar=1.0, in1=col(g, "g_norm1"), op0=ALU.add,
                                     op1=ALU.mult).then_inc(scale_ok, 1)

        @block.tensor
        def _(pe):
            pe.wait_ge(built, 4)
            pe.wait_ge(params, 16 * n_params)
            for i, (rows, n) in enumerate(((rows1, 72), (rows2, TAPS * CM), (rows3, 3 * FM))):
                pe.transpose(psum[:, i, 0:n], rows[0:n, :], ident[0:n, 0:n]).then_inc(cols_ps, 1)
            pe.wait_ge(mod_sum, 1)
            for c in range(16):
                last = pe.matmul(psum[:, 3, c:c + 1], modacc[:, c * P:(c + 1) * P], ones[:, 0:1], start=True, stop=True)
            last.then_inc(mod_ps, 1)
            pe.wait_ge(normed, TT)
            for k in range(KT):
                if k >= 4:
                    pe.wait_ge(xT_sb, k - 3)
                for t in range(TT):
                    last = pe.transpose(psum[:, 4 + k % 4, t * P:(t + 1) * P], xn[:, t, k * P:(k + 1) * P], ident)
                last.then_inc(xT_ps, 1)

        @block.sync
        def _(sp):
            sp.dma_start(res, a["x"][0].rearrange("(t p) n -> p t n", p=P)).then_inc(x_in, 16)
            sp.wait_ge(zeroed, 1)
            sp.dma_start(modacc[0:1, :], a["b_mod"]).then_inc(bias_in, 16)
            first.load_until(sp, 8)
    first.new_phase()


def input_projection(g):
    nc, a, psum, arena = g["nc"], g["a"], g["psum"], g["arena"]
    at, first, hT, modacc = g["at"], g["first"], g["hT"], g["modacc"]
    b = g["base"] + 6144 + 4096
    g["qT"] = qT = modacc[:, 0:2048].rearrange("p (m n) -> p m n", m=4)
    g["kz"] = kz = arena[:, b:b + 4096].rearrange("p (h n) -> p h n", h=HEADS)
    g["v"] = v = arena[:, b + 4096:b + 6144].rearrange("p (t n) -> p t n", t=TT)
    UW = TAPS - 1 + SEQ
    g["uT"] = uT = arena[:, b + 6144:b + 6144 + CM * UW].rearrange("p (m n) -> p m n", m=CM)
    g["base_tmp"] = b + 6144 + CM * UW
    sg = g["spare"][:, 0:1024].rearrange("p (i n) -> p i n", i=2)
    with ExitStack() as cx:
        sem, dma_sem = g["semaphores"](cx)
        ready, taken = sem("projection_in_psum"), sem("projection_taken")
        zeroed, dve_step, gated = sem("pads_zeroed"), sem("p1_dve_step"), sem("gated")
        mod_all = sem("mod_sums_done")
        rows_ps, rows_sb = sem("mod_rows_in_psum"), sem("mod_rows_ready")
        block = cx.enter_context(nc.Block())

        @block.gpsimd
        def _(pool):
            step = Steps(pool, zeroed)
            for h in range(HEADS):
                lo = 64 * (1 - h % 2)
                step(pool.memset(kz[lo:lo + 64, h, :], 0.0))
            step(pool.memset(uT[:, :, 0:TAPS - 1], 0.0))

        @block.tensor
        def _(pe):
            n = 0
            for c in range(5):
                w = first.use(pe, at["win"][c]).rearrange("p (k n) -> p k n", k=KT)
                for m in range(4):
                    if n >= 4:
                        pe.wait_ge(taken, n - 3)
                    for k in range(KT):
                        if c == 2:
                            lhsT, rhs = hT[:, k, m * P:(m + 1) * P], w[:, k, :]
                        else:
                            lhsT, rhs = w[:, k, m * P:(m + 1) * P], hT[:, k, :]
                        last = pe.matmul(psum[:, n % 4, :], lhsT, rhs, start=(k == 0), stop=(k == KT - 1))
                    last.then_inc(ready, 1)
                    n += 1
                first.read_by(at["win"][c], ready, n)
            pe.wait_ge(mod_all, 1)
            for i in range(8):
                if i >= 4:
                    pe.wait_ge(rows_sb, i - 3)
                s = modacc[:, 2048 + 512 * i:2560 + 512 * i]
                pe.matmul(psum[:, 4 + i % 4, :], g["ones"], s, start=True, stop=True).then_inc(rows_ps, 1)

        @block.scalar
        def _(act):
            n = 0
            for c in range(5):
                for m in range(4):
                    act.wait_ge(ready, n + 1)
                    src = psum[:, n % 4, :]
                    if c == 0:
                        act.activation(qT[:, m, :], src, ACT.Copy, scale=HD ** -0.5).then_inc(taken, 1)
                    elif c == 1:
                        act.activation(kz[0:64, 2 * m, :], src[0:64, :], ACT.Copy)
                        act.activation(kz[64:128, 2 * m + 1, :], src[64:128, :], ACT.Copy).then_inc(taken, 1)
                    elif c == 2:
                        act.activation(v[:, m, :], src, ACT.Copy).then_inc(taken, 1)
                    elif c == 3:
                        act.activation(uT[:, m, TAPS - 1:], src, ACT.Copy).then_inc(taken, 1)
                    else:
                        if m >= 2:
                            act.wait_ge(gated, m - 1)
                        act.activation(sg[:, m % 2, :], src, ACT.Sigmoid).then_inc(taken, 1)
                    n += 1
            for i in range(8):
                act.wait_ge(rows_ps, i + 1)
                act.activation(modacc[:, 2048 + 512 * i:2560 + 512 * i], psum[:, 4 + i % 4, :], ACT.Copy).then_inc(rows_sb, 1)

        @block.vector
        def _(dve):
            step = Steps(dve, dve_step)
            for c in range(4, 12):
                n = at["mod"][c]
                mod_step(g, dve, step, n, c, first.use(dve, n))
            dve.engine_nop().then_inc(mod_all, 1)
            for m in range(CM):
                dve.wait_ge(taken, 17 + m)
                dve.tensor_tensor(uT[:, m, TAPS - 1:], uT[:, m, TAPS - 1:], sg[:, m % 2, :], ALU.mult).then_inc(gated, 1)

        @block.sync
        def _(sp):
            first.load_until(sp, len(first.chunks))
    first.new_phase()


def attention_and_conv(g):
    nc, a, psum, arena, spare = g["nc"], g["a"], g["psum"], g["arena"], g["spare"]
    qT, kz, v, uT = g["qT"], g["kz"], g["v"], g["uT"]
    ident, ones = g["ident"], g["ones"]
    g["mixT"] = mixT = g["hT"]
    PT = spare[:, 0:4096].rearrange("p (i j n) -> p i j n", i=2, j=4)
    sc = spare[:, 4096:5120].rearrange("p (i n) -> p i n", i=2)
    pb = spare[:, 5120:6144].rearrange("p (i n) -> p i n", i=2)
    dist, count = spare[:, 6144:6656], spare[:, 6656:7168]
    diag = spare[:, 7168:8192].rearrange("p (i n) -> p i n", i=8)
    ti = PT[:, 0, 0, :].bitcast(I32)
    tj = PT[:, 0, 1, :].bitcast(I32)
    tf = PT[:, 0, 2, :]
    small = g["small"]
    nmax = small[:, 64:96]
    lsum = small[:, 96:128]
    rl = small[:, 128:160]
    UNITS = HEADS * TT
    DVE_TAPS = TAPS - PE_TAPS
    with ExitStack() as cx:
        sem, dma_sem = g["semaphores"](cx)
        iota_ok, tables = sem("distances_counted"), sem("tables_built")
        s_ps, s_sb, mx, e_ok = sem("scores_in_psum"), sem("scores_ready"), sem("max_ready"), sem("exp_ready")
        pw, pt_ps, pt_sb = sem("probs_ready"), sem("probsT_in_psum"), sem("probsT_ready")
        o_ps, o_sb = sem("attn_in_psum"), sem("attn_ready")
        dstep, cstep = sem("attn_dve_step"), sem("conv_dve_step")
        dg, dg_used = sem("diagonals_built"), sem("diagonals_used")
        c_ps, c_sum = sem("conv_in_psum"), sem("conv_summed")
        mean_ps, cent, sq, var_ps = sem("mean_in_psum"), sem("centred"), sem("squared"), sem("variance_in_psum")
        vr, rt, z_ok, conv_out = sem("variance_ready"), sem("root_ready"), sem("normed"), sem("swish_written")
        block = cx.enter_context(nc.Block())

        @block.gpsimd
        def _(pool):
            pool.iota(ti, [[-1, SEQ]], base=SEQ - P, channel_multiplier=1).then_inc(iota_ok, 1)
            for n in range(CM * PE_TAPS):
                m, j = n // PE_TAPS, n % PE_TAPS
                if n >= 8:
                    om, oj = (n - 8) // PE_TAPS, (n - 8) % PE_TAPS
                    if oj < PE_TAPS - 1:
                        pool.wait_ge(dg_used, om * (PE_TAPS - 1) + oj + 1)
                    else:
                        pool.wait_ge(c_ps, om + 1)
                pool.tensor_scalar(diag[:, n % 8, :], ident, g["convw"][:, j * CM + m:j * CM + m + 1], None,
                                   ALU.mult).then_inc(dg, 1)

        @block.vector
        def _(dve):
            step = Steps(dve, dstep)
            cs = Steps(dve, cstep)
            dve.wait_ge(iota_ok, 1)
            step(dve.tensor_copy(dist, ti))
            step(dve.tensor_scalar(count, dist, 128.0, None, ALU.is_le))
            for low in (3, 15):
                step(dve.tensor_scalar(tj, ti, low, None, ALU.bitwise_and))
                step(dve.tensor_copy(tf, tj))
                step(dve.scalar_tensor_tensor(out=count, in0=tf, scalar=0.0, in1=count, op0=ALU.is_equal, op1=ALU.add))
            step(dve.scalar_tensor_tensor(out=count, in0=dist, scalar=0.0, in1=count, op0=ALU.is_ge, op1=ALU.mult))
            step(dve.tensor_scalar(tf, count, 0.0, -NEG, ALU.is_equal, ALU.mult))
            step(dve.tensor_tensor(dist, dist, tf, ALU.add))
            dve.engine_nop().then_inc(tables, 1)

            def conv_taps(u):
                m, r = u // 8, u % 8
                y = mixT[:, 4 + m, :]
                for j in (2 * r, 2 * r + 1):
                    if j >= DVE_TAPS:
                        continue
                    tap = PE_TAPS + j
                    w = g["convw"][:, tap * CM + m:tap * CM + m + 1]
                    src = uT[:, m, tap:tap + SEQ]
                    if j == 0:
                        cs(dve.tensor_scalar(y, src, w, col(g, "conv_b")[:, m:m + 1], ALU.mult, ALU.add))
                    else:
                        cs(dve.scalar_tensor_tensor(out=y, in0=src, scalar=w, in1=y, op0=ALU.mult, op1=ALU.add))
                if r == 7:
                    dve.wait_ge(c_ps, m + 1)
                    dve.tensor_tensor(y, y, psum[:, 7, :], ALU.add).then_inc(c_sum, 1)

            def scores(u):
                h, i = divmod(u, TT)
                n = (i + 1) * P
                off = SEQ - n
                dve.wait_ge(s_ps, u + 1)
                if u >= 2:
                    dve.wait_ge(e_ok, u - 1)
                dve.scalar_tensor_tensor(out=sc[:, u % 2, 0:n], in0=dist[:, off:], scalar=-SLOPES[h],
                                         in1=psum[:, u % 2, 0:n], op0=ALU.mult, op1=ALU.add).then_inc(s_sb, 1)
                dve.wait_ge(s_sb, u + 1)
                dve.tensor_reduce(nmax[:, u:u + 1], sc[:, u % 2, 0:n], AX_X, ALU.max, negate=True).then_inc(mx, 1)

            def weigh(u):
                h, i = divmod(u, TT)
                n = (i + 1) * P
                off = SEQ - n
                dve.wait_ge(e_ok, u + 1)
                p = pb[:, u % 2, 0:n]
                step(dve.tensor_tensor_reduce(p, p, count[:, off:], 1.0, 0.0, ALU.mult, ALU.add, lsum[:, u:u + 1]))
                step(dve.reciprocal(rl[:, u:u + 1], lsum[:, u:u + 1]))
                dve.tensor_scalar(p, p, rl[:, u:u + 1], None, ALU.mult).then_inc(pw, 1)

            for u in range(UNITS + 1):
                if u < UNITS:
                    scores(u)
                    conv_taps(u)
                if u >= 1:
                    weigh(u - 1)
            dve.wait_ge(mean_ps, 1)
            for m in range(CM):
                dve.scalar_tensor_tensor(out=mixT[:, 4 + m, :], in0=psum[:, 0, :], scalar=-1.0 / 512, in1=mixT[:, 4 + m, :],
                                         op0=ALU.mult, op1=ALU.add).then_inc(cent, 1)
            dve.wait_ge(var_ps, 1)
            dve.tensor_scalar(sc[:, 0, :], psum[:, 1, :], 1.0 / 512, EPS, ALU.mult, ALU.add).then_inc(vr, 1)
            dve.wait_ge(rt, 1)
            step(dve.reciprocal(sc[:, 1, :], sc[:, 1, :]))
            dve.wait_ge(cent, CM)
            for m in range(CM):
                dve.tensor_tensor(mixT[:, 4 + m, :], mixT[:, 4 + m, :], sc[:, 1, :], ALU.mult).then_inc(z_ok, 1)

        @block.scalar
        def _(act):
            def exps(u):
                n = (u % TT + 1) * P
                act.wait_ge(mx, u + 1)
                if u >= 2:
                    act.wait_ge(pt_ps, u - 1)
                act.activation(pb[:, u % 2, 0:n], sc[:, u % 2, 0:n], ACT.Exp, bias=nmax[:, u:u + 1]).then_inc(e_ok, 1)

            def take_probs(u):
                h, i = divmod(u, TT)
                act.wait_ge(pt_ps, u + 1)
                if h >= 2:
                    act.wait_ge(o_ps, h - 1)
                src = psum[:, 2 + u % 2, 0:(i + 1) * P].rearrange("p (j n) -> p j n", j=i + 1)
                act.activation(PT[:, h % 2, 0:i + 1, i * P:(i + 1) * P], src, ACT.Copy).then_inc(pt_sb, 1)

            def take_out(h):
                act.wait_ge(o_ps, h + 1)
                lo = 64 * (h % 2)
                act.activation(mixT[lo:lo + 64, h // 2, :], psum[0:64, 4 + h % 2, :], ACT.Copy).then_inc(o_sb, 1)

            act.wait_ge(tables, 1)
            for u in range(UNITS + 2):
                if u < UNITS:
                    exps(u)
                if u >= 2:
                    take_probs(u - 2)
                    if (u - 2) % TT == 1 and u - 2 > TT:
                        take_out((u - 2) // TT - 1)
            take_out(HEADS - 1)
            for m in range(CM):
                act.wait_ge(cent, m + 1)
                act.activation(PT[:, 0, m, :], mixT[:, 4 + m, :], ACT.Square).then_inc(sq, 1)
            act.wait_ge(vr, 1)
            act.activation(sc[:, 1, :], sc[:, 0, :], ACT.Sqrt).then_inc(rt, 1)
            for m in range(CM):
                act.wait_ge(z_ok, m + 1)
                act.activation(mixT[:, 4 + m, :], mixT[:, 4 + m, :], ACT.Silu, bias=col(g, "conv_ln_b")[:, m:m + 1],
                               scale=col(g, "conv_ln_g")[:, m:m + 1]).then_inc(conv_out, 1)

        @block.tensor
        def _(pe):
            def scores(u):
                h, i = divmod(u, TT)
                if u >= 2:
                    pe.wait_ge(s_sb, u - 1)
                pe.matmul(psum[:, u % 2, 0:(i + 1) * P], qT[:, h // 2, i * P:(i + 1) * P], kz[:, h, 0:(i + 1) * P],
                          start=True, stop=True).then_inc(s_ps, 1)

            def turn(u):
                h, i = divmod(u, TT)
                pe.wait_ge(pw, u + 1)
                if u >= 2:
                    pe.wait_ge(pt_sb, u - 1)
                for j in range(i + 1):
                    last = pe.transpose(psum[:, 2 + u % 2, j * P:(j + 1) * P], pb[:, u % 2, j * P:(j + 1) * P], ident)
                last.then_inc(pt_ps, 1)

            def values(h):
                pe.wait_ge(pt_sb, TT * (h + 1))
                if h >= 2:
                    pe.wait_ge(o_sb, h - 1)
                for j in range(TT):
                    last = pe.matmul(psum[0:64, 4 + h % 2, j * P:], v[:, j, h * HD:(h + 1) * HD],
                                     PT[:, h % 2, j, j * P:], start=(j == 0), stop=(j == TT - 1))
                last.then_inc(o_ps, 1)

            def conv_taps(u):
                m, r = u // 8, u % 8
                if r == 0 and m:
                    pe.wait_ge(c_sum, m)
                for j in (2 * r, 2 * r + 1):
                    n = m * PE_TAPS + j
                    pe.wait_ge(dg, n + 1)
                    last = pe.matmul(psum[:, 7, :], diag[:, n % 8, :], uT[:, m, j:j + SEQ], start=(j == 0),
                                     stop=(j == PE_TAPS - 1))
                    if j < PE_TAPS - 1:
                        last.then_inc(dg_used, 1)
                    else:
                        last.then_inc(c_ps, 1)

            for u in range(UNITS + 2):
                if u < UNITS:
                    scores(u)
                    conv_taps(u)
                if u >= 2:
                    turn(u - 2)
                    if (u - 2) % TT == 0 and u - 2 > 0:
                        values((u - 2) // TT - 1)
            values(HEADS - 1)
            pe.wait_ge(c_sum, CM)
            for m in range(CM):
                last = pe.matmul(psum[:, 0, :], ones, mixT[:, 4 + m, :], start=(m == 0), stop=(m == CM - 1))
            last.then_inc(mean_ps, 1)
            for m in range(CM):
                pe.wait_ge(sq, m + 1)
                last = pe.matmul(psum[:, 1, :], ones, PT[:, 0, m, :], start=(m == 0), stop=(m == CM - 1))
            last.then_inc(var_ps, 1)


def output_and_routing(g):
    nc, a, psum, arena, spare, dram = g["nc"], g["a"], g["psum"], g["arena"], g["spare"], g["dram"]
    at, first, mixT, modacc, res = g["at"], g["first"], g["mixT"], g["modacc"], g["res"]
    ident, ones, small = g["ident"], g["ones"], g["small"]
    b = g["base"]
    gt1, sh2, sc2 = (modacc[:, o:o + D] for o in (2048, 3072, 4096))
    g2, squares = modacc[:, 0:D], modacc[:, D:2 * D]
    h2T = arena[:, b + 10240:b + 14336].rearrange("p (k n) -> p k n", k=KT)
    h2 = arena[:, b + 14336:b + 16384].rearrange("p (i n) -> p i n", i=2)
    o = b + 16384
    tmp = arena[:, o:o + 1024].rearrange("p (i n) -> p i n", i=2)
    wr = arena[:, o + 1024:o + 1312].rearrange("p (k n) -> p k n", k=KT)
    rb = arena[:, o + 1312:o + 1348]
    zero_ids = arena[0:TABLE, o + 1348:o + 1476].bitcast(I32)
    slot_rows = arena[0:TABLE, o + 1476:o + 1604]
    ss, rstd = small[:, 8:12], small[:, 12:16]
    g["dest"] = dest = small[:, 160:168].bitcast(I32)
    g["weight"] = weight = small[:, 168:176]
    g["slots"] = slots = small[:, 176:176 + TABLE].bitcast(I32)
    g["expert_of"] = expert_of = small[0:1, 224:224 + BLOCKS].bitcast(I32)
    g["pairs"] = pairs = small[0:1, 272:274].bitcast(I32)
    token_id = small[:, 276:280].bitcast(I32)
    used = [b + 6144]

    def room(n):
        used[0] += n
        assert used[0] <= b + 10240
        return arena[:, used[0] - n:used[0]]

    RL = GROUPS + EXPERTS
    logits = room(TT * RL).rearrange("p (t n) -> p t n", t=TT)
    glog = room(TT * 8).rearrange("p (t n) -> p t n", t=TT)
    gmax = room(TT * 8).rearrange("p (t n) -> p t n", t=TT)
    gidx = room(TT * 8).rearrange("p (t n) -> p t n", t=TT)
    gexp = room(TT * 4).rearrange("p (t n) -> p t n", t=TT)
    gsum = room(TT)
    ngm = room(TT)
    hot_g = room(TT * 4).rearrange("p (t n) -> p t n", t=TT)
    pen = room(TT * 4).rearrange("p (t n) -> p t n", t=TT)
    elog = room(TT * 32).rearrange("p (t n) -> p t n", t=TT)
    emax = room(TT * 8).rearrange("p (t n) -> p t n", t=TT)
    eidx = room(TT * 8).rearrange("p (t n) -> p t n", t=TT)
    chosen = room(TT * 2).rearrange("p (t n) -> p t n", t=TT)
    diff, ediff, den = room(TT), room(TT), room(TT)
    hot = [room(TT * 32).rearrange("p (t n) -> p t n", t=TT) for _ in range(2)]
    both = room(TT * 32).rearrange("p (t n) -> p t n", t=TT)
    where = room(TT * 32).rearrange("p (t n) -> p t n", t=TT)
    picked = room(TT * 32).rearrange("p (t n) -> p t n", t=TT)
    destf = room(TT * 2).rearrange("p (t n) -> p t n", t=TT)
    counts, nblk, end, start = room(32), room(32), room(32), room(32)
    iota = room(64)
    ended = room(BLOCKS * 32)[0:1, :].rearrange("p (b n) -> p b n", b=BLOCKS)
    expf, pairf, pairw = room(BLOCKS)[0:1, :], room(1)[0:1, :], room(BLOCKS)[0:1, :]

    with ExitStack() as cx:
        sem, dma_sem = g["semaphores"](cx)
        ready, taken = sem("mix_in_psum"), sem("mix_taken")
        loads, g2_ok = dma_sem("router_loaded"), sem("norm2_row_ready")
        ids_ok, zstore = sem("ids_built"), dma_sem("slot_table_zeroed")
        x1, ssq, var, root, rs = sem("x1_ready"), sem("x1_squares"), sem("x1_variance"), sem("x1_root"), sem("x1_rstd")
        h2s, stored = sem("h2_ready"), [dma_sem("h2_stored0"), dma_sem("h2_stored1")]
        dstep = sem("routing_dve_step")
        t_ps, t_sb = sem("h2T_in_psum"), sem("h2T_ready")
        r_ps, both_ok, rank_ps = sem("logits_in_psum"), sem("choices_ready"), sem("ranks_in_psum")
        neg_ok, gexp_ok, diff_ok, ediff_ok = sem("max_negated"), sem("group_exp"), sem("gap_ready"), sem("gap_exp")
        dest_ok, scattered, table_in = sem("dest_ready"), dma_sem("slots_scattered"), dma_sem("slot_rows_loaded")
        rows_f, tab_ps = sem("slot_rows_ready"), sem("slots_in_psum")
        block = cx.enter_context(nc.Block())

        @block.sync
        def _(sp):
            sp.dma_start(g2, a["g_norm2"].to_broadcast([P, D])).then_inc(loads, 16)
            sp.dma_start(wr[:, :, 0:GROUPS], a["w_router_group"][0].rearrange("(k p) n -> p k n", p=P)).then_inc(loads, 16)
            sp.dma_start(wr[:, :, GROUPS:], a["w_router_expert"][0].rearrange("(k p) n -> p k n", p=P)).then_inc(loads, 16)
            sp.dma_start(rb[:, 0:GROUPS], a["b_router_group"].to_broadcast([P, GROUPS])).then_inc(loads, 16)
            sp.dma_start(rb[:, GROUPS:], a["b_router_expert"].to_broadcast([P, EXPERTS])).then_inc(loads, 16)
            sp.wait_ge(ids_ok, 2)
            sp.dma_start(dram["slot_token"].rearrange("(b p) a -> b (p a)", p=P), zero_ids).then_inc(zstore, 16)
            for t in range(TT):
                sp.wait_ge(h2s, t + 1)
                sp.dma_start(dram["h2"][t * P:(t + 1) * P, :], h2[:, t % 2, :]).then_inc(stored[t % 2], 16)
            sp.wait_ge(scattered, 16 * 8)
            sp.dma_start(slot_rows.bitcast(I32), dram["slot_token"].rearrange("(b p) a -> b (p a)", p=P)).then_inc(table_in, 16)
            for i in range(2):
                sp.wait_ge(stored[i], 32)

        @block.gpsimd
        def _(pool):
            step = Steps(pool, ids_ok)
            step(pool.memset(zero_ids, 0))
            step(pool.iota(token_id, [[P, TT]], base=0, channel_multiplier=1))
            pool.wait_ge(zstore, 16)
            pool.wait_ge(dest_ok, 1)
            for t in range(TT):
                for k in range(2):
                    pool.indirect_dma_start(
                        out=dram["slot_token"], out_offset=bass.IndirectOffsetOnAxis(ap=dest[:, 2 * t + k:2 * t + k + 1].bitcast(U32), axis=0),
                        in_=token_id[:, t:t + 1], in_offset=None).then_inc(scattered, 16)

        @block.tensor
        def _(pe):
            w = [first.use(pe, at["wout"][n]).rearrange("p (k n) -> p k n", k=KT) for n in range(2)]

            def turn(t):
                pe.wait_ge(h2s, t + 1)
                for half in range(2):
                    if t:
                        pe.wait_ge(t_sb, 2 * t + half - 1)
                    for k in range(4):
                        last = pe.transpose(psum[:, 4 + half, k * P:(k + 1) * P],
                                            h2[:, t % 2, (4 * half + k) * P:(4 * half + k + 1) * P], ident)
                    last.then_inc(t_ps, 1)

            def route(t):
                pe.wait_ge(t_sb, 2 * t + 2)
                for k in range(KT):
                    last = pe.matmul(psum[:, 6, t * RL:(t + 1) * RL], h2T[:, k, t * P:(t + 1) * P], wr[:, k, :],
                                     start=(k == 0), stop=(k == KT - 1))
                last.then_inc(r_ps, 1)

            pe.wait_ge(loads, 16 * 5)
            for t in range(TT):
                for n in range(2):
                    i = 2 * t + n
                    if i >= 4:
                        pe.wait_ge(taken, i - 3)
                    for k in range(KT):
                        last = pe.matmul(psum[:, i % 4, :], mixT[:, k, t * P:(t + 1) * P], w[n][:, k, :],
                                         start=(k == 0), stop=(k == KT - 1))
                    last.then_inc(ready, 1)
                if t:
                    turn(t - 1)
                if t > 1:
                    route(t - 2)
            first.read_by(at["wout"][1], ready, 8)
            turn(TT - 1)
            route(TT - 2)
            route(TT - 1)
            pe.wait_ge(both_ok, 1)
            for t in range(TT):
                for s in range(t + 1):
                    last = pe.matmul(psum[:, 7, t * 32:(t + 1) * 32], g["before"] if s == t else ones, both[:, s, :],
                                     start=(s == 0), stop=(s == t))
            for s in range(TT):
                last = pe.matmul(psum[:, 7, 128:160], ones, both[:, s, :], start=(s == 0), stop=(s == TT - 1))
            last.then_inc(rank_ps, 1)
            pe.wait_ge(rows_f, 1)
            pe.transpose(psum[:, 3, 0:TABLE], slot_rows, ident[0:TABLE, 0:TABLE]).then_inc(tab_ps, 1)

        @block.scalar
        def _(act):
            for t in range(TT):
                act.wait_ge(x1, 2 * t + 2)
                if t:
                    act.wait_ge(ssq, t)
                act.activation(squares, res[:, t, :], ACT.Square, accum_out=ss[:, t:t + 1]).then_inc(ssq, 1)
                act.wait_ge(var, t + 1)
                act.activation(rstd[:, t:t + 1], ss[:, t:t + 1], ACT.Sqrt).then_inc(root, 1)
                for half in range(2):
                    act.wait_ge(t_ps, 2 * t + half + 1)
                    act.activation(h2T[:, 4 * half:4 * half + 4, t * P:(t + 1) * P],
                                   psum[:, 4 + half, :].rearrange("p (k n) -> p k n", k=4), ACT.Copy).then_inc(t_sb, 1)
            act.wait_ge(neg_ok, 1)
            for t in range(TT):
                act.activation(gexp[:, t, :], logits[:, t, 0:GROUPS], ACT.Exp, bias=ngm[:, t:t + 1],
                               accum_out=gsum[:, t:t + 1]).then_inc(gexp_ok, 1)
            act.wait_ge(diff_ok, 1)
            act.activation(ediff, diff, ACT.Exp).then_inc(ediff_ok, 1)

        @block.vector
        def _(dve):
            step = Steps(dve, dstep)
            dve.wait_ge(loads, 16 * 5)
            step(dve.scalar_tensor_tensor(out=sc2, in0=sc2, scalar=1.0, in1=g2, op0=ALU.add, op1=ALU.mult))
            for t in range(TT):
                for n in range(2):
                    i = 2 * t + n
                    dve.wait_ge(ready, i + 1)
                    cols = slice(512 * n, 512 * n + 512)
                    dve.tensor_tensor(tmp[:, i % 2, :], psum[:, i % 4, :], gt1[:, cols], ALU.mult).then_inc(taken, 1)
                    dve.wait_ge(taken, i + 1)
                    dve.tensor_tensor(res[:, t, cols], res[:, t, cols], tmp[:, i % 2, :], ALU.add).then_inc(x1, 1)
                dve.wait_ge(ssq, t + 1)
                dve.tensor_scalar(ss[:, t:t + 1], ss[:, t:t + 1], 1.0 / D, EPS, ALU.mult, ALU.add).then_inc(var, 1)
                dve.wait_ge(root, t + 1)
                step(dve.reciprocal(rstd[:, t:t + 1], rstd[:, t:t + 1]))
                if t >= 2:
                    dve.wait_ge(stored[t % 2], 16)
                    dve.wait_ge(t_ps, 2 * (t - 1))
                step(dve.scalar_tensor_tensor(out=h2[:, t % 2, :], in0=res[:, t, :], scalar=rstd[:, t:t + 1], in1=sc2,
                                              op0=ALU.mult, op1=ALU.mult))
                dve.tensor_tensor(h2[:, t % 2, :], h2[:, t % 2, :], sh2, ALU.add).then_inc(h2s, 1)
            dve.wait_ge(r_ps, TT)
            dve.wait_ge(ready, 8)
            step(dve.tensor_tensor(logits, psum[:, 6, 0:TT * RL].rearrange("p (t n) -> p t n", t=TT),
                                   rb.unsqueeze(1).to_broadcast([P, TT, RL]), ALU.add))
            step(dve.memset(glog, NEG))
            step(dve.tensor_copy(glog[:, :, 0:GROUPS], logits[:, :, 0:GROUPS]))
            for t in range(TT):
                step(dve.max(gmax[:, t, :], glog[:, t, :]))
                step(dve.max_index(gidx[:, t, :].bitcast(U32), gmax[:, t, :], glog[:, t, :]))
            dve.tensor_scalar(ngm, gmax[:, :, 0], -1.0, None, ALU.mult).then_inc(neg_ok, 1)
            step(dve.tensor_copy(chosen[:, :, 0], gidx[:, :, 0].bitcast(U32)))
            step(dve.memset(iota[:, 0:1], 0.0))
            for n in (1, 2, 4, 8, 16, 32):
                step(dve.tensor_scalar(iota[:, n:2 * n], iota[:, 0:n], float(n), None, ALU.add))
            step(dve.tensor_tensor(hot_g, iota[:, 0:GROUPS].unsqueeze(1).to_broadcast([P, TT, GROUPS]),
                                   chosen[:, :, 0:1].to_broadcast([P, TT, GROUPS]), ALU.is_equal))
            step(dve.tensor_scalar(pen, hot_g, 1.0, -NEG, ALU.subtract, ALU.mult))
            e4 = elog.rearrange("p t (q n) -> p (t q) n", q=GROUPS)
            spread = lambda x: x.rearrange("p t (q n) -> p (t q) n", n=1).to_broadcast([P, TT * GROUPS, PER_GROUP])
            step(dve.tensor_copy(elog, logits[:, :, GROUPS:]))
            step(dve.tensor_tensor(e4, e4, spread(hot_g), ALU.mult))
            step(dve.tensor_tensor(e4, e4, spread(pen), ALU.add))
            for t in range(TT):
                step(dve.max(emax[:, t, :], elog[:, t, :]))
                step(dve.max_index(eidx[:, t, :].bitcast(U32), emax[:, t, :], elog[:, t, :]))
            dve.tensor_tensor(diff, emax[:, :, 1], emax[:, :, 0], ALU.subtract).then_inc(diff_ok, 1)
            step(dve.tensor_copy(chosen, eidx[:, :, 0:2].bitcast(U32)))
            for k in range(2):
                step(dve.tensor_tensor(hot[k], iota[:, 0:32].unsqueeze(1).to_broadcast([P, TT, 32]),
                                       chosen[:, :, k:k + 1].to_broadcast([P, TT, 32]), ALU.is_equal))
            dve.tensor_tensor(both, hot[0], hot[1], ALU.add).then_inc(both_ok, 1)
            dve.wait_ge(gexp_ok, TT)
            dve.wait_ge(ediff_ok, 1)
            step(dve.tensor_scalar(den, ediff, 1.0, None, ALU.add))
            step(dve.tensor_tensor(den, den, gsum, ALU.mult))
            wt = weight.rearrange("p (t k) -> p t k", k=2)
            step(dve.reciprocal(wt[:, :, 0], den))
            step(dve.tensor_tensor(wt[:, :, 1], wt[:, :, 0], ediff, ALU.mult))
            dve.wait_ge(rank_ps, 1)
            step(dve.tensor_copy(counts, psum[:, 7, 128:160]))
            step(dve.tensor_scalar(nblk, counts, 0.0, None, ALU.is_gt))
            for j in range(1, SEQ // P):
                step(dve.scalar_tensor_tensor(out=nblk, in0=counts, scalar=float(P * j), in1=nblk, op0=ALU.is_gt, op1=ALU.add))
            step(dve.tensor_tensor_scan(end, ones[:, 0:32], nblk, 0.0, ALU.mult, ALU.add))
            step(dve.tensor_tensor(start, end, nblk, ALU.subtract))
            step(dve.tensor_scalar(start, start, float(P), None, ALU.mult))
            step(dve.tensor_tensor(where, psum[:, 7, 0:128].rearrange("p (t n) -> p t n", t=TT),
                                   start.unsqueeze(1).to_broadcast([P, TT, 32]), ALU.add))
            for k in range(2):
                step(dve.tensor_tensor(picked, where, hot[k], ALU.mult))
                step(dve.tensor_reduce(destf[:, :, k], picked, AX_X, ALU.add))
            dve.tensor_copy(dest.rearrange("p (t k) -> p t k", k=2), destf).then_inc(dest_ok, 1)
            step(dve.tensor_tensor(ended, end[0:1, :].unsqueeze(1).to_broadcast([1, BLOCKS, 32]),
                                   iota[0:1, 0:BLOCKS].rearrange("p (b n) -> p b n", n=1).to_broadcast([1, BLOCKS, 32]), ALU.is_le))
            step(dve.tensor_reduce(expf, ended, AX_X, ALU.add))
            step(dve.tensor_scalar(expf, expf, float(EXPERTS - 1), None, ALU.min))
            step(dve.tensor_copy(expert_of, expf))
            step(dve.tensor_scalar(pairw[:, 0:BLOCKS // 2], iota[0:1, 0:BLOCKS // 2], 2.0, None, ALU.mult))
            step(dve.tensor_scalar(pairw[:, 0:BLOCKS // 2], pairw[:, 0:BLOCKS // 2], end[0:1, 31:32], None, ALU.is_lt))
            step(dve.tensor_reduce(pairf, pairw[:, 0:BLOCKS // 2], AX_X, ALU.add))
            step(dve.tensor_scalar(pairs[:, 0:1], pairf, 2.0, None, ALU.subtract))
            step(dve.tensor_scalar(pairs[:, 1:2], pairf, -1.0, float(BLOCKS // 2), ALU.mult, ALU.add))
            dve.wait_ge(table_in, 16)
            step(dve.tensor_copy(slot_rows, slot_rows.bitcast(I32)))
            dve.engine_nop().then_inc(rows_f, 1)
            dve.wait_ge(tab_ps, 1)
            step(dve.tensor_copy(slots, psum[:, 3, 0:TABLE]))
    first.new_phase()


def experts(g):
    nc, a, psum, arena, dram = g["nc"], g["a"], g["psum"], g["arena"], g["dram"]
    ident, ring, spare = g["ident"], g["ring"], g["spare"]
    b0 = g["base"] + 6144
    xg = arena[:, b0:b0 + 2048].rearrange("p (j n) -> p j n", j=2)
    xT = arena[:, b0 + 2048:b0 + 4096].rearrange("p (j n) -> p j n", j=2)
    yb = arena[:, b0 + 4096:b0 + 6144].rearrange("p (j n) -> p j n", j=2)
    hb = arena[:, b0 + 6144:b0 + 7168].rearrange("p (j n) -> p j n", j=2)
    hT = arena[:, b0 + 7168:b0 + 8192].rearrange("p (j n) -> p j n", j=2)
    zeros = arena[:, b0 + 8192:b0 + 8192 + D].rearrange("p (a n) -> p a n", a=1)
    index = g["small"][:, 280:282].bitcast(I32)
    slots, expert_of, pairs = g["slots"], g["expert_of"], g["pairs"]
    GATE, UP, DOWN = (0, 3), (1, 4), (2, 5)
    slot6 = lambda s: ring[:, s, :] if s < SLOTS else spare[:, (s - SLOTS) * CHUNK:(s - SLOTS + 1) * CHUNK]
    wsrc = {"gate": a["w_exp_gate"].rearrange("l e (k p) n -> p (l e) k n", p=P),
            "up": a["w_exp_up"].rearrange("l e (k p) n -> p (l e) k n", p=P),
            "down": a["w_exp_down"].rearrange("l e (k p) n -> p (l e) k n", p=P)}
    BG, BU, BY, BX, BH = 0, 1, 2, 4, 6
    PAIRS = BLOCKS // 2

    def wait(eng, sem, value):
        if not isinstance(value, int) or value > 0:
            eng.wait_ge(sem, value)

    def run(eng, body, skipped=None):
        n = eng.value_load(pairs[:, 0:1], min_val=0, max_val=PAIRS - 2) + 2
        body(0, 0), body(0, 1), body(1, 0), body(1, 1)
        with eng.Fori(2, PAIRS) as i:
            with eng.If(i < n):
                body(i, 0)
                body(i, 1)
            if skipped:
                with eng.Else():
                    skipped(i)
            eng.nop()
        return n

    with ExitStack() as cx:
        sem, dma_sem = g["semaphores"](cx)
        w_in = [dma_sem(f"expert_weights{s}") for s in range(6)]
        idx_ok, idx_seen = sem("indices_copied"), sem("indices_seen")
        x_in = [dma_sem(f"tokens_gathered{j}") for j in range(2)]
        xt_ps, xt_sb, gate_ps, up_ps = sem("xT_in_psum"), sem("xT_ready"), sem("gate_in_psum"), sem("up_in_psum")
        silu_ok, h_ok, ht_ps, ht_sb = sem("silu_ready"), sem("hidden_ready"), sem("hT_in_psum"), sem("hT_ready")
        y_ps, y_sb = sem("y_in_psum"), sem("y_ready")
        y_st = [dma_sem(f"y_stored{j}") for j in range(2)]
        zero_ok, zeroed = sem("zero_tile_ready"), dma_sem("unused_rows_zeroed")
        block = cx.enter_context(nc.Block())

        @block.sync
        def _(sp):
            def load(kind, s, e):
                k = 4 if kind == "down" else KT
                dst = slot6(s).rearrange("p (e k n) -> p e k n", e=1, k=k)
                sp.dma_start(dst, wsrc[kind][:, bass.ds(e, 1)]).then_inc(w_in[s], 16)

            def body(i, j):
                e = sp.value_load(expert_of[0:1, bass.ds(i * 2 + j, 1)], min_val=0, max_val=EXPERTS - 1)
                wait(sp, gate_ps, i * 2 + j - 1)
                load("gate", GATE[j], e)
                wait(sp, up_ps, i * 2 + j - 1)
                load("up", UP[j], e)
                if isinstance(i, int) and i + j == 0:
                    return
                eb = sp.value_load(expert_of[0:1, bass.ds(i * 2 + j - 1, 1)], min_val=0, max_val=EXPERTS - 1)
                wait(sp, y_ps, (i * 2 + j - 3) * 2 + 2)
                load("down", DOWN[j], eb)

            n = run(sp, body)
            eb = sp.value_load(expert_of[0:1, bass.ds(n * 2 - 1, 1)], min_val=0, max_val=EXPERTS - 1)
            sp.wait_ge(y_ps, n * 4 - 4)
            load("down", DOWN[0], eb)

        @block.gpsimd
        def _(pool):
            idxn = [0]

            def gather(b, j, count):
                pool.tensor_copy(index[:, j:j + 1], slots[:, bass.ds(b, 1)]).then_inc(idx_ok, 1)
                pool.wait_ge(idx_ok, b + 1)
                pool.sem_inc(idx_seen, 1)
                pool.indirect_dma_start(
                    out=xg[:, j, :], out_offset=None, in_=dram["h2"],
                    in_offset=bass.IndirectOffsetOnAxis(ap=index[:, j:j + 1].bitcast(U32), axis=0)).then_inc(x_in[j], 16)

            def store(b, j):
                pool.dma_start(dram["y"].rearrange("(b p) n -> p b n", p=P)[:, bass.ds(b, 1), :],
                               yb[:, j:j + 1, :]).then_inc(y_st[j], 16)

            def body(i, j):
                b = i * 2 + j
                pool.wait_ge(xt_ps, b * 2 + 2)
                pool.wait_ge(x_in[j], i * 16 + 16)
                gather(b + 2, j, i + 1)
                if isinstance(i, int) and i + j == 0:
                    return
                pool.wait_ge(y_sb, b * 2)
                store(b - 1, 1 - j)

            def skipped(i):
                for j in range(2):
                    pool.dma_start(dram["y"].rearrange("(b p) n -> p b n", p=P)[:, bass.ds(i * 2 + j, 1), :],
                                   zeros[:, 0:1, :]).then_inc(zeroed, 16)

            pool.memset(zeros, 0.0).then_inc(zero_ok, 1)
            pool.wait_ge(zero_ok, 1)
            pool.dma_start(dram["y"][BLOCKS * P:(BLOCKS + 1) * P, :], zeros[:, 0, :]).then_inc(zeroed, 16)
            gather(0, 0, 0)
            gather(1, 1, 0)
            n = run(pool, body, skipped)
            unused = pool.value_load(pairs[:, 1:2], min_val=0, max_val=PAIRS)
            pool.wait_ge(zeroed, unused * 32 + 16)
            pool.wait_ge(y_sb, n * 4)
            store(n * 2 - 1, 1)
            for j in range(2):
                pool.wait_ge(y_st[j], n * 16)
                pool.wait_ge(x_in[j], n * 16 + 16)

        @block.tensor
        def _(pe):
            def turn_x(b, j, count):
                pe.wait_ge(x_in[j], count)
                for half in range(2):
                    wait(pe, xt_sb, b * 2 + half - 1)
                    for k in range(4):
                        last = pe.transpose(psum[:, BX + half, k * P:(k + 1) * P],
                                            xg[:, j, (4 * half + k) * P:(4 * half + k + 1) * P], ident)
                    last.then_inc(xt_ps, 1)

            def turn_h(b, j):
                pe.wait_ge(h_ok, b + 1)
                wait(pe, ht_sb, b)
                for k in range(4):
                    last = pe.transpose(psum[:, BH, k * P:(k + 1) * P], hb[:, j, k * P:(k + 1) * P], ident)
                last.then_inc(ht_ps, 1)

            def down(b, j, count):
                w = slot6(DOWN[1 - j]).rearrange("p (k n) -> p k n", k=4)
                pe.wait_ge(w_in[DOWN[1 - j]], count)
                pe.wait_ge(ht_sb, b + 1)
                for n in range(2):
                    wait(pe, y_sb, b * 2 + n - 1)
                    for k in range(4):
                        last = pe.matmul(psum[:, BY + n, :], hT[:, j, k * P:(k + 1) * P], w[:, k, n * 512:(n + 1) * 512],
                                         start=(k == 0), stop=(k == 3))
                    last.then_inc(y_ps, 1)

            def project(s, j, bank, done):
                w = slot6(s).rearrange("p (k n) -> p k n", k=KT)
                for k in range(KT):
                    last = pe.matmul(psum[:, bank, :], xT[:, j, k * P:(k + 1) * P], w[:, k, :], start=(k == 0),
                                     stop=(k == KT - 1))
                last.then_inc(done, 1)

            def body(i, j):
                b = i * 2 + j
                turn_x(b + 1, 1 - j, i * 16 + 16 + 16 * j)
                pe.wait_ge(xt_sb, b * 2 + 2)
                pe.wait_ge(w_in[GATE[j]], i * 16 + 16)
                wait(pe, silu_ok, b)
                project(GATE[j], j, BG, gate_ps)
                head = isinstance(i, int) and i + j == 0
                if not head:
                    turn_h(b - 1, 1 - j)
                pe.wait_ge(w_in[UP[j]], i * 16 + 16)
                wait(pe, h_ok, b)
                project(UP[j], j, BU, up_ps)
                if not head:
                    down(b - 1, 1 - j, i * 16 + 16 * j)

            turn_x(0, 0, 16)
            n = run(pe, body)
            turn_h(n * 2 - 1, 1)
            down(n * 2 - 1, 1, n * 16)

        @block.scalar
        def _(act):
            def take_x(b, j):
                wait(act, up_ps, b - 1)
                for half in range(2):
                    act.wait_ge(xt_ps, b * 2 + half + 1)
                    act.activation(xT[:, j, 512 * half:512 * half + 512], psum[:, BX + half, :], ACT.Copy).then_inc(xt_sb, 1)

            def take_h(b, j):
                act.wait_ge(ht_ps, b + 1)
                wait(act, y_ps, b * 2 - 2)
                act.activation(hT[:, j, :], psum[:, BH, :], ACT.Copy).then_inc(ht_sb, 1)

            def body(i, j):
                b = i * 2 + j
                take_x(b + 1, 1 - j)
                act.wait_ge(gate_ps, b + 1)
                wait(act, ht_ps, b - 1)
                act.activation(hb[:, j, :], psum[:, BG, :], ACT.Silu).then_inc(silu_ok, 1)
                if not (isinstance(i, int) and i + j == 0):
                    take_h(b - 1, 1 - j)

            take_x(0, 0)
            n = run(act, body)
            take_h(n * 2 - 1, 1)

        @block.vector
        def _(dve):
            def take_y(b, j, count):
                wait(dve, y_st[j], count)
                for n in range(2):
                    dve.wait_ge(y_ps, b * 2 + n + 1)
                    dve.tensor_copy(yb[:, j, 512 * n:512 * n + 512], psum[:, BY + n, :]).then_inc(y_sb, 1)

            def body(i, j):
                b = i * 2 + j
                dve.wait_ge(silu_ok, b + 1)
                dve.wait_ge(up_ps, b + 1)
                dve.tensor_tensor(hb[:, j, :], hb[:, j, :], psum[:, BU, :], ALU.mult).then_inc(h_ok, 1)
                if not (isinstance(i, int) and i + j == 0):
                    take_y(b - 1, 1 - j, i * 16 + 16 * j - 16)

            n = run(dve, body)
            take_y(n * 2 - 1, 1, n * 16 - 16)


def combine(g):
    nc, a, psum, arena, dram = g["nc"], g["a"], g["psum"], g["arena"], g["dram"]
    res, meta, ident, small = g["res"], g["meta"], g["ident"], g["small"]
    b = g["base"]
    gt2 = g["modacc"][:, 5120:6144]
    g["hnT"] = hnT = arena[:, b:b + KT * L2].rearrange("p (k n) -> p k n", k=KT)
    o = b + 6144
    y = arena[:, o:o + 4096].rearrange("p (i n) -> p i n", i=4)
    hn = arena[:, o + 4096:o + 6144].rearrange("p (i n) -> p i n", i=2)
    gfin = arena[:, o + 6144:o + 7168]
    squares = arena[:, o + 7168:o + 8192]
    ss, rstd, ss2, rstd2 = small[:, 8:12], small[:, 12:16], small[:, 16:21], small[:, 24:29]
    dest, weight = g["dest"], g["weight"]
    with ExitStack() as cx:
        sem, dma_sem = g["semaphores"](cx)
        y_in, loads = [dma_sem("rows_gathered0"), dma_sem("rows_gathered1")], dma_sem("final_gain_loaded")
        mixed, x2, dstep = sem("rows_mixed"), sem("x2_ready"), sem("combine_dve_step")
        ssq, var, root = sem("x2_squares"), sem("x2_variance"), sem("x2_root")
        x3, ssq2, var2, root2 = sem("h_ready"), sem("h_squares"), sem("h_variance"), sem("h_root")
        hn_ok, hn_ps, hn_sb = sem("hn_ready"), sem("hnT_in_psum"), sem("hnT_ready")
        block = cx.enter_context(nc.Block())

        @block.sync
        def _(sp):
            sp.dma_start(gfin, a["g_final"].rearrange("(a n) -> a n", a=1).to_broadcast([P, D])).then_inc(loads, 16)
            sp.dma_start(meta[0:META, :], a["meta_tokens_2"]).then_inc(loads, 16)
            g["later"].load_until(sp, SLOTS)

        @block.gpsimd
        def _(pool):
            for t in range(TT):
                if t >= 2:
                    pool.wait_ge(mixed, t - 1)
                for k in range(2):
                    pool.indirect_dma_start(
                        out=y[:, 2 * (t % 2) + k, :], out_offset=None, in_=dram["y"],
                        in_offset=bass.IndirectOffsetOnAxis(ap=dest[:, 2 * t + k:2 * t + k + 1].bitcast(U32), axis=0)
                    ).then_inc(y_in[t % 2], 16)

        @block.vector
        def _(dve):
            step = Steps(dve, dstep)

            def mix(t):
                y0, y1 = y[:, 2 * (t % 2), :], y[:, 2 * (t % 2) + 1, :]
                dve.wait_ge(y_in[t % 2], 32 * (t // 2 + 1))
                step(dve.tensor_scalar(y0, y0, weight[:, 2 * t:2 * t + 1], None, ALU.mult))
                step(dve.scalar_tensor_tensor(out=y0, in0=y1, scalar=weight[:, 2 * t + 1:2 * t + 2], in1=y0,
                                              op0=ALU.mult, op1=ALU.add))
                step(dve.tensor_tensor(y0, y0, gt2, ALU.mult))
                step(dve.tensor_tensor(res[:, t, :], res[:, t, :], y0, ALU.add))
                dve.engine_nop().then_inc(mixed, 1)

            def last_norm(t):
                dve.wait_ge(ssq, t + 1)
                dve.tensor_scalar(ss[:, t:t + 1], ss[:, t:t + 1], 1.0 / D, EPS, ALU.mult, ALU.add).then_inc(var, 1)
                dve.wait_ge(root, t + 1)
                step(dve.reciprocal(rstd[:, t:t + 1], rstd[:, t:t + 1]))
                dve.scalar_tensor_tensor(out=res[:, t, :], in0=res[:, t, :], scalar=rstd[:, t:t + 1], in1=gfin,
                                         op0=ALU.mult, op1=ALU.mult).then_inc(x3, 1)

            def pre_norm(t):
                n = P if t < TT else META
                src = res[:, t, :] if t < TT else meta
                dve.wait_ge(ssq2, t + 1)
                dve.tensor_scalar(ss2[0:n, t:t + 1], ss2[0:n, t:t + 1], 1.0 / D, EPS, ALU.mult, ALU.add).then_inc(var2, 1)
                dve.wait_ge(root2, t + 1)
                step(dve.reciprocal(rstd2[0:n, t:t + 1], rstd2[0:n, t:t + 1]))
                if t >= 2:
                    dve.wait_ge(hn_ps, 2 * (t - 1))
                dve.tensor_scalar(hn[0:n, t % 2, :], src[0:n, :], rstd2[0:n, t:t + 1], None, ALU.mult).then_inc(hn_ok, 1)

            dve.wait_ge(loads, 32)
            for t in range(TT + 2):
                if t < TT:
                    mix(t)
                if 1 <= t <= TT:
                    last_norm(t - 1)
                if t >= 2:
                    pre_norm(t - 2)
            pre_norm(TT)

        @block.scalar
        def _(act):
            def squares_of(src, out, n, done, count):
                if squared[0]:
                    act.wait_ge(*squared[0])
                act.activation(squares[0:n, :], src, ACT.Square, accum_out=out).then_inc(done, 1)
                squared[0] = (done, count)

            squared = [None]

            def first_half(t):
                act.wait_ge(mixed, t + 1)
                squares_of(res[:, t, :], ss[:, t:t + 1], P, ssq, t + 1)
                act.wait_ge(var, t + 1)
                act.activation(rstd[:, t:t + 1], ss[:, t:t + 1], ACT.Sqrt).then_inc(root, 1)

            def second_half(t):
                n = P if t < TT else META
                if t < TT:
                    act.wait_ge(x3, t + 1)
                squares_of((res[:, t, :] if t < TT else meta[0:META, :]), ss2[0:n, t:t + 1], n, ssq2, t + 1)
                act.wait_ge(var2, t + 1)
                act.activation(rstd2[0:n, t:t + 1], ss2[0:n, t:t + 1], ACT.Sqrt).then_inc(root2, 1)

            def take(t):
                n, c = (P, META + t * P) if t < TT else (META, 0)
                for half in range(2):
                    act.wait_ge(hn_ps, 2 * t + half + 1)
                    for k in range(4):
                        ins = act.activation(hnT[:, 4 * half + k, c:c + n], psum[:, 2 * (t % 2) + half, k * P:k * P + n],
                                             ACT.Copy, scale=col(g, "norm_mix_pre_2")[:, 4 * half + k:4 * half + k + 1])
                    ins.then_inc(hn_sb, 1)

            act.wait_ge(loads, 32)
            for t in range(TT + 2):
                if t < TT:
                    first_half(t)
                if 1 <= t <= TT:
                    second_half(t - 1)
                if t >= 2:
                    take(t - 2)
            second_half(TT)
            take(TT)

        @block.tensor
        def _(pe):
            for t in range(TT + 1):
                n = P if t < TT else META
                pe.wait_ge(hn_ok, t + 1)
                for half in range(2):
                    if t >= 2:
                        pe.wait_ge(hn_sb, 2 * (t - 2) + half + 1)
                    for k in range(4):
                        last = pe.transpose(psum[:, 2 * (t % 2) + half, k * P:k * P + n],
                                            hn[0:n, t % 2, (4 * half + k) * P:(4 * half + k + 1) * P], ident[0:n, 0:n])
                    last.then_inc(hn_ps, 1)


def products(pe, psum, banks, ready, taken, state, pieces):
    for rows, width, pairs in pieces:
        n = state[0]
        if n >= len(banks):
            sem, value = taken(n - len(banks)) if callable(taken) else (taken, n - len(banks) + 1)
            pe.wait_ge(sem, value)
        for i, (lhsT, rhs) in enumerate(pairs):
            last = pe.matmul(psum[0:rows, banks[n % len(banks)], 0:width], lhsT, rhs, start=(i == 0),
                             stop=(i == len(pairs) - 1))
        last.then_inc(ready, 1)
        state[0] += 1


def turned_pieces(w, x, k_tiles=KT, m_tiles=4, m0=0, width=P, halves=2):
    size = x.shape[2] // halves
    return [(width, size, [(w[:, k, (m0 + m) * P:(m0 + m) * P + width], x[:, k, i * size:(i + 1) * size]) for k in range(k_tiles)])
            for m in range(m_tiles) for i in range(halves)]


def row_pieces(w, x, c0=0, tiles=TT + 1):
    cut = lambda t: slice(META + t * P, META + (t + 1) * P) if t < TT else slice(0, META)
    return [(P if t < TT else META, 512, [(x[:, k, cut(t)], w[:, k, c0:c0 + 512]) for k in range(KT)]) for t in range(tiles)]


Z_AT = {3: 0, 2: 128, 1: 384, 0: 768}
Z_META = 1280
Z_ALL = Z_META + L2


def stick_breaking(g):
    nc, a, psum, arena, spare = g["nc"], g["a"], g["psum"], g["arena"], g["spare"]
    hnT, later, at2, ones, upto, future = g["hnT"], g["later"], g["at2"], g["ones"], g["upto"], g["future"]
    b = g["base"] + KT * L2
    g["sbT"] = sbT = arena[:, b:b + 4 * L2].rearrange("p (m n) -> p m n", m=4)
    b += 4 * L2
    qT = arena[:, b:b + 4 * L2].rearrange("p (m n) -> p m n", m=4)
    kz = arena[:, b + 4 * L2:b + 12 * L2].rearrange("p (h n) -> p h n", h=HEADS)
    b += 12 * L2
    v = arena[:, b:b + 2560].rearrange("p (t n) -> p t n", t=TT + 1)
    wbuf = arena[:, b + 2560:b + 2560 + 2 * Z_ALL].rearrange("p (i n) -> p i n", i=2)
    assert b + 2560 + 2 * Z_ALL <= g["floats"]
    zbuf = spare[:, 0:2 * Z_ALL].rearrange("p (i n) -> p i n", i=2)
    sbuf = spare[:, 2 * Z_ALL:4 * Z_ALL].rearrange("p (i n) -> p i n", i=2)
    BANKS = [0, 1, 2, 3]
    with ExitStack() as cx:
        sem, dma_sem = g["semaphores"](cx)
        ready, taken, zeroed = sem("sb_projection_in_psum"), sem("sb_projection_taken"), sem("sb_pads_set")
        z_ps, z_sb, soft, sp_ok, dstep = sem("z_in_psum"), sem("z_ready"), sem("log_term_ready"), sem("softplus_ready"), sem("sb_dve_step")
        astep = sem("sb_act_step")
        r_ps, arg_ok, w_ok, pv_ps, pv_sb = sem("rest_in_psum"), sem("exponent_ready"), sem("stick_weights_ready"), sem("sb_out_in_psum"), sem("sb_out_ready")
        block = cx.enter_context(nc.Block())

        @block.gpsimd
        def _(pool):
            step = Steps(pool, zeroed)
            for h in range(HEADS):
                lo = 64 * (1 - h % 2)
                step(pool.memset(kz[lo:lo + 64, h, :], 0.0))
            step(pool.memset(v[:, TT, :], 0.0))
            step(pool.memset(zbuf[:, :, Z_META:], NEG))

        @block.tensor
        def _(pe):
            state = [0]
            for c in range(3):
                w = later.use(pe, at2["proj"][c]).rearrange("p (k n) -> p k n", k=KT)
                products(pe, psum, BANKS, ready, taken, state, row_pieces(w, hnT) if c == 2 else turned_pieces(w, hnT))
                later.read_by(at2["proj"][c], ready, state[0])
            n_proj = state[0]
            pe.wait_ge(taken, n_proj)

            def scores(h):
                q = qT[:, h // 2, :]
                for n, i in enumerate((3, 2, 1, 0, "x", "m")):
                    c = 6 * h + n
                    if c >= 2:
                        before = {0: 6 * h - 1, 1: 6 * h - 2, 2: c - 1, 3: c - 1, 4: c - 1, 5: 6 * h}[n]
                        if before > 0:
                            pe.wait_ge(z_sb, before)
                    if i == "m":
                        pe.matmul(psum[0:META, 2, 0:META], kz[:, h, 0:META], q[:, 0:META], start=True, stop=True).then_inc(z_ps, 1)
                    elif i == "x":
                        pe.matmul(psum[0:META, 0, :], kz[:, h, 0:META], q[:, META:], start=True, stop=True).then_inc(z_ps, 1)
                    else:
                        lo = META + i * P
                        pe.matmul(psum[:, n % 2, 0:L2 - lo], kz[:, h, lo:lo + P], q[:, lo:], start=True, stop=True).then_inc(z_ps, 1)

            def rest(h):
                s, tail = sbuf[:, h % 2, :], wbuf[:, h % 2, :]
                pe.wait_ge(sp_ok, h + 1)
                for n, i in enumerate((3, 2, 1, 0, "x", "m")):
                    before = {0: 6 * h - 1, 1: 6 * h - 2, 2: 6 * h + 1, 3: 6 * h + 2, 4: 6 * h + 3, 5: 6 * h}[n]
                    if before > 0:
                        pe.wait_ge(arg_ok, before)
                    if i == "m":
                        last = pe.matmul(psum[0:META, 7, 0:META], upto[:, 0:META], s[:, Z_META:Z_META + META], start=True, stop=True)
                    elif i == "x":
                        pe.matmul(psum[0:META, 3, :], upto[:, 0:META], s[:, Z_META + META:], start=True, stop=False)
                        last = pe.matmul(psum[0:META, 3, :], ones[:, 0:META], tail[:, Z_AT[0]:Z_AT[0] + 512], start=False, stop=True)
                    else:
                        w = (TT - i) * P
                        o = psum[:, 3 + n % 2, 0:w]
                        last = pe.matmul(o, upto, s[:, Z_AT[i]:Z_AT[i] + w], start=True, stop=(i == 3))
                        if i < 3:
                            later_keys = s if i == 2 else tail
                            last = pe.matmul(o[:, P:], ones, later_keys[:, Z_AT[i + 1]:Z_AT[i + 1] + w - P], start=False, stop=True)
                    last.then_inc(r_ps, 1)

            def values(h):
                w = wbuf[:, h % 2, :]
                pe.wait_ge(w_ok, h + 1)
                if h:
                    pe.wait_ge(pv_sb, 2 * h)
                hc = slice(h * HD, (h + 1) * HD)
                pe.matmul(psum[0:HD, 5, :], v[:, TT, hc], w[:, Z_META + META:], start=True, stop=False)
                for i in range(TT):
                    last = pe.matmul(psum[0:HD, 5, i * P:], v[:, i, hc], w[:, Z_AT[i]:Z_AT[i] + (TT - i) * P],
                                     start=False, stop=(i == TT - 1))
                last.then_inc(pv_ps, 1)
                pe.matmul(psum[0:HD, 6, 0:META], v[:, TT, hc], w[:, Z_META:Z_META + META], start=True, stop=True).then_inc(pv_ps, 1)

            pe.wait_ge(zeroed, HEADS + 1)
            scores(0)
            for h in range(HEADS):
                if h + 1 < HEADS:
                    scores(h + 1)
                rest(h)
                if h:
                    values(h - 1)
            values(HEADS - 1)

        @block.scalar
        def _(act):
            n = 0
            for c in range(3):
                for m in range(5 if c == 2 else 8):
                    act.wait_ge(ready, n + 1)
                    src = psum[:, BANKS[n % 4], :]
                    i = slice((m % 2) * HALF, (m % 2 + 1) * HALF)
                    if c == 0:
                        last = act.activation(qT[:, m // 2, i], src[:, 0:HALF], ACT.Copy, scale=HD ** -0.5)
                    elif c == 1:
                        act.activation(kz[0:64, 2 * (m // 2), i], src[0:64, 0:HALF], ACT.Copy)
                        last = act.activation(kz[64:128, 2 * (m // 2) + 1, i], src[64:128, 0:HALF], ACT.Copy)
                    else:
                        if m == TT:
                            act.wait_ge(zeroed, HEADS + 1)
                        rows = P if m < TT else META
                        last = act.activation(v[0:rows, m, :], src[0:rows, :], ACT.Copy)
                    last.then_inc(taken, 1)
                    n += 1

            step = Steps(act, astep)

            def log_term(h):
                act.wait_ge(z_sb, 6 * h + 6)
                if h >= 2:
                    act.wait_ge(pv_ps, 2 * (h - 1))
                z, w = zbuf[:, h % 2, :], wbuf[:, h % 2, :]
                step(act.activation(w, z, ACT.Abs))
                step(act.activation(w, w, ACT.Exp, scale=-1.0))
                act.activation(w, w, ACT.Ln, bias=1.0).then_inc(soft, 1)

            def take(h):
                lo = 64 * (h % 2)
                act.wait_ge(pv_ps, 2 * h + 1)
                act.activation(sbT[lo:lo + 64, h // 2, META:], psum[0:HD, 5, :], ACT.Copy).then_inc(pv_sb, 1)
                act.wait_ge(pv_ps, 2 * h + 2)
                act.activation(sbT[lo:lo + 64, h // 2, 0:META], psum[0:HD, 6, 0:META], ACT.Copy).then_inc(pv_sb, 1)

            act.wait_ge(zeroed, HEADS + 2)
            log_term(0)
            for h in range(HEADS):
                act.wait_ge(arg_ok, 6 * h + 6)
                act.activation(wbuf[:, h % 2, :], zbuf[:, h % 2, :], ACT.Exp).then_inc(w_ok, 1)
                if h + 1 < HEADS:
                    if h:
                        take(h - 1)
                    log_term(h + 1)
            take(HEADS - 2)
            take(HEADS - 1)

        @block.vector
        def _(dve):
            step = Steps(dve, dstep)

            def take_scores(h):
                z = zbuf[:, h % 2, :]
                if h >= 2:
                    dve.wait_ge(w_ok, h - 1)
                for n, i in enumerate((3, 2, 1, 0, "x", "m")):
                    dve.wait_ge(z_ps, 6 * h + n + 1)
                    if i == "m":
                        last = dve.tensor_tensor(z[0:META, Z_META:Z_META + META], psum[0:META, 2, 0:META], future[0:META, 0:META], ALU.add)
                    elif i == "x":
                        last = dve.tensor_copy(z[0:META, Z_META + META:], psum[0:META, 0, :])
                    else:
                        w, o = (TT - i) * P, Z_AT[i]
                        if i < 3:
                            dve.tensor_copy(z[:, o + P:o + w], psum[:, n % 2, P:w])
                        last = dve.tensor_tensor(z[:, o:o + P], psum[:, n % 2, 0:P], future, ALU.add)
                    last.then_inc(z_sb, 1)

            def softplus(h):
                z, w, s = zbuf[:, h % 2, :], wbuf[:, h % 2, :], sbuf[:, h % 2, :]
                dve.wait_ge(soft, h + 1)
                step(dve.scalar_tensor_tensor(out=s, in0=z, scalar=0.0, in1=w, op0=ALU.max, op1=ALU.add))
                for i in (2, 1, 0):
                    o, later_keys = Z_AT[i], (s if i == 2 else w)
                    step(dve.tensor_copy(w[:, o:o + P], s[:, o:o + P]))
                    step(dve.tensor_tensor(w[:, o + P:o + (TT - i) * P], s[:, o + P:o + (TT - i) * P],
                                           later_keys[:, Z_AT[i + 1]:Z_AT[i + 1] + (TT - i - 1) * P], ALU.add))
                dve.engine_nop().then_inc(sp_ok, 1)

            def exponents(h):
                z = zbuf[:, h % 2, :]
                for n, i in enumerate((3, 2, 1, 0, "x", "m")):
                    dve.wait_ge(r_ps, 6 * h + n + 1)
                    if i == "m":
                        p, r = z[0:META, Z_META:Z_META + META], psum[0:META, 7, 0:META]
                    elif i == "x":
                        p, r = z[0:META, Z_META + META:], psum[0:META, 3, :]
                    else:
                        w = (TT - i) * P
                        p, r = z[:, Z_AT[i]:Z_AT[i] + w], psum[:, 3 + n % 2, 0:w]
                    dve.tensor_tensor(p, p, r, ALU.subtract).then_inc(arg_ok, 1)

            dve.wait_ge(zeroed, HEADS + 2)
            take_scores(0)
            for h in range(HEADS):
                softplus(h)
                if h + 1 < HEADS:
                    take_scores(h + 1)
                exponents(h)

        @block.sync
        def _(sp):
            later.load_until(sp, at2["proj"][2] + 1 + SLOTS)
    later.new_phase()


def gated_linear(g):
    nc, a, psum, arena, spare, small = g["nc"], g["a"], g["psum"], g["arena"], g["spare"], g["small"]
    hnT, later, at2, ones, ident = g["hnT"], g["later"], g["at2"], g["ones"], g["ident"]
    b = g["base"] + 12 * L2
    GW = GH * L2
    flat = lambda x: x.rearrange("p h n -> p (h n)")
    heads = lambda x: x.rearrange("p (h n) -> p h n", h=GH)
    q, k = heads(arena[:, b:b + GW]), heads(arena[:, b + GW:b + 2 * GW])
    o = b + 2 * GW
    v = arena[:, o:o + (TT + 1) * D].rearrange("p (t n) -> p t n", t=TT + 1)
    o += (TT + 1) * D
    att = arena[:, o:o + GH * 512].rearrange("p (h n) -> p h n", h=GH)
    attm = arena[0:META, o + 2048:o + 2048 + GH * META].rearrange("p (h n) -> p h n", h=GH)
    o += 2560
    cs = heads(arena[:, o:o + GW])
    wlr = arena[:, o + GW:o + GW + P].rearrange("p (k n) -> p k n", k=KT)
    e, qe, ke = heads(spare[:, 0:GW]), heads(spare[:, GW:2 * GW]), heads(spare[:, 2 * GW:3 * GW])
    masks = spare[:, 3 * GW:3 * GW + LEVELS * P].rearrange("p (l n) -> p l n", l=LEVELS)
    xor = spare[:, 3 * GW + LEVELS * P:3 * GW + LEVELS * P + P]
    wup = spare[0:16, 0:512]
    lrT = spare[0:16, 512:512 + L2]
    pi = spare[:, 1100:1228].bitcast(I32)
    pj = spare[:, 1228:1356].bitcast(I32)
    g["oT"] = oT = spare[:, GW:3 * GW].rearrange("p (k n) -> p k n", k=KT)
    state = spare[:, 0:1024].rearrange("p (h n) -> p h n", h=GH)
    kd = spare[:, 1024:2048].rearrange("p (i n) -> p i n", i=2)
    rows = spare[:, 3 * GW:3 * GW + D]
    squares = spare[:, 3 * GW + D:3 * GW + D + DV]
    nbias = small[:, 300:304]
    elast = small[:, 304:324].rearrange("p (h c) -> p h c", h=GH)
    nlast = small[:, 324:344].rearrange("p (h c) -> p h c", h=GH)
    ss, rstd = small[:, 344:348], small[:, 348:352]
    span = [(0, META)] + [(META + c * P, P) for c in range(TT)]
    BANKS = [0, 1, 2]

    def halves(x, l):
        size = 2 << l
        if size <= META:
            y = flat(x).rearrange("p (b t) -> p b t", t=size)
            return y[:, :, 0:size // 2], y[:, :, size // 2:], y[:, :, size // 2 - 1:size // 2].to_broadcast([P, GW // size, size // 2])
        y = x[:, :, META:].rearrange("p h (b t) -> p h b t", t=size)
        return (y[:, :, :, 0:size // 2], y[:, :, :, size // 2:],
                y[:, :, :, size // 2 - 1:size // 2].to_broadcast([P, GH, 512 // size, size // 2]))

    def level_part(x, l):
        return flat(x) if (2 << l) <= META else x[:, :, META:]

    with ExitStack() as cx:
        sem, dma_sem = g["semaphores"](cx)
        ready, taken, small_in = sem("gla_projection_in_psum"), sem("gla_projection_taken"), dma_sem("gate_weights_loaded")
        iota_ok, masks_ok, att0 = sem("positions_counted"), sem("masks_built"), sem("att_zeroed")
        astep, dstep = sem("gla_act_step"), sem("gla_dve_step")
        nb_ok, nx_ok, soft, cs_ok = sem("gate_bias_negated"), sem("gate_logits_ready"), sem("gate_log_ready"), sem("decay_sums_ready")
        diff, e_ok, qk_ok, lv_ps, lv_ok = sem("exponents_ready"), sem("decays_ready"), sem("decayed_ready"), sem("level_in_psum"), sem("level_taken")
        dec, kd_ps, kd_sb = sem("chunk_decays_applied"), sem("keys_in_psum"), sem("keys_ready")
        qd_e, kd_e, q_done = sem("query_decay_ready"), sem("key_decay_ready"), sem("queries_decayed")
        o_ps, s_ps, s_ok = sem("out_in_psum"), sem("state_in_psum"), sem("state_ready")
        sq, var, root, rs = sem("out_squares"), sem("out_variance"), sem("out_root"), sem("out_rstd")
        rows_ok, oT_ps, oT_ok = sem("out_rows_ready"), sem("oT_in_psum"), sem("oT_ready")
        block = cx.enter_context(nc.Block())

        @block.gpsimd
        def _(pool):
            step = Steps(pool, iota_ok)
            step(pool.iota(pi, [[0, P]], base=0, channel_multiplier=1))
            step(pool.iota(pj, [[1, P]], base=0, channel_multiplier=0))
            pool.memset(att, 0.0).then_inc(att0, 1)
            pool.wait_ge(att0, 1)
            pool.memset(attm, 0.0).then_inc(att0, 1)

        @block.tensor
        def _(pe):
            st = [0]
            pe.wait_ge(small_in, 32)
            products(pe, psum, BANKS, ready, taken, st, [
                (16, HALF, [(wlr[:, kk, :], hnT[:, kk, i * HALF:(i + 1) * HALF]) for kk in range(KT)]) for i in range(2)])
            w = later.use(pe, at2["proj"][3]).rearrange("p (k n) -> p k n", k=KT)
            products(pe, psum, BANKS, ready, taken, st, turned_pieces(w, hnT))
            later.read_by(at2["proj"][3], ready, st[0])
            pe.wait_ge(taken, 2)
            products(pe, psum, BANKS, ready, taken, st, [
                (P, HALF, [(wup[:, h * P:(h + 1) * P], lrT[:, i * HALF:(i + 1) * HALF])]) for h in range(GH) for i in range(2)])
            w = later.use(pe, at2["proj"][4]).rearrange("p (k n) -> p k n", k=KT)
            products(pe, psum, BANKS, ready, taken, st, turned_pieces(w, hnT))
            later.read_by(at2["proj"][4], ready, st[0])
            pe.wait_ge(taken, 26)

            def level(n, l):
                qq, kk = (q, k) if l is None else (qe, ke)
                if l is not None:
                    pe.wait_ge(qk_ok, n)
                if n:
                    pe.wait_ge(lv_ok, n)
                for h in range(GH):
                    for c0, _ in span[1:]:
                        last = pe.matmul(psum[:, 4 + h, c0 - META:c0 - META + P], kk[:, h, c0:c0 + P], qq[:, h, c0:c0 + P],
                                         start=True, stop=True)
                    if l is None or (2 << l) <= META:
                        last = pe.matmul(psum[0:META, 3, h * META:(h + 1) * META], kk[:, h, 0:META], qq[:, h, 0:META],
                                         start=True, stop=True)
                last.then_inc(lv_ps, 1)

            rowsv = []
            for c in range(2):
                w = later.use(pe, at2["proj"][5 + c]).rearrange("p (k n) -> p k n", k=KT)
                rowsv.append(row_pieces(w, hnT))
            level(0, None)
            for n in range(1, LEVELS + 1):
                p = n - 1
                if p < 5:
                    products(pe, psum, BANKS, ready, taken, st, rowsv[p % 2][:0] + [rowsv[0][p]])
                    if p == 4:
                        later.read_by(at2["proj"][5], ready, st[0])
                else:
                    products(pe, psum, BANKS, ready, taken, st, [rowsv[1][p - 5]])
                level(n, n - 1)
            products(pe, psum, BANKS, ready, taken, st, rowsv[1][LEVELS - 5:])
            later.read_by(at2["proj"][6], ready, st[0])
            pe.wait_ge(taken, st[0])
            pe.wait_ge(lv_ok, LEVELS + 1)
            pe.wait_ge(dec, 1)
            for c, (c0, n) in enumerate(span):
                vt = v[0:n, (c - 1) % (TT + 1), :]
                for h in range(GH):
                    if c and h == 0:
                        pe.wait_ge(kd_sb, c)
                    last = pe.transpose(psum[0:n, 0, h * P:(h + 1) * P], k[:, h, c0:c0 + n], ident)
                last.then_inc(kd_ps, 1)
                if c:
                    pe.wait_ge(s_ok, 2 * c)
                    pe.wait_ge(rows_ok, c)
                for h in range(GH):
                    at_ = attm[:, h, :] if c == 0 else att[:, h, c0 - META:c0 - META + P]
                    dst = psum[0:n, 1 + h // 2, (h % 2) * DV:(h % 2 + 1) * DV]
                    last = pe.matmul(dst, at_, vt[:, h * DV:(h + 1) * DV], start=True, stop=(c == 0))
                    if c:
                        last = pe.matmul(dst, q[:, h, c0:c0 + n], state[:, h, :], start=False, stop=True)
                last.then_inc(o_ps, 1)
                if c < TT:
                    pe.wait_ge(kd_sb, c + 1)
                    for h in range(GH):
                        last = pe.matmul(psum[:, 3 + h // 2, (h % 2) * DV:(h % 2 + 1) * DV], kd[0:n, c % 2, h * DK:(h + 1) * DK],
                                         vt[:, h * DV:(h + 1) * DV], start=True, stop=True)
                    last.then_inc(s_ps, 1)
                pe.wait_ge(rows_ok, c + 1)
                for half in range(2):
                    if c:
                        pe.wait_ge(oT_ok, 2 * (c - 1) + half + 1)
                    for kk in range(4):
                        last = pe.transpose(psum[:, 5 + half, kk * P:kk * P + n],
                                            rows[0:n, (4 * half + kk) * P:(4 * half + kk + 1) * P], ident[0:n, 0:n])
                    last.then_inc(oT_ps, 1)

        @block.scalar
        def _(act):
            step = Steps(act, astep)
            count = [0]

            def take(dst, rows_, width, scale=1.0, func=ACT.Copy, bias=None, done=None):
                n = count[0]
                act.wait_ge(ready, n + 1)
                kw = {} if bias is None else {"bias": bias}
                act.activation(dst, psum[0:rows_, BANKS[n % 3], 0:width], func, scale=scale, **kw).then_inc(taken, 1)
                count[0] += 1

            half = lambda x, h, i: x[:, h, i * HALF:(i + 1) * HALF]
            for i in range(2):
                take(lrT[:, i * HALF:(i + 1) * HALF], 16, HALF)
            for h in range(GH):
                for i in range(2):
                    take(half(q, h, i), P, HALF, scale=DK ** -0.5)
            act.wait_ge(nb_ok, 1)
            for h in range(GH):
                for i in range(2):
                    take(half(qe, h, i), P, HALF, scale=-1.0, func=ACT.Identity, bias=nbias[:, h:h + 1])
            act.wait_ge(taken, 18)
            act.wait_ge(masks_ok, 1)
            step(act.activation(flat(e), flat(qe), ACT.Abs))
            step(act.activation(flat(e), flat(e), ACT.Exp, scale=-1.0))
            act.activation(flat(e), flat(e), ACT.Ln, bias=1.0).then_inc(soft, 1)
            for h in range(GH):
                for i in range(2):
                    take(half(k, h, i), P, HALF)
            for n in range(LEVELS):
                t, c = (n, 0) if n < 5 else (n - 5, 1)
                rows_ = P if t < TT else META
                take(v[0:rows_, t, c * 512:(c + 1) * 512], rows_, 512)
                act.wait_ge(diff, n + 1)
                act.activation(level_part(e, n), level_part(e, n), ACT.Exp, scale=1.0 / 16).then_inc(e_ok, 1)
            for t in range(LEVELS - 5, TT + 1):
                rows_ = P if t < TT else META
                take(v[0:rows_, t, 512:1024], rows_, 512)
            act.wait_ge(qk_ok, LEVELS)
            act.activation(flat(e), flat(cs), ACT.Exp, scale=-1.0 / 16).then_inc(qd_e, 1)
            act.wait_ge(q_done, 1)
            for h in range(GH):
                for c, (c0, n) in enumerate(span):
                    last = act.activation(e[:, h, c0:c0 + n], cs[:, h, c0:c0 + n], ACT.Exp, scale=1.0 / 16, bias=nlast[:, h, c:c + 1])
            last.then_inc(kd_e, 1)

            def take_oT(c):
                c0, n = span[c]
                for i in range(2):
                    act.wait_ge(oT_ps, 2 * c + i + 1)
                    act.activation(oT[:, 4 * i:4 * i + 4, c0:c0 + n],
                                   psum[:, 5 + i, :].rearrange("p (k n) -> p k n", k=4)[:, :, 0:n], ACT.Copy).then_inc(oT_ok, 1)

            for c, (c0, n) in enumerate(span):
                act.wait_ge(kd_ps, c + 1)
                act.activation(kd[0:n, c % 2, :], psum[0:n, 0, :], ACT.Copy).then_inc(kd_sb, 1)
                act.wait_ge(o_ps, c + 1)
                for h in range(GH):
                    if 4 * c + h:
                        act.wait_ge(sq, 4 * c + h)
                    act.activation(squares[0:n, :], psum[0:n, 1 + h // 2, (h % 2) * DV:(h % 2 + 1) * DV], ACT.Square,
                                   accum_out=ss[0:n, h:h + 1]).then_inc(sq, 1)
                act.wait_ge(var, c + 1)
                act.activation(rstd[0:n, :], rstd[0:n, :], ACT.Sqrt).then_inc(root, 1)
                take_oT(c)

        @block.vector
        def _(dve):
            step = Steps(dve, dstep)
            dve.tensor_scalar(nbias, col(g, "b_gk_2"), -1.0, None, ALU.mult).then_inc(nb_ok, 1)
            dve.wait_ge(iota_ok, 2)
            step(dve.tensor_tensor(pi, pi, pj, ALU.bitwise_xor))
            for l in range(LEVELS):
                step(dve.tensor_scalar(pj, pi, l, None, ALU.logical_shift_right))
                step(dve.tensor_copy(xor, pj))
                step(dve.scalar_tensor_tensor(out=masks[:, l, :], in0=xor, scalar=1.0, in1=g["before"], op0=ALU.is_equal,
                                              op1=ALU.mult))
            dve.engine_nop().then_inc(masks_ok, 1)
            dve.wait_ge(soft, 1)
            step(dve.scalar_tensor_tensor(out=flat(ke), in0=flat(qe), scalar=0.0, in1=flat(e), op0=ALU.max, op1=ALU.add))
            for h in range(GH):
                for c0, n in span:
                    last = dve.tensor_tensor_scan(cs[:, h, c0:c0 + n], ones[:, 0:n], ke[:, h, c0:c0 + n], 0.0, ALU.mult, ALU.add)
            step(last)

            def exponents(l):
                left, right, mid = halves(cs, l)
                eleft, eright, _ = halves(e, l)
                dve.tensor_tensor(eleft, left, mid, ALU.subtract)
                dve.tensor_tensor(eright, mid, right, ALU.subtract).then_inc(diff, 1)

            def take_level(n, l):
                dve.wait_ge(lv_ps, n + 1)
                m = ident if l is None else masks[:, l, :]
                for h in range(GH):
                    last = dve.copy_predicated(att[:, h, :].rearrange("p (c n) -> p c n", c=TT),
                                               m.bitcast(U32).unsqueeze(1).to_broadcast([P, TT, P]),
                                               psum[:, 4 + h, :].rearrange("p (c n) -> p c n", c=TT))
                if l is None or (2 << l) <= META:
                    last = dve.copy_predicated(attm, m[0:META, 0:META].bitcast(U32).unsqueeze(1).to_broadcast([META, GH, META]),
                                               psum[0:META, 3, 0:GH * META].rearrange("p (h n) -> p h n", h=GH))
                last.then_inc(lv_ok, 1)

            exponents(0)
            dve.wait_ge(att0, 2)
            take_level(0, None)
            for l in range(LEVELS):
                dve.wait_ge(e_ok, l + 1)
                el, er, _ = halves(e, l)
                kl, _, _ = halves(k, l)
                _, qr, _ = halves(q, l)
                kel, _, _ = halves(ke, l)
                _, qer, _ = halves(qe, l)
                dve.tensor_tensor(kel, kl, el, ALU.mult)
                dve.tensor_tensor(qer, qr, er, ALU.mult).then_inc(qk_ok, 1)
                if l + 1 < LEVELS:
                    dve.wait_ge(qk_ok, l + 1)
                    exponents(l + 1)
                take_level(l + 1, l)
            dve.wait_ge(qd_e, 1)
            step(dve.tensor_copy(elast, e[:, :, META - 1:L2:P]))
            step(dve.tensor_scalar(nlast, cs[:, :, META - 1:L2:P], -1.0 / 16, None, ALU.mult))
            dve.tensor_tensor(flat(q), flat(q), flat(e), ALU.mult).then_inc(q_done, 1)
            dve.wait_ge(kd_e, 1)
            dve.tensor_tensor(flat(k), flat(k), flat(e), ALU.mult).then_inc(dec, 1)
            dve.wait_ge(dec, 1)
            for c, (c0, n) in enumerate(span):
                if c < TT:
                    dve.wait_ge(s_ps, c + 1)
                    dve.wait_ge(o_ps, c + 1)
                    for i in range(2):
                        if c == 0:
                            last = dve.tensor_copy(state[:, 2 * i:2 * i + 2, :], psum[:, 3 + i, :].rearrange("p (h n) -> p h n", h=2))
                        else:
                            for h in (2 * i, 2 * i + 1):
                                last = dve.scalar_tensor_tensor(
                                    out=state[:, h, :], in0=state[:, h, :], scalar=elast[:, h, c:c + 1],
                                    in1=psum[:, 3 + i, (h % 2) * DV:(h % 2 + 1) * DV], op0=ALU.mult, op1=ALU.add)
                        last.then_inc(s_ok, 1)
                dve.wait_ge(sq, 4 * c + 4)
                if c:
                    dve.wait_ge(root, c)
                dve.tensor_scalar(rstd[0:n, :], ss[0:n, :], 1.0 / DV, EPS, ALU.mult, ALU.add).then_inc(var, 1)
                dve.wait_ge(root, c + 1)
                step(dve.reciprocal(rstd[0:n, :], rstd[0:n, :]))
                if c:
                    dve.wait_ge(oT_ps, 2 * c)
                for h in range(GH):
                    last = dve.tensor_scalar(rows[0:n, h * DV:(h + 1) * DV], psum[0:n, 1 + h // 2, (h % 2) * DV:(h % 2 + 1) * DV],
                                             rstd[0:n, h:h + 1], None, ALU.mult)
                last.then_inc(rows_ok, 1)

        @block.sync
        def _(sp):
            sp.dma_start(wlr, a["w_in_2"][0][:, 4608:4624].rearrange("(k p) n -> p k n", p=P)).then_inc(small_in, 16)
            sp.dma_start(wup, a["w_gk_up_2"][0]).then_inc(small_in, 16)
            later.load_until(sp, at2["proj"][6] + 1 + SLOTS)
    later.new_phase()


class PostNorm:

    def __init__(self, g, sem, small_at):
        self.g, s = g, g["small"]
        self.parts = s[:, small_at:small_at + 10].rearrange("p (t n) -> p t n", n=2)
        self.ss, self.rstd = s[:, small_at + 10:small_at + 15], s[:, small_at + 15:small_at + 20]
        self.sq, self.var, self.root, self.added = sem("row_squares"), sem("row_variance"), sem("row_root"), sem("rows_added")

    def rows(self, t):
        return (self.g["res"][:, t, :], P) if t < TT else (self.g["meta"][0:META, :], META)

    def act(self, act, t, banks, squares):
        _, n = self.rows(t)
        for i, bank in enumerate(banks):
            if 2 * t + i:
                act.wait_ge(self.sq, 2 * t + i)
            act.activation(squares[0:n, 0:512], self.g["psum"][0:n, bank, :], ACT.Square,
                           accum_out=self.parts[0:n, t, i:i + 1]).then_inc(self.sq, 1)
        act.wait_ge(self.var, t + 1)
        act.activation(self.rstd[0:n, t:t + 1], self.ss[0:n, t:t + 1], ACT.Sqrt).then_inc(self.root, 1)

    def dve(self, dve, step, t, banks, gain, tmp):
        rows, n = self.rows(t)
        rstd = self.rstd[0:n, t:t + 1]
        dve.wait_ge(self.sq, 2 * t + 2)
        step(dve.tensor_tensor(self.ss[0:n, t:t + 1], self.parts[0:n, t, 0:1], self.parts[0:n, t, 1:2], ALU.add))
        dve.tensor_scalar(self.ss[0:n, t:t + 1], self.ss[0:n, t:t + 1], 1.0 / D, EPS, ALU.mult, ALU.add).then_inc(self.var, 1)
        dve.wait_ge(self.root, t + 1)
        step(dve.reciprocal(rstd, rstd))
        for i, bank in enumerate(banks):
            c = slice(512 * i, 512 * i + 512)
            step(dve.scalar_tensor_tensor(out=tmp[0:n, c], in0=self.g["psum"][0:n, bank, :], scalar=rstd, in1=gain[0:n, c],
                                          op0=ALU.mult, op1=ALU.mult))
        dve.tensor_tensor(rows, rows, tmp[0:n, 0:D], ALU.add).then_inc(self.added, 1)


def mix_and_project(g):
    nc, a, psum, arena, spare, small = g["nc"], g["a"], g["psum"], g["arena"], g["spare"], g["small"]
    hnT, later, at2, ident, sbT, oT = g["hnT"], g["later"], g["at2"], g["ident"], g["sbT"], g["oT"]
    b = g["base"] + 12 * L2
    mixT = arena[:, b:b + KT * L2].rearrange("p (k n) -> p k n", k=KT)
    b += KT * L2
    sg = arena[:, b:b + KT * L2].rearrange("p (k n) -> p k n", k=KT)
    b += KT * L2
    tmp = arena[:, b:b + 2 * HALF].rearrange("p (i n) -> p i n", i=2)
    b += 2 * HALF
    gain = arena[:, b:b + D]
    part = arena[:, b + D:b + 2 * D]
    squares = arena[:, b + 2 * D:b + 3 * D]
    hn = sg.rearrange("p k n -> p (k n)")[:, 0:2 * D].rearrange("p (i n) -> p i n", i=2)
    ss, rstd = small[:, 400:405], small[:, 405:410]
    BANKS = [0, 1, 2, 3]
    GR, GLA, SBG, SBO, WO = 0, 16, 48, 64, 80

    with ExitStack() as cx:
        sem, dma_sem = g["semaphores"](cx)
        loads = dma_sem("mix_gain_loaded")
        ready, taken, gate_ok = sem("mixing_in_psum"), sem("mixing_taken"), sem("gate_ready")
        gated, mixed, dstep = sem("linear_output_gated"), sem("mix_ready"), sem("mix_dve_step")
        wo_ps = sem("wo_in_psum")
        sq2, var2, root2, hn_ok, hn_ps, hn_sb = (sem("h2_squares"), sem("h2_variance"), sem("h2_root"), sem("hn2_ready"),
                                                 sem("hn2T_in_psum"), sem("hn2T_ready"))
        post = PostNorm(g, sem, 360)
        block = cx.enter_context(nc.Block())
        WB = [(0, 1), (2, 3)]

        def read(n):
            if n < GLA:
                return gate_ok, n + 1
            if n < SBG:
                c, i = divmod(n - GLA, 16)
                return (gate_ok, GLA + 8 * c + i + 1) if i < 8 else (taken, 8 * c + i - 8 + 1)
            return (gate_ok, 32 + n - SBG + 1) if n < SBO else (taken, 16 + n - SBO + 1)

        @block.tensor
        def _(pe):
            st = [0]

            def use(kind, n):
                return later.use(pe, at2[kind][n])

            def turned(kind, n, x, **kw):
                w = use(kind, n).rearrange("p (k n) -> p k n", k=kw.get("k_tiles", KT))
                products(pe, psum, BANKS, ready, read, st, turned_pieces(w, x, **kw))
                later.read_by(at2[kind][n], ready, st[0])

            turned("proj", 7, hnT)
            turned("proj", 8, hnT)
            pe.wait_ge(gated, 16)
            for c in range(2):
                turned("mgla", c, hnT)
                turned("gout", c, oT)
            for c in range(2):
                turned("msb", c, hnT)
            turned("sbout", 0, sbT, k_tiles=4, m_tiles=8)
            pe.wait_ge(taken, 32)
            pe.wait_ge(mixed, 1)
            w = [use("wo", n).rearrange("p (k n) -> p k n", k=KT) for n in range(2)]
            pieces = [row_pieces(w[n], mixT) for n in range(2)]

            def turn(t):
                n = P if t < TT else META
                pe.wait_ge(hn_ok, t + 1)
                for half in range(2):
                    if t >= 2:
                        pe.wait_ge(hn_sb, 2 * (t - 2) + half + 1)
                    for k in range(4):
                        last = pe.transpose(psum[:, 4 + 2 * (t % 2) + half, k * P:k * P + n],
                                            hn[0:n, t % 2, (4 * half + k) * P:(4 * half + k + 1) * P], ident[0:n, 0:n])
                    last.then_inc(hn_ps, 1)

            for t in range(TT + 1):
                if t >= 2:
                    pe.wait_ge(post.added, t - 1)
                for n in range(2):
                    rows, width, pairs = pieces[n][t]
                    for i, (lhsT, rhs) in enumerate(pairs):
                        last = pe.matmul(psum[0:rows, WB[t % 2][n], :], lhsT, rhs, start=(i == 0), stop=(i == KT - 1))
                    last.then_inc(wo_ps, 1)
                if t >= 2:
                    turn(t - 2)
            later.read_by(at2["wo"][0], wo_ps, 9)
            later.read_by(at2["wo"][1], wo_ps, 10)
            turn(TT - 1)
            turn(TT)

        @block.scalar
        def _(act):
            def gate(n, dst, func):
                act.wait_ge(ready, n + 1)
                act.activation(dst, psum[:, BANKS[n % 4], 0:HALF], func).then_inc(gate_ok, 1)

            half = lambda x, n: x[:, n // 2, (n % 2) * HALF:(n % 2 + 1) * HALF]
            for n in range(16):
                if n >= 2:
                    act.wait_ge(gated, n - 1)
                gate(GR + n, tmp[:, n % 2, :], ACT.Silu)
            for c in range(2):
                if c:
                    act.wait_ge(taken, 8)
                for n in range(8):
                    gate(GLA + 16 * c + n, half(sg, n), ACT.Sigmoid)
            act.wait_ge(taken, 16)
            for n in range(16):
                gate(SBG + n, half(sg, n), ACT.Sigmoid)

            def second_half(t):
                rows, n = post.rows(t)
                act.wait_ge(post.added, t + 1)
                act.wait_ge(post.sq, 2 * t + 2)
                if t:
                    act.wait_ge(sq2, t)
                act.activation(squares[0:n, :], rows, ACT.Square, accum_out=ss[0:n, t:t + 1]).then_inc(sq2, 1)
                act.wait_ge(var2, t + 1)
                act.activation(rstd[0:n, t:t + 1], ss[0:n, t:t + 1], ACT.Sqrt).then_inc(root2, 1)

            def take(t):
                n, c = (P, META + t * P) if t < TT else (META, 0)
                for i in range(2):
                    act.wait_ge(hn_ps, 2 * t + i + 1)
                    for k in range(4):
                        last = act.activation(hnT[:, 4 * i + k, c:c + n], psum[:, 4 + 2 * (t % 2) + i, k * P:k * P + n],
                                              ACT.Copy, scale=col(g, "norm_ffn_pre_2")[:, 4 * i + k:4 * i + k + 1])
                    last.then_inc(hn_sb, 1)

            for t in range(TT + 2):
                if t <= TT:
                    act.wait_ge(wo_ps, 2 * t + 2)
                    if t:
                        act.wait_ge(sq2, t)
                    post.act(act, t, WB[t % 2], squares)
                    second_half(t)
                if t >= 1:
                    take(t - 1)

        @block.vector
        def _(dve):
            step = Steps(dve, dstep)
            half = lambda x, n: x[:, n // 2, (n % 2) * HALF:(n % 2 + 1) * HALF]
            bank = lambda n: psum[:, BANKS[n % 4], 0:HALF]
            for n in range(16):
                dve.wait_ge(gate_ok, n + 1)
                dve.scalar_tensor_tensor(out=half(oT, n), in0=tmp[:, n % 2, :], scalar=col(g, "gla_head_norm_2")[:, (n // 2) % 2:(n // 2) % 2 + 1],
                                         in1=half(oT, n), op0=ALU.mult, op1=ALU.mult).then_inc(gated, 1)
            for c in range(2):
                for n in range(8):
                    dve.wait_ge(gate_ok, 16 + 8 * c + n + 1)
                    dve.wait_ge(ready, GLA + 16 * c + 8 + n + 1)
                    dve.tensor_tensor(half(mixT, 8 * c + n), half(sg, n), bank(n), ALU.mult).then_inc(taken, 1)
            dve.wait_ge(taken, 16)
            for n in range(16):
                dve.wait_ge(gate_ok, 32 + n + 1)
                dve.wait_ge(ready, SBO + n + 1)
                dve.tensor_tensor(half(sg, n), half(sg, n), bank(n), ALU.mult).then_inc(taken, 1)
                dve.wait_ge(taken, 16 + n + 1)
                step(dve.tensor_tensor(half(mixT, n), half(mixT, n), half(sg, n), ALU.add))
            dve.engine_nop().then_inc(mixed, 1)
            dve.wait_ge(loads, 16)

            def rows_out(t):
                rows, n = post.rows(t)
                dve.wait_ge(sq2, t + 1)
                dve.tensor_scalar(ss[0:n, t:t + 1], ss[0:n, t:t + 1], 1.0 / D, EPS, ALU.mult, ALU.add).then_inc(var2, 1)
                dve.wait_ge(root2, t + 1)
                step(dve.reciprocal(rstd[0:n, t:t + 1], rstd[0:n, t:t + 1]))
                if t >= 2:
                    dve.wait_ge(hn_ps, 2 * (t - 1))
                dve.tensor_scalar(hn[0:n, t % 2, :], rows, rstd[0:n, t:t + 1], None, ALU.mult).then_inc(hn_ok, 1)

            for t in range(TT + 1):
                post.dve(dve, step, t, WB[t % 2], gain, part)
                dve.wait_ge(post.added, t + 1)
                rows_out(t)

        @block.sync
        def _(sp):
            sp.dma_start(gain, a["norm_mix_post_2"].to_broadcast([P, D])).then_inc(loads, 16)
            later.load_until(sp, at2["wo"][1] + 1 + SLOTS)
    later.new_phase()


def feed_forward(g):
    nc, a, psum, arena, spare, small = g["nc"], g["a"], g["psum"], g["arena"], g["spare"], g["small"]
    hnT, later, at2, res = g["hnT"], g["later"], g["at2"], g["res"]
    b = g["base"] + KT * L2
    prodT = arena[:, b:b + FM * SEQ].rearrange("p (m n) -> p m n", m=FM)
    UP = SEQ + 2
    up = spare[:, 0:2 * UP].rearrange("p (i n) -> p i n", i=2)
    y = spare[:, 1028:1028 + 1024].rearrange("p (i n) -> p i n", i=2)
    gain, part, squares = spare[:, 2052:2052 + D], spare[:, 3076:3076 + D], spare[:, 4100:4100 + D]
    BANKS = [0, 1, 2, 3, 4, 5]
    convw = lambda j, m: g["convw2"][:, j * FM + m:j * FM + m + 1]
    with ExitStack() as cx:
        sem, dma_sem = g["semaphores"](cx)
        loads, stored = dma_sem("ffn_gain_loaded"), dma_sem("output_stored")
        ready, taken, dstep = sem("ffn_in_psum"), sem("ffn_taken"), sem("ffn_dve_step")
        up_ok, conv_ok, act_ok, prod_ok = sem("up_ready"), sem("ffn_conv_ready"), sem("gelu_ready"), sem("product_ready")
        chunk_read, acc = sem("down_chunk_read"), sem("down_in_psum")
        post = PostNorm(g, sem, 420)
        block = cx.enter_context(nc.Block())

        @block.tensor
        def _(pe):
            n = 0
            chunks = len(at2["up"])
            for c in range(chunks):
                tiles = min(4, FM - 4 * c)
                wu = later.use(pe, at2["up"][c])[:, 0:KT * tiles * P].rearrange("p (k n) -> p k n", k=KT)
                wg = later.use(pe, at2["gate"][c])[:, 0:KT * tiles * P].rearrange("p (k n) -> p k n", k=KT)
                for m in range(tiles):
                    for w, lo, width in ((wu, META - 2, UP // 2), (wu, META - 2 + UP // 2, UP // 2), (wg, META, SEQ)):
                        if n >= 6:
                            pe.wait_ge(taken if n % 3 < 2 else prod_ok, 2 * ((n - 6) // 3) + n % 3 + 1 if n % 3 < 2 else (n - 6) // 3 + 1)
                        for k in range(KT):
                            last = pe.matmul(psum[:, n % 6, 0:width], w[:, k, m * P:(m + 1) * P], hnT[:, k, lo:lo + width],
                                             start=(k == 0), stop=(k == KT - 1))
                        last.then_inc(ready, 1)
                        n += 1
                later.read_by(at2["up"][c], ready, n - 1)
                later.read_by(at2["gate"][c], ready, n)
            pe.wait_ge(prod_ok, FM)
            for c in range(len(at2["down"])):
                tiles = min(4, FM - 4 * c)
                w = later.use(pe, at2["down"][c])[:, 0:tiles * D].rearrange("p (k n) -> p k n", k=tiles)
                final = c == len(at2["down"]) - 1
                order = ([(t, k) for t in range(TT) for k in range(tiles)] if final else
                         [(t, k) for k in range(tiles) for t in range(TT)])
                for t, k in order:
                    for i in range(2):
                        kk = 4 * c + k
                        last = pe.matmul(psum[:, 2 * t + i, :], prodT[:, kk, t * P:(t + 1) * P], w[:, k, 512 * i:512 * i + 512],
                                         start=(kk == 0), stop=(kk == FM - 1))
                    if final and k == tiles - 1:
                        last.then_inc(acc, 1)
                if not final:
                    last.then_inc(chunk_read, 1)
                    later.read_by(at2["down"][c], chunk_read, c + 1)

        @block.scalar
        def _(act):
            for m in range(FM):
                if m >= 2:
                    act.wait_ge(conv_ok, m - 1)
                for i in range(2):
                    act.wait_ge(ready, 3 * m + i + 1)
                    act.activation(up[:, m % 2, i * (UP // 2):(i + 1) * (UP // 2)], psum[:, (3 * m + i) % 6, 0:UP // 2],
                                   ACT.Copy).then_inc(taken, 1)
                if m:
                    act.wait_ge(conv_ok, m)
                    act.activation(y[:, (m - 1) % 2, :], y[:, (m - 1) % 2, :], ACT.Gelu_apprx_tanh).then_inc(act_ok, 1)
            act.wait_ge(conv_ok, FM)
            act.activation(y[:, (FM - 1) % 2, :], y[:, (FM - 1) % 2, :], ACT.Gelu_apprx_tanh).then_inc(act_ok, 1)
            for t in range(TT):
                act.wait_ge(acc, t + 1)
                post.act(act, t, (2 * t, 2 * t + 1), squares)

        @block.vector
        def _(dve):
            step = Steps(dve, dstep)

            def conv(m):
                dve.wait_ge(taken, 2 * m + 2)
                src, dst = up[:, m % 2, :], y[:, m % 2, :]
                if m >= 2:
                    dve.wait_ge(prod_ok, m - 1)
                step(dve.tensor_scalar(dst, src[:, 0:SEQ], convw(0, m), col(g, "conv_b_2")[:, m:m + 1], ALU.mult, ALU.add))
                step(dve.scalar_tensor_tensor(out=dst, in0=src[:, 1:SEQ + 1], scalar=convw(1, m), in1=dst, op0=ALU.mult, op1=ALU.add))
                dve.scalar_tensor_tensor(out=dst, in0=src[:, 2:SEQ + 2], scalar=convw(2, m), in1=dst, op0=ALU.mult,
                                         op1=ALU.add).then_inc(conv_ok, 1)

            def product(m):
                dve.wait_ge(act_ok, m + 1)
                dve.wait_ge(ready, 3 * m + 3)
                dve.tensor_tensor(prodT[:, m, :], y[:, m % 2, :], psum[:, (3 * m + 2) % 6, :], ALU.mult).then_inc(prod_ok, 1)

            for m in range(FM):
                conv(m)
                if m:
                    product(m - 1)
            product(FM - 1)
            dve.wait_ge(loads, 16)
            for t in range(TT):
                if t:
                    dve.wait_ge(post.added, t)
                post.dve(dve, step, t, (2 * t, 2 * t + 1), gain, part)

        @block.sync
        def _(sp):
            sp.dma_start(gain, a["norm_ffn_post_2"].to_broadcast([P, D])).then_inc(loads, 16)
            later.load_until(sp, len(later.chunks))
            for t in range(TT):
                sp.wait_ge(post.added, t + 1)
                sp.dma_start(g["out"][0, t * P:(t + 1) * P, :], res[:, t, :]).then_inc(stored, 16)
            sp.wait_ge(stored, 16 * TT)
    later.new_phase()


def second_block(g):
    stick_breaking(g)
    gated_linear(g)
    mix_and_project(g)
    feed_forward(g)


_INS = ["x", "c", "w_mod", "b_mod", "g_norm1", "w_in", "conv_w", "conv_b", "conv_ln_g", "conv_ln_b", "w_out", "g_norm2",
        "w_router_group", "b_router_group", "w_router_expert", "b_router_expert", "w_exp_gate", "w_exp_up", "w_exp_down",
        "g_final", "meta_tokens_2", "norm_mix_pre_2", "w_in_2", "w_gk_up_2", "b_gk_2", "gla_head_norm_2", "w_sb_out_2",
        "w_gla_out_2", "w_o_2", "norm_mix_post_2", "norm_ffn_pre_2", "w_ffn_up_2", "w_ffn_gate_2", "conv_w_2", "conv_b_2",
        "w_ffn_down_2", "norm_ffn_post_2"]


def kernel(**inputs):
    import numpy as _np
    import concourse.bacc as _bacc
    from concourse import mybir as _mybir
    from concourse.bass_utils import run_bass_kernel_spmd as _run

    nc = _bacc.Bacc("TRN2", target_bir_lowering=False, num_devices=1)
    arrays, args = {}, {}
    for name in _INS:
        x = _np.ascontiguousarray(inputs[name])
        arrays[f"in_{name}_dram"] = x
        args[name] = nc.dram_tensor(f"in_{name}_dram", x.shape, _mybir.dt.from_np(x.dtype), kind="ExternalInput").ap()
    out = nc.dram_tensor("out_0_dram", (1, SEQ, D), _mybir.dt.float32, kind="ExternalOutput").ap()
    build_program(nc, args, out)
    r = _run(nc, [arrays], core_ids=[0])
    return r.results[0]["out_0_dram"]
```

```python
from contextlib import ExitStack

import concourse.bass as bass
from concourse import mybir

ALU = mybir.AluOpType
ACT = mybir.ActivationFunctionType
F32 = mybir.dt.float32
I32 = mybir.dt.int32
F32R = mybir.dt.float32r
U32 = mybir.dt.uint32
AX_X = mybir.AxisListType.X

P = 128
D = 1024
KT = D // P
SEQ = 512
TT = SEQ // P
META = 16
L2 = SEQ + META
HALF = L2 // 2
CHUNK = 4096
SLOTS = 4
EPS = 1e-6
NEG = -1.0e30

HEADS, HD = 8, 64
TAPS = 31
CM = 512 // P
MOD_DVE_TILES = 6
PE_TAPS = 12
POOL_TAPS = 12
UNIT_TAPS = -(-PE_TAPS // 8)
SLOPES = [2.0 ** (-8.0 * (h + 1) / HEADS) for h in range(HEADS)]

GROUPS, PER_GROUP, EXPERTS, FE = 4, 8, 32, 512
BLOCKS = EXPERTS + (2 * SEQ - EXPERTS) // P
BLOCKS += BLOCKS % 2
TABLE = BLOCKS + 2

GH, DK, DV = 4, 128, 256
LEVELS = 7
FF = 2816
FM = FF // P
COMPUTE_SEMAPHORES = range(140, 256)
ZERO_STORES = 8
HALF_BLOCK = P // 2


class Steps:

    def __init__(self, eng, sem):
        self.eng, self.sem, self.n = eng, sem, 0

    def __call__(self, ins):
        self.n += 1
        ins.then_inc(self.sem, 1)
        self.eng.wait_ge(self.sem, self.n)


class Stream:

    def __init__(self, ring, arrived, chunks):
        self.ring, self.arrived, self.chunks = ring, arrived, chunks
        self.issued, self.readers, self.phase_start = 0, {}, 0

    def load_until(self, sp, n):
        while self.issued < min(n, len(self.chunks)):
            c = self.issued
            if c - SLOTS in self.readers:
                sem, value = self.readers[c - SLOTS]
                sp.wait_ge(sem, value)
            dst, src = self.chunks[c](self.ring[:, c % SLOTS, :])
            sp.dma_start(dst, src).then_inc(self.arrived[c % SLOTS], 16)
            self.issued += 1

    def use(self, eng, n):
        eng.wait_ge(self.arrived[n % SLOTS], 16 * (n // SLOTS + 1))
        return self.ring[:, n % SLOTS, :]

    def read_by(self, n, sem, value):
        self.readers[n] = (sem, value)

    def new_phase(self):
        self.readers = {}


def columns_chunk(w, c0, width=512):
    def make(slot):
        dst = slot[:, 0:KT * width].rearrange("p (k n) -> p k n", k=KT)
        return dst, w[:, c0:c0 + width].rearrange("(k p) n -> p k n", p=P)
    return make


def rows_chunk(w, r0, rows):
    def make(slot):
        k = rows // P
        dst = slot[:, 0:k * D].rearrange("p (k n) -> p k n", k=k)
        return dst, w[r0:r0 + rows, :].rearrange("(k p) n -> p k n", p=P)
    return make


def build_program(nc, a, out):
    ctx = ExitStack()
    with ctx:
        fixed = 24200
        fixed_mem = ctx.enter_context(nc.sbuf_tensor("fixed", [P, fixed], F32))
        psum = ctx.enter_context(nc.psum_tensor("psum", [P, 8, 512], F32))
        scratch = {
            "h2": nc.dram_tensor("h2_rows", (SEQ, D), F32, kind="Internal").ap(),
            "y": nc.dram_tensor("expert_rows", (BLOCKS * P, D), F32, kind="Internal").ap(),
        }
        place = [0]

        def region(n):
            place[0] += n
            assert place[0] <= fixed, place[0]
            return fixed_mem[:, place[0] - n:place[0]]

        ring = region(SLOTS * CHUNK).rearrange("p (s n) -> p s n", s=SLOTS)
        ident = region(P)
        ones = region(P)
        before = region(P)
        upto = region(P)
        future = region(P)
        cols1 = region(72)
        convw = region(TAPS * CM)
        convw2 = region(3 * FM)
        small = region(640)
        res = region(TT * D).rearrange("p (t n) -> p t n", t=TT)
        meta = region(D)
        gt2 = region(D)
        base = 2 * CHUNK
        floats = 29000

        counter = [COMPUTE_SEMAPHORES.start]

        def semaphores(cx):
            def sem(name):
                counter[0] += 1
                return cx.enter_context(nc.semaphore(name, num=counter[0] - 1))
            return sem, lambda name: cx.enter_context(nc.semaphore(name))

        arrived = [ctx.enter_context(nc.semaphore(f"weights_arrived{i}")) for i in range(SLOTS)]
        arrived2 = [ctx.enter_context(nc.semaphore(f"later_weights_arrived{i}")) for i in range(SLOTS)]

        expert_arrived = [ctx.enter_context(nc.semaphore(f"expert_{kind}_arrived")) for kind in ("gate", "up", "down")]
        table_zeroed = ctx.enter_context(nc.semaphore("expert_rows_zeroed"))

        w_mod, w_in, w_out = a["w_mod"][0], a["w_in"][0], a["w_out"][0]
        mod = lambda c: ("mod", columns_chunk(w_mod, 512 * c))
        win = lambda c: ("win", columns_chunk(w_in, 512 * c))
        plan = [mod(0), mod(1), mod(2), mod(3), win(0), mod(4), win(1), mod(5), win(2), mod(6), mod(7), win(3),
                mod(8), mod(9), win(4), mod(10), mod(11),
                ("wout", columns_chunk(w_out, 0)), ("wout", columns_chunk(w_out, 512))]
        at = {}
        for n, (kind, _) in enumerate(plan):
            at.setdefault(kind, []).append(n)
        first = Stream(ring, arrived, [c for _, c in plan])

        w_in2 = a["w_in_2"][0]
        plan2 = [("proj", columns_chunk(w_in2, 512 * c)) for c in range(9)]
        plan2 += [("mgla", columns_chunk(w_in2, 4624 + 1024)), ("gout", columns_chunk(a["w_gla_out_2"][0], 0)),
                  ("mgla", columns_chunk(w_in2, 4624 + 1536)), ("gout", columns_chunk(a["w_gla_out_2"][0], 512)),
                  ("msb", columns_chunk(w_in2, 4624)), ("msb", columns_chunk(w_in2, 4624 + 512)),
                  ("sbout", rows_chunk(a["w_sb_out_2"][0], 0, 512)),
                  ("wo", columns_chunk(a["w_o_2"][0], 0)), ("wo", columns_chunk(a["w_o_2"][0], 512))]
        for c0 in range(0, FF, 512):
            width = min(512, FF - c0)
            plan2 += [("up", columns_chunk(a["w_ffn_up_2"][0], c0, width)),
                      ("gate", columns_chunk(a["w_ffn_gate_2"][0], c0, width))]
        for r0 in range(0, FF, 512):
            plan2 += [("down", rows_chunk(a["w_ffn_down_2"][0], r0, min(512, FF - r0)))]
        at2 = {}
        for n, (kind, _) in enumerate(plan2):
            at2.setdefault(kind, []).append(n)
        later = Stream(ring, arrived2, [c for _, c in plan2])

        g = dict(semaphores=semaphores, table_zeroed=table_zeroed, expert_arrived=expert_arrived,
                 nc=nc, a=a, psum=psum, dram=scratch, ring=ring, gt2=gt2, ident=ident, ones=ones, before=before,
                 upto=upto, future=future, cols1=cols1, convw=convw, convw2=convw2, small=small, res=res, meta=meta,
                 base=base, first=first, later=later, at=at, at2=at2, out=out, floats=floats)

        with nc.sbuf_tensor("first_block_memory", [P, floats], F32) as arena:
            g["arena"], g["spare"] = arena, arena[:, 0:base]
            prologue(g)
            input_projection(g)
            attention_and_conv(g)
            output_and_routing(g)
        experts(g)
        arena = ctx.enter_context(nc.sbuf_tensor("second_block_memory", [P, floats], F32))
        g["arena"], g["spare"] = arena, arena[:, 0:base]
        combine(g)
        nc.sync.sem_clear(COMPUTE_SEMAPHORES)
        nc.all_engine_barrier()
        counter[0] = COMPUTE_SEMAPHORES.start
        second_block(g)


COLS = [("c", 8), ("g_norm1", 8), ("conv_b", 4), ("conv_ln_g", 4), ("conv_ln_b", 4), ("b_gk_2", 4),
        ("gla_head_norm_2", 2), ("norm_mix_pre_2", 8), ("norm_ffn_pre_2", 8), ("conv_b_2", 22)]


def col(g, name):
    at = 0
    for n, k in COLS:
        if n == name:
            return g["cols1"][:, at:at + k]
        at += k


def mod_step(g, dve, step, n, chunk, slot, k_tiles=KT):
    acc = g["modacc"][:, 512 * chunk:512 * chunk + 512]
    w = slot.rearrange("p (k n) -> p k n", k=KT)
    for k in range(k_tiles):
        step(dve.scalar_tensor_tensor(out=acc, in0=w[:, k, :], scalar=g["csil"][:, k:k + 1], in1=acc,
                                      op0=ALU.mult, op1=ALU.add))
    if k_tiles == KT:
        g["first"].read_by(n, step.sem, step.n)


def prologue(g):
    nc, a, psum, base, arena = g["nc"], g["a"], g["psum"], g["base"], g["arena"]
    at, first = g["at"], g["first"]
    g["modacc"] = modacc = arena[:, base:base + 6144]
    base2 = base + 6144
    g["hT"] = hT = arena[:, base2:base2 + 4096].rearrange("p (k n) -> p k n", k=KT)
    spare, small = g["spare"], g["small"]
    rows1, rows2, rows3 = spare[:, 0:P], spare[:, P:2 * P], spare[:, 2 * P:3 * P]
    squares = spare[:, 512:512 + D]
    xn = spare[:, 2048:2048 + 4096].rearrange("p (t n) -> p t n", t=TT)
    g["csil"] = csil = small[:, 0:8]
    ss, rstd, A, modc = small[:, 8:12], small[:, 12:16], small[:, 16:24], small[:, 24:40]
    cbar, ident, ones = ExitStack(), g["ident"], g["ones"]
    res = g["res"]
    with cbar:
        sem, dma_sem = g["semaphores"](cbar)
        params, x_in, bias_in = dma_sem("params_loaded"), dma_sem("x_loaded"), dma_sem("mod_bias_loaded")
        built, zeroed = sem("constants_built"), sem("mod_sums_zeroed")
        act_step, dve_step = sem("p0_act_step"), sem("p0_dve_step")
        cols_ps, cols_sb, c_ready = sem("columns_in_psum"), sem("columns_in_sbuf"), sem("silu_c_ready")
        ssq, var, root, normed = sem("x_squares"), sem("x_variance"), sem("x_root"), sem("x_normed")
        mod_sum, mod_ps, scale_ok = sem("mod_sums_ready"), sem("mod_columns_in_psum"), sem("scale_ready")
        xT_ps, xT_sb = sem("xT_in_psum"), sem("hT_ready")
        block = cbar.enter_context(nc.Block())

        @block.gpsimd
        def _(pool):
            step = Steps(pool, built)
            step(pool.memset(g["ident"], 0.0))
            step(pool.memset(g["ones"], 1.0))
            step(pool.memset(g["future"], 0.0))
            step(pool.affine_select(out=g["ident"], in_=g["ident"], compare_op=ALU.not_equal, fill=1.0, base=0,
                                    pattern=[[-1, P]], channel_multiplier=1))
            pool.memset(modacc, 0.0).then_inc(zeroed, 1)
            step(pool.affine_select(out=g["before"], in_=g["ones"], compare_op=ALU.is_gt, fill=0.0, base=0,
                                    pattern=[[1, P]], channel_multiplier=-1))
            step(pool.affine_select(out=g["upto"], in_=g["ones"], compare_op=ALU.is_ge, fill=0.0, base=0,
                                    pattern=[[-1, P]], channel_multiplier=1))
            step(pool.affine_select(out=g["future"], in_=g["future"], compare_op=ALU.is_gt, fill=NEG, base=0,
                                    pattern=[[1, P]], channel_multiplier=-1))

        n_params = len(COLS) + 2

        @block.scalar
        def _(act):
            r = 0
            for name, k in COLS:
                src = a[name].rearrange("a (k p) -> (a k) p", p=P)
                act.dma_start(rows1[r:r + k, :], src).then_inc(params, 16)
                r += k
            act.dma_start(rows2[0:TAPS * CM, :], a["conv_w"][0].rearrange("j (m p) -> (j m) p", p=P)).then_inc(params, 16)
            act.dma_start(rows3[0:3 * FM, :], a["conv_w_2"][0].rearrange("j (m p) -> (j m) p", p=P)).then_inc(params, 16)
            act.wait_ge(x_in, 16)
            for t in range(TT):
                if t:
                    act.wait_ge(ssq, t)
                act.activation(squares, res[:, t, :], ACT.Square, accum_out=ss[:, t:t + 1]).then_inc(ssq, 1)
            act.wait_ge(cols_ps, 3)
            act.activation(g["cols1"], psum[:, 0, 0:72], ACT.Copy).then_inc(cols_sb, 1)
            act.activation(csil, psum[:, 0, 0:8], ACT.Silu).then_inc(c_ready, 1)
            act.activation(g["convw"], psum[:, 1, 0:TAPS * CM], ACT.Copy).then_inc(cols_sb, 1)
            act.activation(g["convw2"], psum[:, 2, 0:3 * FM], ACT.Copy).then_inc(cols_sb, 1)
            act.wait_ge(var, 1)
            act.activation(rstd, rstd, ACT.Sqrt).then_inc(root, 1)
            act.wait_ge(scale_ok, 2)
            for k in range(KT):
                act.wait_ge(xT_ps, k + 1)
                act.activation(hT[:, k, :], psum[:, 4 + k % 4, :], ACT.Identity, bias=modc[:, k:k + 1],
                               scale=A[:, k:k + 1]).then_inc(xT_sb, 1)

        @block.vector
        def _(dve):
            step = Steps(dve, dve_step)
            dve.wait_ge(ssq, TT)
            dve.tensor_scalar(rstd, ss, 1.0 / D, EPS, ALU.mult, ALU.add).then_inc(var, 1)
            dve.wait_ge(root, 1)
            step(dve.reciprocal(rstd, rstd))
            for t in range(TT):
                dve.tensor_scalar(xn[:, t, :], res[:, t, :], rstd[:, t:t + 1], None, ALU.mult).then_inc(normed, 1)
            dve.wait_ge(zeroed, 1)
            dve.wait_ge(bias_in, 16)
            dve.wait_ge(c_ready, 1)
            for c in range(4):
                n = at["mod"][c]
                slot = first.use(dve, n)
                mod_step(g, dve, step, n, c, slot, MOD_DVE_TILES)
                dve.engine_nop().then_inc(mod_sum, 1)
            dve.wait_ge(mod_ps, 4)
            dve.wait_ge(cols_sb, 1)
            step(dve.tensor_copy(modc, psum[:, 3, 0:16]))
            dve.tensor_tensor(modc, modc, psum[:, 3, 16:32], ALU.add).then_inc(scale_ok, 1)
            dve.wait_ge(scale_ok, 1)
            dve.scalar_tensor_tensor(out=A, in0=modc[:, 8:16], scalar=1.0, in1=col(g, "g_norm1"), op0=ALU.add,
                                     op1=ALU.mult).then_inc(scale_ok, 1)

        @block.tensor
        def _(pe):
            pe.wait_ge(built, 4)
            pe.wait_ge(params, 16 * n_params)
            for i, (rows, n) in enumerate(((rows1, 72), (rows2, TAPS * CM), (rows3, 3 * FM))):
                pe.transpose(psum[:, i, 0:n], rows[0:n, :], ident[0:n, 0:n]).then_inc(cols_ps, 1)
            def turn(k):
                if k >= 4:
                    pe.wait_ge(xT_sb, k - 3)
                for t in range(TT):
                    last = pe.transpose(psum[:, 4 + k % 4, t * P:(t + 1) * P], xn[:, t, k * P:(k + 1) * P], ident)
                last.then_inc(xT_ps, 1)

            pe.wait_ge(c_ready, 1)
            for chunk in range(4):
                w = first.use(pe, at["mod"][chunk]).rearrange("p (k n) -> p k n", k=KT)
                for c in range(4):
                    for k in range(MOD_DVE_TILES, KT):
                        last = pe.matmul(psum[:, 3, 4 * chunk + c:4 * chunk + c + 1], w[:, k, c * P:(c + 1) * P], csil[:, k:k + 1],
                                         start=(k == MOD_DVE_TILES), stop=(k == KT - 1))
                pe.wait_ge(mod_sum, chunk + 1)
                for c in range(4 * chunk, 4 * chunk + 4):
                    last = pe.matmul(psum[:, 3, 16 + c:17 + c], modacc[:, c * P:(c + 1) * P], ones[:, 0:1], start=True, stop=True)
                last.then_inc(mod_ps, 1)
                first.read_by(at["mod"][chunk], mod_ps, chunk + 1)
                if chunk == 1:
                    pe.wait_ge(normed, TT)
                    for k in range(4):
                        turn(k)
            for k in range(4, KT):
                turn(k)

        @block.sync
        def _(sp):
            sp.dma_start(res, a["x"][0].rearrange("(t p) n -> p t n", p=P)).then_inc(x_in, 16)
            sp.wait_ge(zeroed, 1)
            sp.dma_start(modacc[0:1, :], a["b_mod"]).then_inc(bias_in, 16)
            first.load_until(sp, 8)
    first.new_phase()


def input_projection(g):
    nc, a, psum, arena = g["nc"], g["a"], g["psum"], g["arena"]
    at, first, hT, modacc = g["at"], g["first"], g["hT"], g["modacc"]
    b = g["base"] + 6144 + 4096
    g["qT"] = qT = modacc[:, 0:2048].rearrange("p (m n) -> p m n", m=4)
    g["kz"] = kz = arena[:, b:b + 4096].rearrange("p (h n) -> p h n", h=HEADS)
    g["v"] = v = arena[:, b + 4096:b + 6144].rearrange("p (t n) -> p t n", t=TT)
    UW = TAPS - 1 + SEQ
    g["uT"] = uT = arena[:, b + 6144:b + 6144 + CM * UW].rearrange("p (m n) -> p m n", m=CM)
    g["base_tmp"] = b + 6144 + CM * UW
    sg = g["spare"][:, 0:1024].rearrange("p (i n) -> p i n", i=2)
    g["dist"], g["count"] = dist, count = g["spare"][:, 6144:6656], g["spare"][:, 6656:7168]
    ti, tj = (g["spare"][:, o:o + SEQ].bitcast(I32) for o in (1024, 1536))
    tf = g["spare"][:, 2048:2048 + SEQ]
    with ExitStack() as cx:
        sem, dma_sem = g["semaphores"](cx)
        ready, taken = sem("projection_in_psum"), sem("projection_taken")
        zeroed, dve_step, gated = sem("pads_zeroed"), sem("p1_dve_step"), sem("gated")
        mod_all, iota_ok = sem("mod_sums_done"), sem("distances_counted")
        rows_ps, rows_sb = sem("mod_rows_in_psum"), sem("mod_rows_ready")
        block = cx.enter_context(nc.Block())

        @block.gpsimd
        def _(pool):
            pool.iota(ti, [[-1, SEQ]], base=SEQ - P, channel_multiplier=1).then_inc(iota_ok, 1)
            pool.wait_ge(iota_ok, 1)
            step = Steps(pool, zeroed)
            for h in range(HEADS):
                lo = 64 * (1 - h % 2)
                step(pool.memset(kz[lo:lo + 64, h, :], 0.0))
            step(pool.memset(uT[:, :, 0:TAPS - 1], 0.0))
            step(pool.memset(g["meta"], 0.0))

        @block.tensor
        def _(pe):
            n = 0
            for c in range(5):
                w = first.use(pe, at["win"][c]).rearrange("p (k n) -> p k n", k=KT)
                for m in range(4):
                    if n >= 4:
                        pe.wait_ge(taken, n - 3)
                    for k in range(KT):
                        if c == 2:
                            lhsT, rhs = hT[:, k, m * P:(m + 1) * P], w[:, k, :]
                        else:
                            lhsT, rhs = w[:, k, m * P:(m + 1) * P], hT[:, k, :]
                        last = pe.matmul(psum[:, n % 4, :], lhsT, rhs, start=(k == 0), stop=(k == KT - 1))
                    last.then_inc(ready, 1)
                    n += 1
                first.read_by(at["win"][c], ready, n)
            pe.wait_ge(mod_all, 1)
            for i in range(8):
                if i >= 4:
                    pe.wait_ge(rows_sb, i - 3)
                s = modacc[:, 2048 + 512 * i:2560 + 512 * i]
                pe.matmul(psum[:, 4 + i % 4, :], g["ones"], s, start=True, stop=True).then_inc(rows_ps, 1)

        @block.scalar
        def _(act):
            n = 0
            for c in range(5):
                for m in range(4):
                    act.wait_ge(ready, n + 1)
                    src = psum[:, n % 4, :]
                    if c == 0:
                        act.activation(qT[:, m, :], src, ACT.Copy, scale=HD ** -0.5).then_inc(taken, 1)
                    elif c == 1:
                        act.activation(kz[0:64, 2 * m, :], src[0:64, :], ACT.Copy)
                        act.activation(kz[64:128, 2 * m + 1, :], src[64:128, :], ACT.Copy).then_inc(taken, 1)
                    elif c == 2:
                        act.activation(v[:, m, :], src, ACT.Copy).then_inc(taken, 1)
                    elif c == 3:
                        act.activation(uT[:, m, TAPS - 1:], src, ACT.Copy).then_inc(taken, 1)
                    else:
                        if m >= 2:
                            act.wait_ge(gated, m - 1)
                        act.activation(sg[:, m % 2, :], src, ACT.Sigmoid).then_inc(taken, 1)
                    n += 1
            for i in range(8):
                act.wait_ge(rows_ps, i + 1)
                act.activation(modacc[:, 2048 + 512 * i:2560 + 512 * i], psum[:, 4 + i % 4, :], ACT.Copy).then_inc(rows_sb, 1)

        @block.vector
        def _(dve):
            step = Steps(dve, dve_step)
            dve.wait_ge(iota_ok, 1)
            step(dve.tensor_copy(dist, ti))
            step(dve.tensor_scalar(count, dist, 128.0, None, ALU.is_le))
            for low in (3, 15):
                step(dve.tensor_scalar(tj, ti, low, None, ALU.bitwise_and))
                step(dve.tensor_copy(tf, tj))
                step(dve.scalar_tensor_tensor(out=count, in0=tf, scalar=0.0, in1=count, op0=ALU.is_equal, op1=ALU.add))
            step(dve.scalar_tensor_tensor(out=count, in0=dist, scalar=0.0, in1=count, op0=ALU.is_ge, op1=ALU.mult))
            step(dve.tensor_scalar(tf, count, 0.0, -NEG, ALU.is_equal, ALU.mult))
            step(dve.tensor_tensor(dist, dist, tf, ALU.add))
            for c in range(4, 12):
                n = at["mod"][c]
                mod_step(g, dve, step, n, c, first.use(dve, n))
            dve.engine_nop().then_inc(mod_all, 1)
            for m in range(CM):
                dve.wait_ge(taken, 17 + m)
                dve.tensor_tensor(uT[:, m, TAPS - 1:], uT[:, m, TAPS - 1:], sg[:, m % 2, :], ALU.mult).then_inc(gated, 1)

        @block.sync
        def _(sp):
            first.load_until(sp, len(first.chunks))
    first.new_phase()


def attention_and_conv(g):
    nc, a, psum, arena, spare, dram = g["nc"], g["a"], g["psum"], g["arena"], g["spare"], g["dram"]
    qT, kz, v, uT = g["qT"], g["kz"], g["v"], g["uT"]
    ident, ones = g["ident"], g["ones"]
    g["mixT"] = mixT = g["hT"]
    PT = spare[:, 0:4096].rearrange("p (i j n) -> p i j n", i=2, j=4)
    sc = spare[:, 4096:5120].rearrange("p (i n) -> p i n", i=2)
    pb = spare[:, 5120:6144].rearrange("p (i n) -> p i n", i=2)
    dist, count = g["dist"], g["count"]
    diag = spare[:, 7168:8192].rearrange("p (i n) -> p i n", i=8)
    small = g["small"]
    nmax = small[:, 64:96]
    lsum = small[:, 96:128]
    rl = small[:, 128:160]
    UNITS = HEADS * TT
    assert PE_TAPS + POOL_TAPS + 7 == TAPS
    o = g["base_tmp"]
    yd = arena[:, o:o + SEQ]
    tap_tmp = arena[:, o + SEQ:o + 4 * SEQ].rearrange("p (i n) -> p i n", i=3)
    tap_weight = lambda m, tap: g["convw"][:, tap * CM + m:tap * CM + m + 1]
    with ExitStack() as cx:
        sem, dma_sem = g["semaphores"](cx)
        s_ps, s_sb, mx, e_ok = sem("scores_in_psum"), sem("scores_ready"), sem("max_ready"), sem("exp_ready")
        pw, pt_ps, pt_sb = sem("probs_ready"), sem("probsT_in_psum"), sem("probsT_ready")
        o_ps, o_sb = sem("attn_in_psum"), sem("attn_ready")
        dstep, cstep = sem("attn_dve_step"), sem("conv_dve_step")
        y_done = sem("conv_tile_finished")
        prod_ok, pool_sum = sem("tap_products_ready"), sem("tap_products_summed")
        dg, dg_used = sem("diagonals_built"), sem("diagonals_used")
        c_ps, c_sum = sem("conv_in_psum"), sem("conv_summed")
        mean_ps, cent, sq, var_ps = sem("mean_in_psum"), sem("centred"), sem("squared"), sem("variance_in_psum")
        block = cx.enter_context(nc.Block())

        @block.gpsimd
        def _(pool):
            for m in range(CM):
                for j in range(1, POOL_TAPS):
                    k = m * (POOL_TAPS - 1) + j - 1
                    pool.wait_ge(prod_ok, m * POOL_TAPS + j + 1)
                    y = mixT[:, 4 + m, :]
                    pool.tensor_tensor(y, y, tap_tmp[:, k % 3, :], ALU.add).then_inc(pool_sum, 1)
                    pool.wait_ge(pool_sum, k + 1)

        @block.vector
        def _(dve):
            step = Steps(dve, dstep)
            cs = Steps(dve, cstep)
            def conv_taps(u):
                m, r = u // 8, u % 8
                if r == 0:
                    if m:
                        finish_tile(m - 1)
                    return
                tap = PE_TAPS + POOL_TAPS + r - 1
                w, src = tap_weight(m, tap), uT[:, m, tap:tap + SEQ]
                if r == 1:
                    cs(dve.tensor_scalar(yd, src, w, col(g, "conv_b")[:, m:m + 1], ALU.mult, ALU.add))
                else:
                    cs(dve.scalar_tensor_tensor(out=yd, in0=src, scalar=w, in1=yd, op0=ALU.mult, op1=ALU.add))
                if r == 7:
                    dve.wait_ge(c_ps, m + 1)
                    cs(dve.tensor_tensor(yd, yd, psum[:, 7, :], ALU.add))
                    dve.engine_nop().then_inc(c_sum, 1)

            def finish_tile(m):
                dve.wait_ge(pool_sum, (m + 1) * (POOL_TAPS - 1))
                dve.tensor_tensor(mixT[:, 4 + m, :], mixT[:, 4 + m, :], yd, ALU.add).then_inc(y_done, 1)
                dve.wait_ge(y_done, m + 1)

            def scores(u):
                h, i = divmod(u, TT)
                n = (i + 1) * P
                off = SEQ - n
                dve.wait_ge(s_ps, u + 1)
                if u >= 2:
                    dve.wait_ge(e_ok, u - 1)
                dve.scalar_tensor_tensor(out=sc[:, u % 2, 0:n], in0=dist[:, off:], scalar=-SLOPES[h],
                                         in1=psum[:, u % 2, 0:n], op0=ALU.mult, op1=ALU.add).then_inc(s_sb, 1)
                dve.wait_ge(s_sb, u + 1)
                dve.tensor_reduce(nmax[:, u:u + 1], sc[:, u % 2, 0:n], AX_X, ALU.max, negate=True).then_inc(mx, 1)

            def weigh(u):
                h, i = divmod(u, TT)
                n = (i + 1) * P
                off = SEQ - n
                dve.wait_ge(e_ok, u + 1)
                p = pb[:, u % 2, 0:n]
                step(dve.tensor_tensor_reduce(p, p, count[:, off:], 1.0, 0.0, ALU.mult, ALU.add, lsum[:, u:u + 1]))
                step(dve.reciprocal(rl[:, u:u + 1], lsum[:, u:u + 1]))
                dve.tensor_scalar(p, p, rl[:, u:u + 1], None, ALU.mult).then_inc(pw, 1)

            for u in range(UNITS + 1):
                if u < UNITS:
                    scores(u)
                    conv_taps(u)
                if u >= 1:
                    weigh(u - 1)
            finish_tile(CM - 1)
            dve.wait_ge(mean_ps, 1)
            for m in range(CM):
                dve.scalar_tensor_tensor(out=mixT[:, 4 + m, :], in0=psum[:, 0, :], scalar=-1.0 / 512, in1=mixT[:, 4 + m, :],
                                         op0=ALU.mult, op1=ALU.add).then_inc(cent, 1)

        @block.scalar
        def _(act):
            def exps(u):
                n = (u % TT + 1) * P
                act.wait_ge(mx, u + 1)
                if u >= 2:
                    act.wait_ge(pt_ps, u - 1)
                act.activation(pb[:, u % 2, 0:n], sc[:, u % 2, 0:n], ACT.Exp, bias=nmax[:, u:u + 1]).then_inc(e_ok, 1)

            def take_probs(u):
                h, i = divmod(u, TT)
                act.wait_ge(pt_ps, u + 1)
                if h >= 2:
                    act.wait_ge(o_ps, h - 1)
                src = psum[:, 2 + u % 2, 0:(i + 1) * P].rearrange("p (j n) -> p j n", j=i + 1)
                act.activation(PT[:, h % 2, 0:i + 1, i * P:(i + 1) * P], src, ACT.Copy).then_inc(pt_sb, 1)

            def take_out(h):
                act.wait_ge(o_ps, h + 1)
                lo = 64 * (h % 2)
                act.activation(mixT[lo:lo + 64, h // 2, :], psum[0:64, 4 + h % 2, :], ACT.Copy).then_inc(o_sb, 1)

            def diagonals(u):
                m, r = u // 8, u % 8
                for j in range(UNIT_TAPS * r, min(UNIT_TAPS * (r + 1), PE_TAPS)):
                    n = m * PE_TAPS + j
                    if n >= 8:
                        om, oj = (n - 8) // PE_TAPS, (n - 8) % PE_TAPS
                        if oj < PE_TAPS - 1:
                            act.wait_ge(dg_used, om * (PE_TAPS - 1) + oj + 1)
                        else:
                            act.wait_ge(c_ps, om + 1)
                    act.activation(diag[:, n % 8, :], ident, ACT.Copy, scale=tap_weight(m, j)).then_inc(dg, 1)

            def tap_products(u):
                m, r = u // 8, u % 8
                for j in range(2 * r, min(2 * r + 2, POOL_TAPS)):
                    tap, k = PE_TAPS + j, m * (POOL_TAPS - 1) + j - 1
                    if j and k >= 3:
                        act.wait_ge(pool_sum, k - 2)
                    act.activation(tap_tmp[:, k % 3, :] if j else mixT[:, 4 + m, :], uT[:, m, tap:tap + SEQ], ACT.Copy,
                                   scale=tap_weight(m, tap)).then_inc(prod_ok, 1)

            diagonals(0)
            diagonals(1)
            for u in range(UNITS + 2):
                if u < UNITS:
                    exps(u)
                if u + 2 < UNITS:
                    diagonals(u + 2)
                if u < UNITS:
                    tap_products(u)
                if u >= 2:
                    take_probs(u - 2)
                    if (u - 2) % TT == 1 and u - 2 > TT:
                        take_out((u - 2) // TT - 1)
            take_out(HEADS - 1)
            for m in range(CM):
                act.wait_ge(cent, m + 1)
                act.activation(PT[:, 0, m, :], mixT[:, 4 + m, :], ACT.Square).then_inc(sq, 1)

        @block.tensor
        def _(pe):
            def scores(u):
                h, i = divmod(u, TT)
                if u >= 2:
                    pe.wait_ge(s_sb, u - 1)
                pe.matmul(psum[:, u % 2, 0:(i + 1) * P], qT[:, h // 2, i * P:(i + 1) * P], kz[:, h, 0:(i + 1) * P],
                          start=True, stop=True).then_inc(s_ps, 1)

            def turn(u):
                h, i = divmod(u, TT)
                pe.wait_ge(pw, u + 1)
                if u >= 2:
                    pe.wait_ge(pt_sb, u - 1)
                for j in range(i + 1):
                    last = pe.transpose(psum[:, 2 + u % 2, j * P:(j + 1) * P], pb[:, u % 2, j * P:(j + 1) * P], ident)
                last.then_inc(pt_ps, 1)

            def values(h):
                pe.wait_ge(pt_sb, TT * (h + 1))
                if h >= 2:
                    pe.wait_ge(o_sb, h - 1)
                for j in range(TT):
                    last = pe.matmul(psum[0:64, 4 + h % 2, j * P:], v[:, j, h * HD:(h + 1) * HD],
                                     PT[:, h % 2, j, j * P:], start=(j == 0), stop=(j == TT - 1))
                last.then_inc(o_ps, 1)

            def conv_taps(u):
                m, r = u // 8, u % 8
                if r == 0 and m:
                    pe.wait_ge(c_sum, m)
                for j in range(UNIT_TAPS * r, min(UNIT_TAPS * (r + 1), PE_TAPS)):
                    n = m * PE_TAPS + j
                    pe.wait_ge(dg, n + 1)
                    last = pe.matmul(psum[:, 7, :], diag[:, n % 8, :], uT[:, m, j:j + SEQ], start=(j == 0),
                                     stop=(j == PE_TAPS - 1))
                    if j < PE_TAPS - 1:
                        last.then_inc(dg_used, 1)
                    else:
                        last.then_inc(c_ps, 1)

            scores(0)
            for u in range(UNITS + 2):
                if u + 1 < UNITS:
                    scores(u + 1)
                if u < UNITS:
                    conv_taps(u)
                if u >= 2:
                    turn(u - 2)
                    if (u - 2) % TT == 0 and u - 2 > 0:
                        values((u - 2) // TT - 1)
            values(HEADS - 1)
            pe.wait_ge(y_done, CM)
            for m in range(CM):
                last = pe.matmul(psum[:, 0, :], ones, mixT[:, 4 + m, :], start=(m == 0), stop=(m == CM - 1))
            last.then_inc(mean_ps, 1)
            for m in range(CM):
                pe.wait_ge(sq, m + 1)
                last = pe.matmul(psum[:, 7, :], ones, PT[:, 0, m, :], start=(m == 0), stop=(m == CM - 1))
            last.then_inc(var_ps, 1)

        @block.sync
        def _(sp):
            table = dram["y"].rearrange("(b p) n -> p b n", p=P)
            per = BLOCKS // ZERO_STORES
            for n in range(ZERO_STORES):
                sp.dma_start(table[:, n * per:(n + 1) * per, :], g["meta"].unsqueeze(1).to_broadcast([P, per, D])).then_inc(
                    g["table_zeroed"], 16)


def output_and_routing(g):
    nc, a, psum, arena, spare, dram = g["nc"], g["a"], g["psum"], g["arena"], g["spare"], g["dram"]
    at, first, mixT, modacc, res = g["at"], g["first"], g["mixT"], g["modacc"], g["res"]
    ident, ones, small = g["ident"], g["ones"], g["small"]
    b = g["base"]
    gt1, sh2, sc2 = (modacc[:, o:o + D] for o in (2048, 3072, 4096))
    g2, squares = modacc[:, 0:D], modacc[:, D:2 * D]
    h2T = arena[:, b + 10240:b + 14336].rearrange("p (k n) -> p k n", k=KT)
    h2 = arena[:, b + 14336:b + 16384].rearrange("p (i n) -> p i n", i=2)
    o = b + 16384
    tmp = arena[:, o:o + 1024].rearrange("p (i n) -> p i n", i=2)
    variance, deviation = spare[:, 0:SEQ], spare[:, SEQ:2 * SEQ]
    wr = arena[:, o + 1024:o + 1312].rearrange("p (k n) -> p k n", k=KT)
    rb = arena[:, o + 1312:o + 1348]
    ss, rstd = small[:, 8:12], small[:, 12:16]
    g["dest"] = dest = small[:, 160:168].bitcast(I32)
    g["weight"] = weight = small[:, 168:176]
    g["slots"] = slots = small[:, 176:176 + TABLE].bitcast(I32)
    g["expert_of"] = expert_of = small[0:1, 224:224 + BLOCKS].bitcast(I32)
    g["pairs"] = pairs = small[0:1, 272:274].bitcast(I32)
    token_id = small[:, 276:280].bitcast(I32)
    g["rows_in"] = rows_in = small[0:1, 440:440 + TABLE].bitcast(I32)
    block_sum = small[:, 500:500 + TABLE]
    first_expert = small[0:1, 550:551].bitcast(I32)
    empty, first_f = small[0:1, 560:592], small[0:1, 592:593]
    used = [b + 6144]

    def room(n):
        used[0] += n
        assert used[0] <= b + 10240
        return arena[:, used[0] - n:used[0]]

    RL = GROUPS + EXPERTS
    logits = room(TT * RL).rearrange("p (t n) -> p t n", t=TT)
    glog = room(TT * 8).rearrange("p (t n) -> p t n", t=TT)
    gmax = room(TT * 8).rearrange("p (t n) -> p t n", t=TT)
    gidx = room(TT * 8).rearrange("p (t n) -> p t n", t=TT)
    gexp = room(TT * 4).rearrange("p (t n) -> p t n", t=TT)
    gsum = room(TT)
    ngm = room(TT)
    hot_g = room(TT * 4).rearrange("p (t n) -> p t n", t=TT)
    pen = room(TT * 4).rearrange("p (t n) -> p t n", t=TT)
    elog = room(TT * 32).rearrange("p (t n) -> p t n", t=TT)
    emax = room(TT * 8).rearrange("p (t n) -> p t n", t=TT)
    eidx = room(TT * 8).rearrange("p (t n) -> p t n", t=TT)
    chosen = room(TT * 2).rearrange("p (t n) -> p t n", t=TT)
    diff, ediff, den = room(TT), room(TT), room(TT)
    hot = [room(TT * 32).rearrange("p (t n) -> p t n", t=TT) for _ in range(2)]
    both = room(TT * 32).rearrange("p (t n) -> p t n", t=TT)
    earlier = room(TT * 32).rearrange("p (t n) -> p t n", t=TT)
    all_tiles = room(32)
    where = room(TT * 32).rearrange("p (t n) -> p t n", t=TT)
    picked = room(TT * 32).rearrange("p (t n) -> p t n", t=TT)
    destf = room(TT * 2).rearrange("p (t n) -> p t n", t=TT)
    counts, nblk, end, start = room(32), room(32), room(32), room(32)
    iota = room(P)
    block_of = room(TT * 2)
    place_of, token_f = room(TT * 2), room(TT)
    assigned = h2T.rearrange("p k n -> p (k n)")
    place_hot = assigned[:, 0:2 * TT * P].rearrange("p (a n) -> p a n", n=P)
    block_hot = assigned[:, 2 * TT * P:2 * TT * (P + TABLE)].rearrange("p (a n) -> p a n", n=TABLE)
    ended = room(BLOCKS * 32)[0:1, :].rearrange("p (b n) -> p b n", b=BLOCKS)
    expf, pairf, pairw = room(BLOCKS)[0:1, :], room(1)[0:1, :], room(BLOCKS)[0:1, :]

    with ExitStack() as cx:
        sem, dma_sem = g["semaphores"](cx)
        ready, taken = sem("mix_in_psum"), sem("mix_taken")
        loads, g2_ok = dma_sem("router_loaded"), sem("norm2_row_ready")
        ids_ok = sem("ids_built")
        x1, ssq, var, root = sem("x1_ready"), sem("x1_squares"), sem("x1_variance"), sem("x1_root")
        h2s, stored = sem("h2_ready"), [dma_sem("h2_stored0"), dma_sem("h2_stored1")]
        dstep = sem("routing_dve_step")
        t_ps, t_sb = sem("h2T_in_psum"), sem("h2T_ready")
        r_ps, both_ok, rank_ps = sem("logits_in_psum"), sem("choices_ready"), sem("ranks_in_psum")
        neg_ok, gexp_ok, diff_ok, ediff_ok = sem("max_negated"), sem("group_exp"), sem("gap_ready"), sem("gap_exp")
        first_ok = sem("first_expert_known")
        vr, rt, z_ok, conv_out = sem("variance_ready"), sem("root_ready"), sem("conv_normed"), sem("swish_written")
        hot_ok, tab_ps = sem("slots_one_hot"), sem("slots_in_psum")
        block = cx.enter_context(nc.Block())

        @block.sync
        def _(sp):
            sp.dma_start(g2, a["g_norm2"].to_broadcast([P, D])).then_inc(loads, 16)
            sp.dma_start(wr[:, :, 0:GROUPS], a["w_router_group"][0].rearrange("(k p) n -> p k n", p=P)).then_inc(loads, 16)
            sp.dma_start(wr[:, :, GROUPS:], a["w_router_expert"][0].rearrange("(k p) n -> p k n", p=P)).then_inc(loads, 16)
            sp.dma_start(rb[:, 0:GROUPS], a["b_router_group"].to_broadcast([P, GROUPS])).then_inc(loads, 16)
            sp.dma_start(rb[:, GROUPS:], a["b_router_expert"].to_broadcast([P, EXPERTS])).then_inc(loads, 16)
            for t in range(TT):
                sp.wait_ge(h2s, t + 1)
                sp.dma_start(dram["h2"][t * P:(t + 1) * P, :], h2[:, t % 2, :]).then_inc(stored[t % 2], 16)
            sp.wait_ge(ready, 2 * TT)
            sp.wait_ge(first_ok, 1)
            e = sp.value_load(first_expert, min_val=0, max_val=EXPERTS - 1)
            for slot in EXPERT_SLOTS[:2]:
                load_expert(g, sp, slot, e)
            for i in range(2):
                sp.wait_ge(stored[i], 32)
            sp.wait_ge(g["table_zeroed"], 16 * ZERO_STORES)

        @block.gpsimd
        def _(pool):
            pool.iota(token_id, [[P, TT]], base=0, channel_multiplier=1).then_inc(ids_ok, 1)
            pool.wait_ge(ids_ok, 1)
            pool.memset(g["ring"][:, 3, 0:2 * D], 0.0).then_inc(ids_ok, 1)

        @block.tensor
        def _(pe):
            w = [first.use(pe, at["wout"][n]).rearrange("p (k n) -> p k n", k=KT) for n in range(2)]

            def turn(t):
                pe.wait_ge(h2s, t + 1)
                for half in range(2):
                    if t:
                        pe.wait_ge(t_sb, 2 * t + half - 1)
                    for k in range(4):
                        last = pe.transpose(psum[:, 4 + half, k * P:(k + 1) * P],
                                            h2[:, t % 2, (4 * half + k) * P:(4 * half + k + 1) * P], ident)
                    last.then_inc(t_ps, 1)

            def route(t):
                if t == 0:
                    pe.wait_ge(loads, 16 * 5)
                pe.wait_ge(t_sb, 2 * t + 2)
                for k in range(KT):
                    last = pe.matmul(psum[:, 6, t * RL:(t + 1) * RL], h2T[:, k, t * P:(t + 1) * P], wr[:, k, :],
                                     start=(k == 0), stop=(k == KT - 1))
                last.then_inc(r_ps, 1)

            def mix(i, ks):
                t, n = divmod(i, 2)
                for k in ks:
                    last = pe.matmul(psum[:, i % 4, :], mixT[:, k, t * P:(t + 1) * P], w[n][:, k, :],
                                     start=(k == 0), stop=(k == KT - 1))
                return last

            for i in range(4):
                mix(i, range(4))
            pe.wait_ge(conv_out, CM)
            for t in range(TT):
                for n in range(2):
                    i = 2 * t + n
                    if i >= 4:
                        pe.wait_ge(taken, i - 3)
                    mix(i, range(4 if i < 4 else 0, KT)).then_inc(ready, 1)
                if t:
                    turn(t - 1)
                if t > 1:
                    route(t - 2)
            first.read_by(at["wout"][1], ready, 8)
            route(TT - 2)
            turn(TT - 1)
            route(TT - 1)
            pe.wait_ge(both_ok, 1)
            rows = lambda x: x.rearrange("p t n -> p (t n)")
            pe.matmul(psum[:, 7, 0:P], g["before"], rows(both), start=True, stop=False)
            pe.matmul(psum[:, 7, 0:P], ones, rows(earlier), start=False, stop=True)
            pe.matmul(psum[:, 7, P:P + EXPERTS], ones, all_tiles, start=True, stop=True).then_inc(rank_ps, 1)
            pe.wait_ge(hot_ok, 1)
            for i in range(2 * TT):
                last = pe.matmul(psum[:, 3, 0:TABLE], place_hot[:, i, :], block_hot[:, i, :], start=(i == 0), stop=(i == 2 * TT - 1))
            pe.matmul(psum[:, 3, P:P + TABLE], ones, block_sum, start=True, stop=True).then_inc(tab_ps, 1)

        @block.scalar
        def _(act):
            act.wait_ge(vr, 1)
            act.activation(deviation, variance, ACT.Sqrt).then_inc(rt, 1)
            for m in range(CM):
                act.wait_ge(z_ok, m + 1)
                act.activation(mixT[:, 4 + m, :], mixT[:, 4 + m, :], ACT.Silu, bias=col(g, "conv_ln_b")[:, m:m + 1],
                               scale=col(g, "conv_ln_g")[:, m:m + 1]).then_inc(conv_out, 1)
            for t in range(TT):
                act.wait_ge(x1, 2 * t + 2)
                if t:
                    act.wait_ge(ssq, t)
                act.activation(squares, res[:, t, :], ACT.Square, accum_out=ss[:, t:t + 1]).then_inc(ssq, 1)
                act.wait_ge(var, t + 1)
                act.activation(rstd[:, t:t + 1], ss[:, t:t + 1], ACT.Sqrt).then_inc(root, 1)
                for half in range(2):
                    act.wait_ge(t_ps, 2 * t + half + 1)
                    act.activation(h2T[:, 4 * half:4 * half + 4, t * P:(t + 1) * P],
                                   psum[:, 4 + half, :].rearrange("p (k n) -> p k n", k=4), ACT.Copy).then_inc(t_sb, 1)
            act.wait_ge(neg_ok, 1)
            for t in range(TT):
                act.activation(gexp[:, t, :], logits[:, t, 0:GROUPS], ACT.Exp, bias=ngm[:, t:t + 1],
                               accum_out=gsum[:, t:t + 1]).then_inc(gexp_ok, 1)
            act.wait_ge(diff_ok, 1)
            act.activation(ediff, diff, ACT.Exp).then_inc(ediff_ok, 1)

        @block.vector
        def _(dve):
            step = Steps(dve, dstep)
            dve.tensor_scalar(variance, psum[:, 7, :], 1.0 / 512, EPS, ALU.mult, ALU.add).then_inc(vr, 1)
            dve.wait_ge(rt, 1)
            step(dve.reciprocal(deviation, deviation))
            for m in range(CM):
                dve.tensor_tensor(mixT[:, 4 + m, :], mixT[:, 4 + m, :], deviation, ALU.mult).then_inc(z_ok, 1)
            step(dve.tensor_copy(g["gt2"], modacc[:, 5120:6144]))
            dve.wait_ge(loads, 16 * 5)
            step(dve.scalar_tensor_tensor(out=sc2, in0=sc2, scalar=1.0, in1=g2, op0=ALU.add, op1=ALU.mult))
            for t in range(TT):
                for n in range(2):
                    i = 2 * t + n
                    dve.wait_ge(ready, i + 1)
                    cols = slice(512 * n, 512 * n + 512)
                    dve.tensor_tensor(tmp[:, i % 2, :], psum[:, i % 4, :], gt1[:, cols], ALU.mult).then_inc(taken, 1)
                    dve.wait_ge(taken, i + 1)
                    dve.tensor_tensor(res[:, t, cols], res[:, t, cols], tmp[:, i % 2, :], ALU.add).then_inc(x1, 1)
                dve.wait_ge(ssq, t + 1)
                dve.tensor_scalar(ss[:, t:t + 1], ss[:, t:t + 1], 1.0 / D, EPS, ALU.mult, ALU.add).then_inc(var, 1)
                dve.wait_ge(root, t + 1)
                step(dve.reciprocal(rstd[:, t:t + 1], rstd[:, t:t + 1]))
                if t >= 2:
                    dve.wait_ge(stored[t % 2], 16)
                    dve.wait_ge(t_ps, 2 * (t - 1))
                step(dve.scalar_tensor_tensor(out=h2[:, t % 2, :], in0=res[:, t, :], scalar=rstd[:, t:t + 1], in1=sc2,
                                              op0=ALU.mult, op1=ALU.mult))
                dve.tensor_tensor(h2[:, t % 2, :], h2[:, t % 2, :], sh2, ALU.add).then_inc(h2s, 1)
            dve.wait_ge(ready, 8)
            step(dve.memset(glog, NEG))
            step(dve.memset(earlier[:, 0, :], 0.0))
            step(dve.memset(iota[:, 0:1], 0.0))
            for n in (1, 2, 4, 8, 16, 32, 64):
                step(dve.tensor_scalar(iota[:, n:2 * n], iota[:, 0:n], float(n), None, ALU.add))
            dve.wait_ge(ids_ok, 1)
            step(dve.tensor_copy(token_f, token_id))
            dve.wait_ge(r_ps, TT)
            step(dve.tensor_tensor(logits, psum[:, 6, 0:TT * RL].rearrange("p (t n) -> p t n", t=TT),
                                   rb.unsqueeze(1).to_broadcast([P, TT, RL]), ALU.add))
            step(dve.tensor_copy(glog[:, :, 0:GROUPS], logits[:, :, 0:GROUPS]))
            for t in range(TT):
                step(dve.max(gmax[:, t, :], glog[:, t, :]))
                step(dve.max_index(gidx[:, t, :].bitcast(U32), gmax[:, t, :], glog[:, t, :]))
            dve.tensor_scalar(ngm, gmax[:, :, 0], -1.0, None, ALU.mult).then_inc(neg_ok, 1)
            step(dve.tensor_copy(chosen[:, :, 0], gidx[:, :, 0].bitcast(U32)))
            step(dve.tensor_tensor(hot_g, iota[:, 0:GROUPS].unsqueeze(1).to_broadcast([P, TT, GROUPS]),
                                   chosen[:, :, 0:1].to_broadcast([P, TT, GROUPS]), ALU.is_equal))
            step(dve.tensor_scalar(pen, hot_g, 1.0, -NEG, ALU.subtract, ALU.mult))
            e4 = elog.rearrange("p t (q n) -> p (t q) n", q=GROUPS)
            spread = lambda x: x.rearrange("p t (q n) -> p (t q) n", n=1).to_broadcast([P, TT * GROUPS, PER_GROUP])
            step(dve.tensor_copy(elog, logits[:, :, GROUPS:]))
            step(dve.tensor_tensor(e4, e4, spread(hot_g), ALU.mult))
            step(dve.tensor_tensor(e4, e4, spread(pen), ALU.add))
            for t in range(TT):
                step(dve.max(emax[:, t, :], elog[:, t, :]))
                step(dve.max_index(eidx[:, t, :].bitcast(U32), emax[:, t, :], elog[:, t, :]))
            dve.tensor_tensor(diff, emax[:, :, 1], emax[:, :, 0], ALU.subtract).then_inc(diff_ok, 1)
            step(dve.tensor_copy(chosen, eidx[:, :, 0:2].bitcast(U32)))
            for k in range(2):
                step(dve.tensor_tensor(hot[k], iota[:, 0:32].unsqueeze(1).to_broadcast([P, TT, 32]),
                                       chosen[:, :, k:k + 1].to_broadcast([P, TT, 32]), ALU.is_equal))
            step(dve.tensor_tensor(both, hot[0], hot[1], ALU.add))
            for t in range(1, TT + 1):
                out = earlier[:, t, :] if t < TT else all_tiles
                step(dve.tensor_tensor(out, earlier[:, t - 1, :], both[:, t - 1, :], ALU.add))
            dve.engine_nop().then_inc(both_ok, 1)
            dve.wait_ge(gexp_ok, TT)
            dve.wait_ge(ediff_ok, 1)
            step(dve.tensor_scalar(den, ediff, 1.0, None, ALU.add))
            step(dve.tensor_tensor(den, den, gsum, ALU.mult))
            wt = weight.rearrange("p (t k) -> p t k", k=2)
            step(dve.reciprocal(wt[:, :, 0], den))
            step(dve.tensor_tensor(wt[:, :, 1], wt[:, :, 0], ediff, ALU.mult))
            dve.wait_ge(rank_ps, 1)
            step(dve.tensor_copy(counts, psum[:, 7, 128:160]))
            step(dve.tensor_scalar(nblk, counts, 0.0, None, ALU.is_gt))
            for j in range(1, SEQ // P):
                step(dve.scalar_tensor_tensor(out=nblk, in0=counts, scalar=float(P * j), in1=nblk, op0=ALU.is_gt, op1=ALU.add))
            step(dve.tensor_tensor_scan(end, ones[:, 0:32], nblk, 0.0, ALU.mult, ALU.add))
            step(dve.tensor_scalar(empty, end[0:1, :], 0.0, None, ALU.is_le))
            step(dve.tensor_reduce(first_f, empty, AX_X, ALU.add))
            dve.tensor_copy(first_expert, first_f).then_inc(first_ok, 1)
            step(dve.tensor_tensor(start, end, nblk, ALU.subtract))
            step(dve.tensor_scalar(start, start, float(P), None, ALU.mult))
            step(dve.tensor_tensor(where, psum[:, 7, 0:128].rearrange("p (t n) -> p t n", t=TT),
                                   start.unsqueeze(1).to_broadcast([P, TT, 32]), ALU.add))
            for k in range(2):
                step(dve.tensor_tensor(picked, where, hot[k], ALU.mult))
                step(dve.tensor_reduce(destf[:, :, k], picked, AX_X, ALU.add))
            step(dve.tensor_copy(dest.rearrange("p (t k) -> p t k", k=2), destf))
            step(dve.tensor_scalar(place_of.bitcast(I32), dest, 7, None, ALU.logical_shift_right))
            step(dve.tensor_copy(block_of, place_of.bitcast(I32)))
            step(dve.scalar_tensor_tensor(out=place_of, in0=block_of, scalar=-float(P), in1=destf.rearrange("p t k -> p (t k)"),
                                          op0=ALU.mult, op1=ALU.add))
            along = lambda x, n: x.rearrange("p (a n) -> p a n", n=1).to_broadcast([P, 2 * TT, n])
            step(dve.tensor_tensor(block_hot, iota[:, 0:TABLE].unsqueeze(1).to_broadcast([P, 2 * TT, TABLE]),
                                   along(block_of, TABLE), ALU.is_equal))
            step(dve.tensor_reduce(block_sum, block_hot.rearrange("p a n -> p n a"), AX_X, ALU.add))
            for k in range(2):
                step(dve.tensor_tensor(block_hot[:, k::2, :], block_hot[:, k::2, :],
                                       token_f.rearrange("p (a n) -> p a n", n=1).to_broadcast([P, TT, TABLE]), ALU.mult))
            dve.tensor_tensor(place_hot, iota.unsqueeze(1).to_broadcast([P, 2 * TT, P]), along(place_of, P),
                              ALU.is_equal).then_inc(hot_ok, 1)
            step(dve.tensor_tensor(ended, end[0:1, :].unsqueeze(1).to_broadcast([1, BLOCKS, 32]),
                                   iota[0:1, 0:BLOCKS].rearrange("p (b n) -> p b n", n=1).to_broadcast([1, BLOCKS, 32]), ALU.is_le))
            step(dve.tensor_reduce(expf, ended, AX_X, ALU.add))
            step(dve.tensor_scalar(expf, expf, float(EXPERTS - 1), None, ALU.min))
            step(dve.tensor_copy(expert_of, expf))
            step(dve.tensor_scalar(pairw[:, 0:BLOCKS // 2], iota[0:1, 0:BLOCKS // 2], 2.0, None, ALU.mult))
            step(dve.tensor_scalar(pairw[:, 0:BLOCKS // 2], pairw[:, 0:BLOCKS // 2], end[0:1, 31:32], None, ALU.is_lt))
            step(dve.tensor_reduce(pairf, pairw[:, 0:BLOCKS // 2], AX_X, ALU.add))
            step(dve.tensor_scalar(pairs[:, 0:1], pairf, 2.0, None, ALU.subtract))
            dve.wait_ge(tab_ps, 1)
            step(dve.tensor_copy(slots, psum[:, 3, 0:TABLE]))
            step(dve.tensor_copy(rows_in, psum[0:1, 3, P:P + TABLE]))
    first.new_phase()


EXPERT_SLOTS = 0, 1, 2


def load_expert(g, sp, slot, e):
    w = g["a"][("w_exp_gate", "w_exp_up", "w_exp_down")[slot]].rearrange("l e (k p) n -> p (l e) k n", p=P)
    dst = g["ring"][:, slot, :].rearrange("p (e k n) -> p e k n", e=1, k=w.shape[2])
    sp.dma_start(dst, w[:, bass.ds(e, 1)]).then_inc(g["expert_arrived"][slot], 16)


def experts(g):
    nc, a, psum, dram = g["nc"], g["a"], g["psum"], g["dram"]
    ident, ring = g["ident"], g["ring"]
    index = g["small"][:, 280:282].bitcast(I32)
    slots, expert_of, pairs, rows_in = g["slots"], g["expert_of"], g["pairs"], g["rows_in"]
    GATE, UP, DOWN = EXPERT_SLOTS
    PIECE, PIECES = 1024, 8
    xg = ring[:, 3, 0:2 * D].rearrange("p (j n) -> p j n", j=2)
    yb = ring[:, 3, 2 * D:4 * D].rearrange("p (j n) -> p j n", j=2)
    BG, BU, BY, BX, BH = 0, 1, 2, 4, 6
    PAIRS = BLOCKS // 2

    first_block = lambda b: isinstance(b, int) and b == 0
    gate_at = lambda b: 0 if first_block(b) else b * 12 - 4
    up_at = lambda b: 4 if first_block(b) else b * 12
    down_at = lambda b: b * 12 + 4
    last_down_at = lambda b: b * 12 - 4
    gate_done, up_done = (lambda b: gate_at(b) + 4), (lambda b: up_at(b) + 4)
    down_done = lambda b: down_at(b + 1) + 4

    def held(at, j, q):
        return (at(2 + j) + q) % PIECES

    def wait(eng, sem, value):
        if not isinstance(value, int) or value > 0:
            eng.wait_ge(sem, value)

    def run(eng, body):
        n = eng.value_load(pairs[:, 0:1], min_val=0, max_val=PAIRS - 2) + 2
        body(0, 0), body(0, 1), body(1, 0), body(1, 1)
        with eng.Fori(2, PAIRS) as i:
            with eng.If(i < n):
                body(i, 0)
                body(i, 1)
            eng.nop()
        return n

    with ExitStack() as cx:
        hb = cx.enter_context(nc.sbuf_tensor("hidden_rows", [P, 2, 512], F32))
        weights = cx.enter_context(nc.sbuf_tensor("weight_parts", [P, 2, PIECES, PIECE], F32R))
        xT = cx.enter_context(nc.sbuf_tensor("token_parts", [P, 2, 2, D], F32R))
        hT = cx.enter_context(nc.sbuf_tensor("hidden_parts", [P, 2, 2, 512], F32R))
        sem, dma_sem = g["semaphores"](cx)
        w_in = g["expert_arrived"]
        idx_ok, idx_seen = sem("indices_copied"), sem("indices_seen")
        x_in = [dma_sem(f"tokens_gathered{j}") for j in range(2)]
        high_ok, low_ok, w_read = sem("weight_high_parts"), sem("weight_low_parts"), sem("weight_pieces_read")
        xt_ps, xt_high, xt_low = sem("xT_in_psum"), sem("xT_high_ready"), sem("xT_low_ready")
        ht_ps, ht_high, ht_low = sem("hT_in_psum"), sem("hT_high_ready"), sem("hT_low_ready")
        silu_ok, h_ok, y_sb = sem("silu_ready"), sem("hidden_ready"), sem("y_ready")
        y_st = [dma_sem(f"y_stored{j}") for j in range(2)]
        block = cx.enter_context(nc.Block())

        @block.sync
        def _(sp):
            def body(i, j):
                b = i * 2 + j
                if first_block(b):
                    return
                e = sp.value_load(expert_of[0:1, bass.ds(b, 1)], min_val=0, max_val=EXPERTS - 1)
                sp.wait_ge(low_ok, gate_done(b - 1))
                load_expert(g, sp, GATE, e)
                sp.wait_ge(low_ok, up_done(b - 1))
                load_expert(g, sp, UP, e)
                eb = sp.value_load(expert_of[0:1, bass.ds(b - 1, 1)], min_val=0, max_val=EXPERTS - 1)
                if not (isinstance(b, int) and b == 1):
                    sp.wait_ge(low_ok, down_done(b - 2))
                load_expert(g, sp, DOWN, eb)

            n = run(sp, body)
            eb = sp.value_load(expert_of[0:1, bass.ds(n * 2 - 1, 1)], min_val=0, max_val=EXPERTS - 1)
            sp.wait_ge(low_ok, down_done(n * 2 - 2))
            load_expert(g, sp, DOWN, eb)

        @block.gpsimd
        def _(pool):
            def gather(b, j, count):
                pool.tensor_copy(index[:, j:j + 1], slots[:, bass.ds(b, 1)]).then_inc(idx_ok, 1)
                pool.wait_ge(idx_ok, b + 1)
                pool.sem_inc(idx_seen, 1)

                def rows(n):
                    pool.indirect_dma_start(
                        out=xg[0:n, j, :], out_offset=None, in_=dram["h2"],
                        in_offset=bass.IndirectOffsetOnAxis(ap=index[0:n, j:j + 1].bitcast(U32), axis=0)).then_inc(x_in[j], 16)

                by_size(b, rows)

            def store(b, j):
                def rows(n):
                    pool.dma_start(dram["y"].rearrange("(b p) n -> p b n", p=P)[0:n, bass.ds(b, 1), :],
                                   yb[0:n, j:j + 1, :]).then_inc(y_st[j], 16)

                by_size(b, rows)

            def by_size(b, move):
                used = pool.value_load(rows_in[0:1, bass.ds(b, 1)], min_val=0, max_val=P)
                with pool.If(used > HALF_BLOCK):
                    move(P)
                with pool.Else():
                    move(HALF_BLOCK)
                pool.nop()

            def body(i, j):
                b = i * 2 + j
                pool.wait_ge(xt_ps, b * 2 + 2)
                pool.wait_ge(x_in[j], i * 16 + 16)
                gather(b + 2, j, i + 1)
                if isinstance(i, int) and i == 0:
                    return
                pool.wait_ge(y_sb, b * 2 - 2)
                store(b - 2, j)

            gather(0, 0, 0)
            gather(1, 1, 0)
            n = run(pool, body)
            for j in range(2):
                pool.wait_ge(y_sb, n * 4 - 2 + 2 * j)
                store(n * 2 - 2 + j, j)
            for j in range(2):
                pool.wait_ge(y_st[j], n * 16)
                pool.wait_ge(x_in[j], n * 16 + 16)

        @block.tensor
        def _(pe):
            def three(out, x, w, start, stop):
                pe.matmul(out, x(0), w(0), start=start, stop=False)
                pe.matmul(out, x(0), w(1), start=False, stop=False)
                return pe.matmul(out, x(1), w(0), start=False, stop=stop)

            def turn_x(b, j, count):
                pe.wait_ge(x_in[j], count)
                for half in range(2):
                    wait(pe, xt_low, b * 2 + half - 1)
                    for k in range(4):
                        last = pe.transpose(psum[:, BX + half, k * P:(k + 1) * P],
                                            xg[:, j, (4 * half + k) * P:(4 * half + k + 1) * P], ident)
                    last.then_inc(xt_ps, 1)

            def turn_h(b, j):
                pe.wait_ge(h_ok, b + 1)
                wait(pe, ht_low, b)
                for k in range(4):
                    last = pe.transpose(psum[:, BH, k * P:(k + 1) * P], hb[:, j, k * P:(k + 1) * P], ident)
                last.then_inc(ht_ps, 1)

            def down(b, j, at, next_block):
                pe.wait_ge(ht_low, b + 1)
                wait(pe, y_sb, b * 2)
                for q in range(4):
                    piece = held(at, 1 - j, q)
                    pe.wait_ge(low_ok, at(next_block) + q + 1)
                    for n in range(2):
                        last = three(psum[:, BY + n, :], lambda part: hT[:, part, j, q * P:(q + 1) * P],
                                     lambda part: weights[:, part, piece, n * 512:(n + 1) * 512], q == 0, q == 3)
                    last.then_inc(w_read, 1)

            def project(b, j, at, bank):
                for q in range(4):
                    piece = (at(b) + q) % PIECES if isinstance(b, int) else held(at, j, q)
                    pe.wait_ge(low_ok, at(b) + q + 1)
                    for k in range(2):
                        kk = 2 * q + k
                        last = three(psum[:, bank, :], lambda part: xT[:, part, j, kk * P:(kk + 1) * P],
                                     lambda part: weights[:, part, piece, k * 512:(k + 1) * 512], kk == 0, kk == KT - 1)
                    last.then_inc(w_read, 1)

            def body(i, j):
                b = i * 2 + j
                turn_x(b + 1, 1 - j, i * 16 + 16 + 16 * j)
                pe.wait_ge(xt_low, b * 2 + 2)
                wait(pe, silu_ok, b)
                project(b, j, gate_at, BG)
                if not first_block(b):
                    turn_h(b - 1, 1 - j)
                wait(pe, h_ok, b)
                project(b, j, up_at, BU)
                if not first_block(b):
                    down(b - 1, 1 - j, down_at, b)

            turn_x(0, 0, 16)
            n = run(pe, body)
            turn_h(n * 2 - 1, 1)
            down(n * 2 - 1, 1, last_down_at, n * 2)

        @block.scalar
        def _(act):
            def high(b, j, at, s, count):
                act.wait_ge(w_in[s], count)
                for q in range(4):
                    piece = (at(b) + q) % PIECES if isinstance(b, int) else held(at, j, q)
                    wait(act, w_read, at(b) + q - PIECES + 1)
                    act.activation(weights[:, 0, piece, :], ring[:, s, q * PIECE:(q + 1) * PIECE], ACT.Copy).then_inc(high_ok, 1)

            def take_x(b, j):
                if not (isinstance(b, int) and b < 2):
                    act.wait_ge(w_read, up_done(b - 2))
                for half in range(2):
                    act.wait_ge(xt_ps, b * 2 + half + 1)
                    act.activation(xT[:, 0, j, 512 * half:512 * half + 512], psum[:, BX + half, :], ACT.Copy).then_inc(xt_high, 1)

            def take_h(b, j):
                act.wait_ge(ht_ps, b + 1)
                if not (isinstance(b, int) and b < 2):
                    act.wait_ge(w_read, down_done(b - 2))
                act.activation(hT[:, 0, j, :], psum[:, BH, :], ACT.Copy).then_inc(ht_high, 1)

            def take_y(b, j, stored, done):
                wait(act, y_st[j], stored)
                act.wait_ge(w_read, done)
                for n in range(2):
                    act.activation(yb[:, j, 512 * n:512 * n + 512], psum[:, BY + n, :], ACT.Copy).then_inc(y_sb, 1)

            def body(i, j):
                b = i * 2 + j
                high(b, j, gate_at, GATE, i * 32 + 16 * j + 16)
                take_x(b + 1, 1 - j)
                if not (isinstance(i, int) and i == 0):
                    take_y(b - 2, j, i * 16 - 16, down_done(b - 2))
                high(b, j, up_at, UP, i * 32 + 16 * j + 16)
                if not first_block(b):
                    take_h(b - 1, 1 - j)
                act.wait_ge(w_read, gate_done(b))
                wait(act, ht_ps, b - 1)
                act.activation(hb[:, j, :], psum[:, BG, :], ACT.Silu).then_inc(silu_ok, 1)
                if not first_block(b):
                    high(b, j, down_at, DOWN, i * 32 + 16 * j)

            take_x(0, 0)
            n = run(act, body)
            take_y(n * 2 - 2, 0, n * 16 - 16, down_done(n * 2 - 2))
            take_h(n * 2 - 1, 1)
            high(n * 2, 0, last_down_at, DOWN, n * 32)
            take_y(n * 2 - 1, 1, n * 16 - 16, last_down_at(n * 2) + 4)

        @block.vector
        def _(dve):
            def low_part(out, src, high_part, done):
                dve.tensor_tensor(out, src, high_part.bitcast(F32), ALU.subtract).then_inc(done, 1)

            def low(b, j, at, s):
                for q in range(4):
                    piece = (at(b) + q) % PIECES if isinstance(b, int) else held(at, j, q)
                    dve.wait_ge(high_ok, at(b) + q + 1)
                    low_part(weights[:, 1, piece, :], ring[:, s, q * PIECE:(q + 1) * PIECE], weights[:, 0, piece, :], low_ok)

            def take_x(b, j):
                for half in range(2):
                    c = slice(512 * half, 512 * half + 512)
                    dve.wait_ge(xt_high, b * 2 + half + 1)
                    low_part(xT[:, 1, j, c], psum[:, BX + half, :], xT[:, 0, j, c], xt_low)

            def take_h(b, j):
                dve.wait_ge(ht_high, b + 1)
                low_part(hT[:, 1, j, :], psum[:, BH, :], hT[:, 0, j, :], ht_low)

            def hidden(b, j):
                dve.wait_ge(silu_ok, b + 1)
                dve.wait_ge(w_read, up_done(b))
                dve.tensor_tensor(hb[:, j, :], hb[:, j, :], psum[:, BU, :], ALU.mult).then_inc(h_ok, 1)

            def body(i, j):
                b = i * 2 + j
                low(b, j, gate_at, GATE)
                if not first_block(b):
                    hidden(b - 1, 1 - j)
                take_x(b + 1, 1 - j)
                low(b, j, up_at, UP)
                if not first_block(b):
                    take_h(b - 1, 1 - j)
                    low(b, j, down_at, DOWN)

            take_x(0, 0)
            n = run(dve, body)
            hidden(n * 2 - 1, 1)
            take_h(n * 2 - 1, 1)
            low(n * 2, 0, last_down_at, DOWN)


def combine(g):
    nc, a, psum, arena, dram = g["nc"], g["a"], g["psum"], g["arena"], g["dram"]
    res, meta, ident, small = g["res"], g["meta"], g["ident"], g["small"]
    b = g["base"]
    gt2 = g["gt2"]
    g["hnT"] = hnT = arena[:, b:b + KT * L2].rearrange("p (k n) -> p k n", k=KT)
    o = b + 6144
    y = g["spare"].rearrange("p (i n) -> p i n", i=2 * TT)
    hn = arena[:, o + 4096:o + 6144].rearrange("p (i n) -> p i n", i=2)
    gfin = arena[:, o + 6144:o + 7168]
    squares = arena[:, o + 7168:o + 8192]
    ss, rstd, ss2, rstd2 = small[:, 8:12], small[:, 12:16], small[:, 16:21], small[:, 24:29]
    dest, weight = g["dest"], g["weight"]
    with ExitStack() as cx:
        sem, dma_sem = g["semaphores"](cx)
        y_in, loads = [dma_sem(f"rows_gathered{t}") for t in range(TT)], dma_sem("final_gain_loaded")
        weighted, mixed, dstep = sem("rows_weighted"), sem("rows_mixed"), sem("combine_dve_step")
        ssq, var, root = sem("x2_squares"), sem("x2_variance"), sem("x2_root")
        x3, ssq2, var2, root2 = sem("h_ready"), sem("h_squares"), sem("h_variance"), sem("h_root")
        hn_ok, hn_ps, hn_sb = sem("hn_ready"), sem("hnT_in_psum"), sem("hnT_ready")
        block = cx.enter_context(nc.Block())

        @block.sync
        def _(sp):
            sp.dma_start(gfin, a["g_final"].rearrange("(a n) -> a n", a=1).to_broadcast([P, D])).then_inc(loads, 16)
            sp.dma_start(meta[0:META, :], a["meta_tokens_2"]).then_inc(loads, 16)
            sp.wait_ge(y_in[TT - 1], 32)
            g["later"].load_until(sp, SLOTS)

        @block.gpsimd
        def _(pool):
            for t in range(TT):
                for k in range(2):
                    pool.indirect_dma_start(
                        out=y[:, 2 * t + k, :], out_offset=None, in_=dram["y"],
                        in_offset=bass.IndirectOffsetOnAxis(ap=dest[:, 2 * t + k:2 * t + k + 1].bitcast(U32), axis=0)
                    ).then_inc(y_in[t], 16)

        @block.vector
        def _(dve):
            step = Steps(dve, dstep)

            def mix(t):
                y0, y1 = y[:, 2 * t, :], y[:, 2 * t + 1, :]
                dve.wait_ge(weighted, t + 1)
                step(dve.scalar_tensor_tensor(out=y0, in0=y1, scalar=weight[:, 2 * t + 1:2 * t + 2], in1=y0,
                                              op0=ALU.mult, op1=ALU.add))
                step(dve.tensor_tensor(y0, y0, gt2, ALU.mult))
                dve.tensor_tensor(res[:, t, :], res[:, t, :], y0, ALU.add).then_inc(mixed, 1)

            def last_norm(t):
                dve.wait_ge(ssq, t + 1)
                dve.tensor_scalar(ss[:, t:t + 1], ss[:, t:t + 1], 1.0 / D, EPS, ALU.mult, ALU.add).then_inc(var, 1)
                dve.wait_ge(root, t + 1)
                step(dve.reciprocal(rstd[:, t:t + 1], rstd[:, t:t + 1]))
                dve.scalar_tensor_tensor(out=res[:, t, :], in0=res[:, t, :], scalar=rstd[:, t:t + 1], in1=gfin,
                                         op0=ALU.mult, op1=ALU.mult).then_inc(x3, 1)

            def pre_norm(t):
                i, n = t + 1, P if t >= 0 else META
                src = res[:, t, :] if t >= 0 else meta
                dve.wait_ge(ssq2, i + 1)
                dve.tensor_scalar(ss2[0:n, i:i + 1], ss2[0:n, i:i + 1], 1.0 / D, EPS, ALU.mult, ALU.add).then_inc(var2, 1)
                dve.wait_ge(root2, i + 1)
                step(dve.reciprocal(rstd2[0:n, i:i + 1], rstd2[0:n, i:i + 1]))
                if i >= 2:
                    dve.wait_ge(hn_ps, 2 * (i - 1))
                dve.tensor_scalar(hn[0:n, i % 2, :], src[0:n, :], rstd2[0:n, i:i + 1], None, ALU.mult).then_inc(hn_ok, 1)

            dve.wait_ge(loads, 32)
            pre_norm(-1)
            for t in range(TT + 2):
                if t < TT:
                    mix(t)
                if 1 <= t <= TT:
                    last_norm(t - 1)
                if t >= 2:
                    pre_norm(t - 2)

        @block.scalar
        def _(act):
            def squares_of(src, out, n, done, count):
                if squared[0]:
                    act.wait_ge(*squared[0])
                act.activation(squares[0:n, :], src, ACT.Square, accum_out=out).then_inc(done, 1)
                squared[0] = (done, count)

            squared = [None]

            def first_half(t):
                act.wait_ge(mixed, t + 1)
                squares_of(res[:, t, :], ss[:, t:t + 1], P, ssq, t + 1)
                act.wait_ge(var, t + 1)
                act.activation(rstd[:, t:t + 1], ss[:, t:t + 1], ACT.Sqrt).then_inc(root, 1)

            def second_half(t):
                i, n = t + 1, P if t >= 0 else META
                if t >= 0:
                    act.wait_ge(x3, t + 1)
                squares_of((res[:, t, :] if t >= 0 else meta[0:META, :]), ss2[0:n, i:i + 1], n, ssq2, i + 1)
                act.wait_ge(var2, i + 1)
                act.activation(rstd2[0:n, i:i + 1], ss2[0:n, i:i + 1], ACT.Sqrt).then_inc(root2, 1)

            def take(t):
                i, n, c = (t + 1, P, META + t * P) if t >= 0 else (0, META, 0)
                for half in range(2):
                    act.wait_ge(hn_ps, 2 * i + half + 1)
                    for k in range(4):
                        ins = act.activation(hnT[:, 4 * half + k, c:c + n], psum[:, 2 * (i % 2) + half, k * P:k * P + n],
                                             ACT.Copy, scale=col(g, "norm_mix_pre_2")[:, 4 * half + k:4 * half + k + 1])
                    ins.then_inc(hn_sb, 1)

            def weigh(t):
                act.wait_ge(y_in[t], 32)
                y0 = y[:, 2 * t, :]
                act.activation(y0, y0, ACT.Copy, scale=weight[:, 2 * t:2 * t + 1]).then_inc(weighted, 1)

            act.wait_ge(loads, 32)
            second_half(-1)
            take(-1)
            weigh(0)
            for t in range(TT + 2):
                if t + 1 < TT:
                    weigh(t + 1)
                if t < TT:
                    first_half(t)
                if 1 <= t <= TT:
                    second_half(t - 1)
                if t >= 2:
                    take(t - 2)

        @block.tensor
        def _(pe):
            def project(n):
                w = g["later"].use(pe, g["at2"]["proj"][0]).rearrange("p (k n) -> p k n", k=KT)
                early = half_major(turned_pieces(w, hnT))
                rows, width, pairs = early[n]
                for i, (lhsT, rhs) in enumerate(pairs):
                    pe.matmul(psum[0:rows, 4 + n, 0:width], lhsT, rhs, start=(i == 0), stop=(i == KT - 1))

            for t in range(TT + 1):
                n = P if t else META
                pe.wait_ge(hn_ok, t + 1)
                for half in range(2):
                    if t >= 2:
                        pe.wait_ge(hn_sb, 2 * (t - 2) + half + 1)
                    for k in range(4):
                        last = pe.transpose(psum[:, 2 * (t % 2) + half, k * P:k * P + n],
                                            hn[0:n, t % 2, (4 * half + k) * P:(4 * half + k + 1) * P], ident[0:n, 0:n])
                    last.then_inc(hn_ps, 1)
                if t >= 3:
                    pe.wait_ge(hn_sb, 6)
                    project(t - 3)


def products(pe, psum, banks, ready, taken, state, pieces):
    for rows, width, pairs in pieces:
        n = state[0]
        if n >= len(banks):
            sem, value = taken(n - len(banks)) if callable(taken) else (taken, n - len(banks) + 1)
            pe.wait_ge(sem, value)
        for i, (lhsT, rhs) in enumerate(pairs):
            last = pe.matmul(psum[0:rows, banks[n % len(banks)], 0:width], lhsT, rhs, start=(i == 0),
                             stop=(i == len(pairs) - 1))
        last.then_inc(ready, 1)
        state[0] += 1


def turned_pieces(w, x, k_tiles=KT, m_tiles=4, m0=0, width=P, halves=2):
    size = x.shape[2] // halves
    return [(width, size, [(w[:, k, (m0 + m) * P:(m0 + m) * P + width], x[:, k, i * size:(i + 1) * size]) for k in range(k_tiles)])
            for m in range(m_tiles) for i in range(halves)]


def half_major(pieces):
    return [pieces[2 * m + i] for i in range(2) for m in range(4)]


def row_pieces(w, x, c0=0, tiles=TT + 1):
    cut = lambda t: slice(META + t * P, META + (t + 1) * P) if t < TT else slice(0, META)
    return [(P if t < TT else META, 512, [(x[:, k, cut(t)], w[:, k, c0:c0 + 512]) for k in range(KT)]) for t in range(tiles)]


Z_AT = {3: 0, 2: 128, 1: 384, 0: 768}
Z_META = 1280
Z_ALL = Z_META + L2


def stick_breaking(g):
    nc, a, psum, arena, spare = g["nc"], g["a"], g["psum"], g["arena"], g["spare"]
    hnT, later, at2, ones, upto, future = g["hnT"], g["later"], g["at2"], g["ones"], g["upto"], g["future"]
    b = g["base"] + KT * L2
    g["sbT"] = sbT = arena[:, b:b + 4 * L2].rearrange("p (m n) -> p m n", m=4)
    b += 4 * L2
    qT = arena[:, b:b + 4 * L2].rearrange("p (m n) -> p m n", m=4)
    kz = arena[:, b + 4 * L2:b + 12 * L2].rearrange("p (h n) -> p h n", h=HEADS)
    b += 12 * L2
    v = arena[:, b:b + 2560].rearrange("p (t n) -> p t n", t=TT + 1)
    wbuf = arena[:, b + 2560:b + 2560 + 2 * Z_ALL].rearrange("p (i n) -> p i n", i=2)
    last = arena[:, g["floats"] - 3 * L2:g["floats"]].rearrange("p (h n) -> p h n", h=3)
    g["wlr"] = wlr = spare[:, 7424 + L2:7424 + L2 + P].rearrange("p (k n) -> p k n", k=KT)
    g["gq"] = gq = [last[:, h, :] for h in range(3)] + [spare[:, 7424:7424 + L2]]
    assert b + 2560 + 2 * Z_ALL <= g["floats"] - 3 * L2
    zbuf = spare[:, 0:2 * Z_ALL].rearrange("p (i n) -> p i n", i=2)
    sbuf = spare[:, 2 * Z_ALL:4 * Z_ALL].rearrange("p (i n) -> p i n", i=2)
    BANKS = [4, 5, 6, 7]
    EARLY = 2
    with ExitStack() as cx:
        sem, dma_sem = g["semaphores"](cx)
        ready, taken, zeroed = sem("sb_projection_in_psum"), sem("sb_projection_taken"), sem("sb_pads_set")
        z_ps, z_sb, soft, sp_ok, dstep = sem("z_in_psum"), sem("z_ready"), sem("log_term_ready"), sem("softplus_ready"), sem("sb_dve_step")
        astep = sem("sb_act_step")
        low_rank_in = dma_sem("low_rank_weights_loaded")
        q_ps, q_sb = sem("linear_queries_in_psum"), sem("linear_queries_taken")
        r_ps, arg_ok, w_ok, pv_ps, pv_sb = sem("rest_in_psum"), sem("exponent_ready"), sem("stick_weights_ready"), sem("sb_out_in_psum"), sem("sb_out_ready")
        block = cx.enter_context(nc.Block())

        @block.gpsimd
        def _(pool):
            step = Steps(pool, zeroed)
            for h in range(HEADS):
                lo = 64 * (1 - h % 2)
                step(pool.memset(kz[lo:lo + 64, h, :], 0.0))
            step(pool.memset(v[:, TT, :], 0.0))
            step(pool.memset(zbuf[:, :, Z_META:], NEG))

        @block.tensor
        def _(pe):
            state = [EARLY]
            for n in range(EARLY):
                pe.nop().then_inc(ready, 1)

            def project(c):
                w = later.use(pe, at2["proj"][c]).rearrange("p (k n) -> p k n", k=KT)
                pieces = row_pieces(w, hnT) if c == 2 else half_major(turned_pieces(w, hnT))
                products(pe, psum, BANKS, ready, taken, state, pieces[EARLY if c == 0 else 0:])
                later.read_by(at2["proj"][c], ready, state[0])

            project(0)
            project(1)

            wq = later.use(pe, at2["proj"][3]).rearrange("p (k n) -> p k n", k=KT)
            q_pieces, q_state = turned_pieces(wq, hnT), [0]
            def scores(h):
                q = qT[:, h // 2, :]
                for n, i in enumerate((3, 2, 1, 0, "x", "m")):
                    c = 6 * h + n
                    if c >= 2:
                        before = {0: 6 * h - 1, 1: 6 * h - 2, 2: c - 1, 3: c - 1, 4: c - 1, 5: 6 * h}[n]
                        if before > 0:
                            pe.wait_ge(z_sb, before)
                    if i == "m":
                        pe.matmul(psum[0:META, 2, 0:META], kz[:, h, 0:META], q[:, 0:META], start=True, stop=True).then_inc(z_ps, 1)
                    elif i == "x":
                        pe.matmul(psum[0:META, 0, :], kz[:, h, 0:META], q[:, META:], start=True, stop=True).then_inc(z_ps, 1)
                    else:
                        lo = META + i * P
                        pe.matmul(psum[:, n % 2, 0:L2 - lo], kz[:, h, lo:lo + P], q[:, lo:], start=True, stop=True).then_inc(z_ps, 1)

            def rest(h):
                s, tail = sbuf[:, h % 2, :], wbuf[:, h % 2, :]
                pe.wait_ge(sp_ok, h + 1)
                for n, i in enumerate((3, 2, 1, 0, "x", "m")):
                    before = {0: 6 * h - 1, 1: 6 * h - 2, 2: 6 * h + 1, 3: 6 * h + 2, 4: 6 * h + 3, 5: 6 * h}[n]
                    if before > 0:
                        pe.wait_ge(arg_ok, before)
                    if i == "m":
                        last = pe.matmul(psum[0:META, 2, META:2 * META], upto[:, 0:META], s[:, Z_META:Z_META + META], start=True, stop=True)
                    elif i == "x":
                        pe.matmul(psum[0:META, 3, :], upto[:, 0:META], s[:, Z_META + META:], start=True, stop=False)
                        last = pe.matmul(psum[0:META, 3, :], ones[:, 0:META], tail[:, Z_AT[0]:Z_AT[0] + 512], start=False, stop=True)
                    else:
                        w = (TT - i) * P
                        o = psum[:, 3 + n % 2, 0:w]
                        last = pe.matmul(o, upto, s[:, Z_AT[i]:Z_AT[i] + w], start=True, stop=(i == 3))
                        if i < 3:
                            later_keys = s if i == 2 else tail
                            last = pe.matmul(o[:, P:], ones, later_keys[:, Z_AT[i + 1]:Z_AT[i + 1] + w - P], start=False, stop=True)
                    last.then_inc(r_ps, 1)

            def values(h):
                w = wbuf[:, h % 2, :]
                pe.wait_ge(w_ok, h + 1)
                if h:
                    pe.wait_ge(pv_sb, 2 * h)
                hc = slice(h * HD, (h + 1) * HD)
                pe.matmul(psum[0:HD, 5, :], v[:, TT, hc], w[:, Z_META + META:], start=True, stop=False)
                for i in range(TT):
                    last = pe.matmul(psum[0:HD, 5, i * P:], v[:, i, hc], w[:, Z_AT[i]:Z_AT[i] + (TT - i) * P],
                                     start=False, stop=(i == TT - 1))
                last.then_inc(pv_ps, 1)
                pe.matmul(psum[0:HD, 6, 0:META], v[:, TT, hc], w[:, Z_META:Z_META + META], start=True, stop=True).then_inc(pv_ps, 1)

            pe.wait_ge(zeroed, HEADS + 1)
            pe.wait_ge(taken, 16)
            scores(0)
            scores(1)
            project(2)
            pe.wait_ge(taken, state[0])
            for h in range(HEADS):
                rest(h)
                products(pe, psum, [7], q_ps, q_sb, q_state, [q_pieces[h]])
                values(h)
                if h + 2 < HEADS:
                    scores(h + 2)
            later.read_by(at2["proj"][3], q_ps, HEADS)

        @block.scalar
        def _(act):
            def take_projection(c, m):
                n = 8 * c + m
                act.wait_ge(ready, n + 1)
                src = psum[:, BANKS[n % 4], :]
                i = slice((m // 4) * HALF, (m // 4 + 1) * HALF)
                if c == 0:
                    last = act.activation(qT[:, m % 4, i], src[:, 0:HALF], ACT.Copy, scale=HD ** -0.5)
                elif c == 1:
                    act.activation(kz[0:64, 2 * (m % 4), i], src[0:64, 0:HALF], ACT.Copy)
                    last = act.activation(kz[64:128, 2 * (m % 4) + 1, i], src[64:128, 0:HALF], ACT.Copy)
                else:
                    if m == TT:
                        act.wait_ge(zeroed, HEADS + 1)
                    rows = P if m < TT else META
                    last = act.activation(v[0:rows, m, :], src[0:rows, :], ACT.Copy)
                last.then_inc(taken, 1)

            for n in range(16):
                take_projection(n // 8, n % 8)
            step = Steps(act, astep)

            def log_term(h):
                act.wait_ge(z_sb, 6 * h + 6)
                if h >= 2:
                    act.wait_ge(pv_ps, 2 * (h - 1))
                z, w = zbuf[:, h % 2, :], wbuf[:, h % 2, :]
                step(act.activation(w, z, ACT.Abs))
                step(act.activation(w, w, ACT.Exp, scale=-1.0))
                act.activation(w, w, ACT.Ln, bias=1.0).then_inc(soft, 1)

            def take(h):
                lo = 64 * (h % 2)
                act.wait_ge(pv_ps, 2 * h + 1)
                act.activation(sbT[lo:lo + 64, h // 2, META:], psum[0:HD, 5, :], ACT.Copy).then_inc(pv_sb, 1)
                act.wait_ge(pv_ps, 2 * h + 2)
                act.activation(sbT[lo:lo + 64, h // 2, 0:META], psum[0:HD, 6, 0:META], ACT.Copy).then_inc(pv_sb, 1)

            act.wait_ge(zeroed, HEADS + 2)
            log_term(0)
            take_projection(2, 0)
            take_projection(2, 1)
            log_term(1)
            for m in range(2, TT + 1):
                take_projection(2, m)
            for h in range(HEADS):
                act.wait_ge(arg_ok, 6 * h + 6)
                act.activation(wbuf[:, h % 2, :], zbuf[:, h % 2, :], ACT.Exp).then_inc(w_ok, 1)
                act.wait_ge(q_ps, h + 1)
                act.activation(gq[h // 2][:, (h % 2) * HALF:(h % 2 + 1) * HALF], psum[:, 7, 0:HALF], ACT.Copy,
                               scale=DK ** -0.5).then_inc(q_sb, 1)
                take(h)
                if h + 2 < HEADS:
                    log_term(h + 2)

        @block.vector
        def _(dve):
            step = Steps(dve, dstep)

            def take_scores(h):
                z = zbuf[:, h % 2, :]
                if h >= 2:
                    dve.wait_ge(w_ok, h - 1)
                for n, i in enumerate((3, 2, 1, 0, "x", "m")):
                    dve.wait_ge(z_ps, 6 * h + n + 1)
                    if i == "m":
                        last = dve.tensor_tensor(z[0:META, Z_META:Z_META + META], psum[0:META, 2, 0:META], future[0:META, 0:META], ALU.add)
                    elif i == "x":
                        last = dve.tensor_copy(z[0:META, Z_META + META:], psum[0:META, 0, :])
                    else:
                        w, o = (TT - i) * P, Z_AT[i]
                        if i < 3:
                            dve.tensor_copy(z[:, o + P:o + w], psum[:, n % 2, P:w])
                        last = dve.tensor_tensor(z[:, o:o + P], psum[:, n % 2, 0:P], future, ALU.add)
                    last.then_inc(z_sb, 1)

            def softplus(h):
                z, w, s = zbuf[:, h % 2, :], wbuf[:, h % 2, :], sbuf[:, h % 2, :]
                dve.wait_ge(soft, h + 1)
                step(dve.scalar_tensor_tensor(out=s, in0=z, scalar=0.0, in1=w, op0=ALU.max, op1=ALU.add))
                for i in (2, 1, 0):
                    o, later_keys = Z_AT[i], (s if i == 2 else w)
                    step(dve.tensor_copy(w[:, o:o + P], s[:, o:o + P]))
                    step(dve.tensor_tensor(w[:, o + P:o + (TT - i) * P], s[:, o + P:o + (TT - i) * P],
                                           later_keys[:, Z_AT[i + 1]:Z_AT[i + 1] + (TT - i - 1) * P], ALU.add))
                dve.engine_nop().then_inc(sp_ok, 1)

            def exponents(h):
                z = zbuf[:, h % 2, :]
                for n, i in enumerate((3, 2, 1, 0, "x", "m")):
                    dve.wait_ge(r_ps, 6 * h + n + 1)
                    if i == "m":
                        p, r = z[0:META, Z_META:Z_META + META], psum[0:META, 2, META:2 * META]
                    elif i == "x":
                        p, r = z[0:META, Z_META + META:], psum[0:META, 3, :]
                    else:
                        w = (TT - i) * P
                        p, r = z[:, Z_AT[i]:Z_AT[i] + w], psum[:, 3 + n % 2, 0:w]
                    dve.tensor_tensor(p, p, r, ALU.subtract).then_inc(arg_ok, 1)

            dve.wait_ge(zeroed, HEADS + 2)
            take_scores(0)
            take_scores(1)
            softplus(0)
            for h in range(HEADS):
                exponents(h)
                if h + 1 < HEADS:
                    softplus(h + 1)
                if h + 2 < HEADS:
                    take_scores(h + 2)

        @block.sync
        def _(sp):
            later.load_until(sp, at2["proj"][3] + 1)
            sp.dma_start(wlr, a["w_in_2"][0][:, 4608:4624].rearrange("(k p) n -> p k n", p=P)).then_inc(low_rank_in, 16)
            later.load_until(sp, at2["proj"][3] + 1 + SLOTS)
            sp.wait_ge(low_rank_in, 16)
    later.new_phase()


def gated_linear(g):
    nc, a, psum, arena, spare, small = g["nc"], g["a"], g["psum"], g["arena"], g["spare"], g["small"]
    hnT, later, at2, ones, ident = g["hnT"], g["later"], g["at2"], g["ones"], g["ident"]
    b = g["base"] + 12 * L2
    GW = GH * L2
    flat = lambda x: x.rearrange("p h n -> p (h n)")
    heads = lambda x: x.rearrange("p (h n) -> p h n", h=GH)
    q, k = heads(arena[:, b:b + GW]), heads(arena[:, b + GW:b + 2 * GW])
    o = b + 2 * GW
    v = arena[:, o:o + (TT + 1) * D].rearrange("p (t n) -> p t n", t=TT + 1)
    o += (TT + 1) * D
    att = arena[:, o:o + GH * 512].rearrange("p (h n) -> p h n", h=GH)
    attm = arena[0:META, o + 2048:o + 2048 + GH * META].rearrange("p (h n) -> p h n", h=GH)
    o += 2560
    cs = heads(arena[:, o:o + GW])
    g["gr"] = gr = arena[:, g["floats"] - (TT + 1) * HALF:g["floats"]].rearrange("p (i n) -> p i n", i=TT + 1)
    wlr = g["wlr"]
    e, qe, ke = heads(spare[:, 0:GW]), heads(spare[:, GW:2 * GW]), heads(spare[:, 2 * GW:3 * GW])
    masks = spare[:, 3 * GW:3 * GW + LEVELS * P].rearrange("p (l n) -> p l n", l=LEVELS)
    xor = spare[:, 3 * GW + LEVELS * P:3 * GW + LEVELS * P + P]
    wup = spare[0:16, 0:512]
    lrT = spare[0:16, 512:512 + L2]
    pi = spare[:, 1100:1228].bitcast(I32)
    pj = spare[:, 1228:1356].bitcast(I32)
    g["oT"] = oT = spare[:, GW:3 * GW].rearrange("p (k n) -> p k n", k=KT)
    state = spare[:, 0:1024].rearrange("p (h n) -> p h n", h=GH)
    kd = spare[:, 1024:2048].rearrange("p (i n) -> p i n", i=2)
    rows = spare[:, 3 * GW:3 * GW + D]
    squares = spare[:, 3 * GW + D:3 * GW + D + DV]
    nbias = small[:, 300:304]
    elast = small[:, 304:324].rearrange("p (h c) -> p h c", h=GH)
    nlast = small[:, 324:344].rearrange("p (h c) -> p h c", h=GH)
    ss, rstd = small[:, 344:348], small[:, 348:352]
    span = [(0, META)] + [(META + c * P, P) for c in range(TT)]
    BANKS = [0, 1, 2]

    def halves(x, l):
        size = 2 << l
        if size <= META:
            y = flat(x).rearrange("p (b t) -> p b t", t=size)
            return y[:, :, 0:size // 2], y[:, :, size // 2:], y[:, :, size // 2 - 1:size // 2].to_broadcast([P, GW // size, size // 2])
        y = x[:, :, META:].rearrange("p h (b t) -> p h b t", t=size)
        return (y[:, :, :, 0:size // 2], y[:, :, :, size // 2:],
                y[:, :, :, size // 2 - 1:size // 2].to_broadcast([P, GH, 512 // size, size // 2]))

    def level_part(x, l):
        return flat(x) if (2 << l) <= META else x[:, :, META:]

    with ExitStack() as cx:
        sem, dma_sem = g["semaphores"](cx)
        ready, taken, small_in = sem("gla_projection_in_psum"), sem("gla_projection_taken"), dma_sem("gate_weights_loaded")
        q_ok = sem("queries_in_place")
        gr_ps, gr_sb = sem("gate_rows_in_psum"), sem("gate_rows_taken")
        iota_ok, masks_ok, att0 = sem("positions_counted"), sem("masks_built"), sem("att_zeroed")
        astep, dstep = sem("gla_act_step"), sem("gla_dve_step")
        nb_ok, nx_ok, soft, cs_ok = sem("gate_bias_negated"), sem("gate_logits_ready"), sem("gate_log_ready"), sem("decay_sums_ready")
        diff, e_ok, qk_ok, lv_ps, lv_ok = sem("exponents_ready"), sem("decays_ready"), sem("decayed_ready"), sem("level_in_psum"), sem("level_taken")
        dec, kd_ps, kd_sb = sem("chunk_decays_applied"), sem("keys_in_psum"), sem("keys_ready")
        qd_e, kd_e, q_done = sem("query_decay_ready"), sem("key_decay_ready"), sem("queries_decayed")
        o_ps, s_ps, s_ok = sem("out_in_psum"), sem("state_in_psum"), sem("state_ready")
        sq, var, root = sem("out_squares"), sem("out_variance"), sem("out_root")
        rows_ok, oT_ps, oT_ok = sem("out_rows_ready"), sem("oT_in_psum"), sem("oT_ready")
        block = cx.enter_context(nc.Block())

        @block.gpsimd
        def _(pool):
            step = Steps(pool, iota_ok)
            step(pool.iota(pi, [[0, P]], base=0, channel_multiplier=1))
            step(pool.iota(pj, [[1, P]], base=0, channel_multiplier=0))
            pool.memset(att, 0.0).then_inc(att0, 1)
            pool.wait_ge(att0, 1)
            pool.memset(attm, 0.0).then_inc(att0, 1)

        @block.tensor
        def _(pe):
            st = [0]
            products(pe, psum, BANKS, ready, taken, st, [
                (16, HALF, [(wlr[:, kk, :], hnT[:, kk, i * HALF:(i + 1) * HALF]) for kk in range(KT)]) for i in range(2)])
            pe.wait_ge(taken, 2)
            pe.wait_ge(small_in, 16)
            products(pe, psum, BANKS, ready, taken, st, [
                (P, HALF, [(wup[:, h * P:(h + 1) * P], lrT[:, i * HALF:(i + 1) * HALF])]) for h in range(GH) for i in range(2)])
            w = later.use(pe, at2["proj"][4]).rearrange("p (k n) -> p k n", k=KT)
            products(pe, psum, BANKS, ready, taken, st, turned_pieces(w, hnT))
            later.read_by(at2["proj"][4], ready, st[0])
            pe.wait_ge(taken, 18)

            def level(n, l):
                qq, kk = (q, k) if l is None else (qe, ke)
                if l is not None:
                    pe.wait_ge(qk_ok, n)
                if n:
                    pe.wait_ge(lv_ok, n)
                for h in range(GH):
                    for c0, _ in span[1:]:
                        last = pe.matmul(psum[:, 4 + h, c0 - META:c0 - META + P], kk[:, h, c0:c0 + P], qq[:, h, c0:c0 + P],
                                         start=True, stop=True)
                    if l is None or (2 << l) <= META:
                        last = pe.matmul(psum[0:META, 3, h * META:(h + 1) * META], kk[:, h, 0:META], qq[:, h, 0:META],
                                         start=True, stop=True)
                last.then_inc(lv_ps, 1)

            rowsv = []
            for c in range(2):
                w = later.use(pe, at2["proj"][5 + c]).rearrange("p (k n) -> p k n", k=KT)
                rowsv.append(row_pieces(w, hnT))
            pe.wait_ge(q_ok, 1)
            level(0, None)
            for n in range(1, LEVELS + 1):
                p = n - 1
                if p < 5:
                    products(pe, psum, BANKS, ready, taken, st, [rowsv[0][p]])
                    if p == 4:
                        later.read_by(at2["proj"][5], ready, st[0])
                else:
                    products(pe, psum, BANKS, ready, taken, st, [rowsv[1][p - 5]])
                level(n, n - 1)
            products(pe, psum, BANKS, ready, taken, st, rowsv[1][LEVELS - 5:])
            later.read_by(at2["proj"][6], ready, st[0])
            pe.wait_ge(taken, st[0])
            pe.wait_ge(lv_ok, LEVELS + 1)
            wr = later.use(pe, at2["proj"][7]).rearrange("p (k n) -> p k n", k=KT)
            gr_pieces, gr_state = turned_pieces(wr, hnT), [0]
            pe.wait_ge(dec, 1)
            for c, (c0, n) in enumerate(span):
                vt = v[0:n, (c - 1) % (TT + 1), :]
                for h in range(GH):
                    if c and h == 0:
                        pe.wait_ge(kd_sb, c)
                    last = pe.transpose(psum[0:n, 0, h * P:(h + 1) * P], k[:, h, c0:c0 + n], ident)
                last.then_inc(kd_ps, 1)
                if c:
                    pe.wait_ge(s_ok, 2 * c)
                    pe.wait_ge(rows_ok, c)
                for h in range(GH):
                    at_ = attm[:, h, :] if c == 0 else att[:, h, c0 - META:c0 - META + P]
                    dst = psum[0:n, 1 + h // 2, (h % 2) * DV:(h % 2 + 1) * DV]
                    last = pe.matmul(dst, at_, vt[:, h * DV:(h + 1) * DV], start=True, stop=(c == 0))
                    if c:
                        last = pe.matmul(dst, q[:, h, c0:c0 + n], state[:, h, :], start=False, stop=True)
                last.then_inc(o_ps, 1)
                if c < TT:
                    pe.wait_ge(kd_sb, c + 1)
                    for h in range(GH):
                        last = pe.matmul(psum[:, 3 + h // 2, (h % 2) * DV:(h % 2 + 1) * DV], kd[0:n, c % 2, h * DK:(h + 1) * DK],
                                         vt[:, h * DV:(h + 1) * DV], start=True, stop=True)
                    last.then_inc(s_ps, 1)
                products(pe, psum, [7], gr_ps, gr_sb, gr_state, [gr_pieces[c]])
                pe.wait_ge(rows_ok, c + 1)
                for half in range(2):
                    if c:
                        pe.wait_ge(oT_ok, 2 * (c - 1) + half + 1)
                    for kk in range(4):
                        last = pe.transpose(psum[:, 5 + half, kk * P:kk * P + n],
                                            rows[0:n, (4 * half + kk) * P:(4 * half + kk + 1) * P], ident[0:n, 0:n])
                    last.then_inc(oT_ps, 1)

        @block.scalar
        def _(act):
            step = Steps(act, astep)
            count = [0]

            def take(dst, rows_, width, scale=1.0, func=ACT.Copy, bias=None, done=None):
                n = count[0]
                act.wait_ge(ready, n + 1)
                kw = {} if bias is None else {"bias": bias}
                act.activation(dst, psum[0:rows_, BANKS[n % 3], 0:width], func, scale=scale, **kw).then_inc(taken, 1)
                count[0] += 1

            half = lambda x, h, i: x[:, h, i * HALF:(i + 1) * HALF]
            for i in range(2):
                take(lrT[:, i * HALF:(i + 1) * HALF], 16, HALF)
            act.wait_ge(nb_ok, 1)
            for h in range(GH):
                for i in range(2):
                    take(half(qe, h, i), P, HALF, scale=-1.0, func=ACT.Identity, bias=nbias[:, h:h + 1])
            for h in range(GH):
                last = act.activation(q[:, h, :], g["gq"][h], ACT.Copy)
            last.then_inc(q_ok, 1)
            act.wait_ge(taken, 10)
            act.wait_ge(masks_ok, 1)
            step(act.activation(flat(e), flat(qe), ACT.Abs))
            step(act.activation(flat(e), flat(e), ACT.Exp, scale=-1.0))
            act.activation(flat(e), flat(e), ACT.Ln, bias=1.0).then_inc(soft, 1)
            for h in range(GH):
                for i in range(2):
                    take(half(k, h, i), P, HALF)
            for n in range(LEVELS):
                t, c = (n, 0) if n < 5 else (n - 5, 1)
                rows_ = P if t < TT else META
                act.wait_ge(diff, n + 1)
                act.activation(level_part(e, n), level_part(e, n), ACT.Exp, scale=1.0 / 16).then_inc(e_ok, 1)
                take(v[0:rows_, t, c * 512:(c + 1) * 512], rows_, 512)
            act.wait_ge(qk_ok, LEVELS)
            act.activation(flat(e), flat(cs), ACT.Exp, scale=-1.0 / 16).then_inc(qd_e, 1)
            act.wait_ge(q_done, 1)
            for h in range(GH):
                for c, (c0, n) in enumerate(span):
                    last = act.activation(e[:, h, c0:c0 + n], cs[:, h, c0:c0 + n], ACT.Exp, scale=1.0 / 16, bias=nlast[:, h, c:c + 1])
            last.then_inc(kd_e, 1)
            for t in range(LEVELS - 5, TT + 1):
                rows_ = P if t < TT else META
                take(v[0:rows_, t, 512:1024], rows_, 512)

            def take_oT(c):
                c0, n = span[c]
                for i in range(2):
                    act.wait_ge(oT_ps, 2 * c + i + 1)
                    act.activation(oT[:, 4 * i:4 * i + 4, c0:c0 + n],
                                   psum[:, 5 + i, :].rearrange("p (k n) -> p k n", k=4)[:, :, 0:n], ACT.Copy).then_inc(oT_ok, 1)

            for c, (c0, n) in enumerate(span):
                act.wait_ge(kd_ps, c + 1)
                act.activation(kd[0:n, c % 2, :], psum[0:n, 0, :], ACT.Copy).then_inc(kd_sb, 1)
                act.wait_ge(o_ps, c + 1)
                for h in range(GH):
                    if 4 * c + h:
                        act.wait_ge(sq, 4 * c + h)
                    act.activation(squares[0:n, :], psum[0:n, 1 + h // 2, (h % 2) * DV:(h % 2 + 1) * DV], ACT.Square,
                                   accum_out=ss[0:n, h:h + 1]).then_inc(sq, 1)
                act.wait_ge(var, c + 1)
                act.activation(rstd[0:n, :], rstd[0:n, :], ACT.Sqrt).then_inc(root, 1)
                act.wait_ge(gr_ps, c + 1)
                act.activation(gr[:, c, :], psum[:, 7, 0:HALF], ACT.Copy).then_inc(gr_sb, 1)
                take_oT(c)

        @block.vector
        def _(dve):
            step = Steps(dve, dstep)
            dve.tensor_scalar(nbias, col(g, "b_gk_2"), -1.0, None, ALU.mult).then_inc(nb_ok, 1)
            dve.wait_ge(iota_ok, 2)
            step(dve.tensor_tensor(pi, pi, pj, ALU.bitwise_xor))
            for l in range(LEVELS):
                step(dve.tensor_scalar(pj, pi, l, None, ALU.logical_shift_right))
                step(dve.tensor_copy(xor, pj))
                step(dve.scalar_tensor_tensor(out=masks[:, l, :], in0=xor, scalar=1.0, in1=g["before"], op0=ALU.is_equal,
                                              op1=ALU.mult))
            dve.engine_nop().then_inc(masks_ok, 1)
            dve.wait_ge(q_ok, 1)
            dve.wait_ge(soft, 1)
            step(dve.scalar_tensor_tensor(out=flat(ke), in0=flat(qe), scalar=0.0, in1=flat(e), op0=ALU.max, op1=ALU.add))
            for h in range(GH):
                for c0, n in span:
                    last = dve.tensor_tensor_scan(cs[:, h, c0:c0 + n], ones[:, 0:n], ke[:, h, c0:c0 + n], 0.0, ALU.mult, ALU.add)
            step(last)

            def exponents(l):
                left, right, mid = halves(cs, l)
                eleft, eright, _ = halves(e, l)
                dve.tensor_tensor(eleft, left, mid, ALU.subtract)
                dve.tensor_tensor(eright, mid, right, ALU.subtract).then_inc(diff, 1)

            def take_level(n, l):
                dve.wait_ge(lv_ps, n + 1)
                m = ident if l is None else masks[:, l, :]
                for h in range(GH):
                    last = dve.copy_predicated(att[:, h, :].rearrange("p (c n) -> p c n", c=TT),
                                               m.bitcast(U32).unsqueeze(1).to_broadcast([P, TT, P]),
                                               psum[:, 4 + h, :].rearrange("p (c n) -> p c n", c=TT))
                if l is None or (2 << l) <= META:
                    last = dve.copy_predicated(attm, m[0:META, 0:META].bitcast(U32).unsqueeze(1).to_broadcast([META, GH, META]),
                                               psum[0:META, 3, 0:GH * META].rearrange("p (h n) -> p h n", h=GH))
                last.then_inc(lv_ok, 1)

            exponents(0)
            dve.wait_ge(att0, 2)
            take_level(0, None)
            for l in range(LEVELS):
                dve.wait_ge(e_ok, l + 1)
                el, er, _ = halves(e, l)
                kl, _, _ = halves(k, l)
                _, qr, _ = halves(q, l)
                kel, _, _ = halves(ke, l)
                _, qer, _ = halves(qe, l)
                dve.tensor_tensor(kel, kl, el, ALU.mult)
                dve.tensor_tensor(qer, qr, er, ALU.mult).then_inc(qk_ok, 1)
                if l + 1 < LEVELS:
                    dve.wait_ge(qk_ok, l + 1)
                    exponents(l + 1)
                take_level(l + 1, l)
            dve.wait_ge(qd_e, 1)
            step(dve.tensor_copy(elast, e[:, :, META - 1:L2:P]))
            step(dve.tensor_scalar(nlast, cs[:, :, META - 1:L2:P], -1.0 / 16, None, ALU.mult))
            dve.tensor_tensor(flat(q), flat(q), flat(e), ALU.mult).then_inc(q_done, 1)
            dve.wait_ge(kd_e, 1)
            dve.tensor_tensor(flat(k), flat(k), flat(e), ALU.mult).then_inc(dec, 1)
            dve.wait_ge(dec, 1)
            for c, (c0, n) in enumerate(span):
                if c < TT:
                    dve.wait_ge(s_ps, c + 1)
                    dve.wait_ge(o_ps, c + 1)
                    for i in range(2):
                        if c == 0:
                            last = dve.tensor_copy(state[:, 2 * i:2 * i + 2, :], psum[:, 3 + i, :].rearrange("p (h n) -> p h n", h=2))
                        else:
                            for h in (2 * i, 2 * i + 1):
                                last = dve.scalar_tensor_tensor(
                                    out=state[:, h, :], in0=state[:, h, :], scalar=elast[:, h, c:c + 1],
                                    in1=psum[:, 3 + i, (h % 2) * DV:(h % 2 + 1) * DV], op0=ALU.mult, op1=ALU.add)
                        last.then_inc(s_ok, 1)
                dve.wait_ge(sq, 4 * c + 4)
                if c:
                    dve.wait_ge(root, c)
                dve.tensor_scalar(rstd[0:n, :], ss[0:n, :], 1.0 / DV, EPS, ALU.mult, ALU.add).then_inc(var, 1)
                dve.wait_ge(root, c + 1)
                step(dve.reciprocal(rstd[0:n, :], rstd[0:n, :]))
                if c:
                    dve.wait_ge(oT_ps, 2 * c)
                for h in range(GH):
                    last = dve.tensor_scalar(rows[0:n, h * DV:(h + 1) * DV], psum[0:n, 1 + h // 2, (h % 2) * DV:(h % 2 + 1) * DV],
                                             rstd[0:n, h:h + 1], None, ALU.mult)
                last.then_inc(rows_ok, 1)

        @block.sync
        def _(sp):
            sp.dma_start(wup, a["w_gk_up_2"][0]).then_inc(small_in, 16)
            later.load_until(sp, at2["proj"][6] + 1 + SLOTS)
    later.new_phase()


class PostNorm:

    def __init__(self, g, sem, small_at, meta_first=False):
        self.g, s, self.meta_first = g, g["small"], meta_first
        self.parts = s[:, small_at:small_at + 10].rearrange("p (t n) -> p t n", n=2)
        self.ss, self.rstd = s[:, small_at + 10:small_at + 15], s[:, small_at + 15:small_at + 20]
        self.sq, self.var, self.root, self.added = sem("row_squares"), sem("row_variance"), sem("row_root"), sem("rows_added")

    def rows(self, t):
        if self.meta_first:
            return (self.g["res"][:, t - 1, :], P) if t else (self.g["meta"][0:META, :], META)
        return self.g["res"][:, t, :], P

    def act(self, act, t, banks, squares):
        _, n = self.rows(t)
        for i, bank in enumerate(banks):
            if 2 * t + i:
                act.wait_ge(self.sq, 2 * t + i)
            act.activation(squares[0:n, 0:512], self.g["psum"][0:n, bank, :], ACT.Square,
                           accum_out=self.parts[0:n, t, i:i + 1]).then_inc(self.sq, 1)
        act.wait_ge(self.var, t + 1)
        act.activation(self.rstd[0:n, t:t + 1], self.ss[0:n, t:t + 1], ACT.Sqrt).then_inc(self.root, 1)

    def dve(self, dve, step, t, banks, gain, tmp):
        rows, n = self.rows(t)
        rstd = self.rstd[0:n, t:t + 1]
        dve.wait_ge(self.sq, 2 * t + 2)
        step(dve.tensor_tensor(self.ss[0:n, t:t + 1], self.parts[0:n, t, 0:1], self.parts[0:n, t, 1:2], ALU.add))
        dve.tensor_scalar(self.ss[0:n, t:t + 1], self.ss[0:n, t:t + 1], 1.0 / D, EPS, ALU.mult, ALU.add).then_inc(self.var, 1)
        dve.wait_ge(self.root, t + 1)
        step(dve.reciprocal(rstd, rstd))
        for i, bank in enumerate(banks):
            c = slice(512 * i, 512 * i + 512)
            step(dve.scalar_tensor_tensor(out=tmp[0:n, c], in0=self.g["psum"][0:n, bank, :], scalar=rstd, in1=gain[0:n, c],
                                          op0=ALU.mult, op1=ALU.mult))
        dve.tensor_tensor(rows, rows, tmp[0:n, 0:D], ALU.add).then_inc(self.added, 1)


FFN_BANKS = (2, 0, 1, 3, 4, 5)
UP_HALF = (SEQ + 2) // 2


def mix_and_project(g):
    nc, a, psum, arena, spare, small = g["nc"], g["a"], g["psum"], g["arena"], g["spare"], g["small"]
    hnT, later, at2, ident, sbT, oT = g["hnT"], g["later"], g["at2"], g["ident"], g["sbT"], g["oT"]
    b = g["base"] + 12 * L2
    mixT = arena[:, b:b + KT * L2].rearrange("p (k n) -> p k n", k=KT)
    b += KT * L2
    sg = arena[:, b:b + KT * L2].rearrange("p (k n) -> p k n", k=KT)
    b += KT * L2
    tmp = arena[:, b:b + 2 * HALF].rearrange("p (i n) -> p i n", i=2)
    b += 2 * HALF
    gain = arena[:, b:b + D]
    part = arena[:, b + D:b + 2 * D]
    squares = arena[:, b + 2 * D:b + 3 * D]
    hn = sg.rearrange("p k n -> p (k n)")[:, 0:2 * D].rearrange("p (i n) -> p i n", i=2)
    ss, rstd = small[:, 400:405], small[:, 405:410]
    BANKS = [0, 1, 2, 3]
    GR, GLA, SBG, SBO, WO = 0, 16, 48, 64, 80
    EARLY = TT + 1

    with ExitStack() as cx:
        sem, dma_sem = g["semaphores"](cx)
        loads = dma_sem("mix_gain_loaded")
        ready, taken, gate_ok = sem("mixing_in_psum"), sem("mixing_taken"), sem("gate_ready")
        gated, mixed, dstep = sem("linear_output_gated"), sem("mix_ready"), sem("mix_dve_step")
        wo_ps = sem("wo_in_psum")
        sq2, var2, root2, hn_ok, hn_ps, hn_sb = (sem("h2_squares"), sem("h2_variance"), sem("h2_root"), sem("hn2_ready"),
                                                 sem("hn2T_in_psum"), sem("hn2T_ready"))
        post = PostNorm(g, sem, 360, meta_first=True)
        block = cx.enter_context(nc.Block())
        WB = [(0, 1), (2, 3)]

        def read(n):
            if n < GLA:
                return gate_ok, n + 1
            if n < SBG:
                c, i = divmod(n - GLA, 16)
                return (gate_ok, GLA + 8 * c + i + 1) if i < 8 else (taken, 8 * c + i - 8 + 1)
            return (gate_ok, 32 + n - SBG + 1) if n < SBO else (taken, 16 + n - SBO + 1)

        @block.tensor
        def _(pe):
            st = [EARLY]
            for n in range(EARLY):
                pe.nop().then_inc(ready, 1)

            def use(kind, n):
                return later.use(pe, at2[kind][n])

            def turned(kind, n, x, skip=0, **kw):
                w = use(kind, n).rearrange("p (k n) -> p k n", k=kw.get("k_tiles", KT))
                products(pe, psum, BANKS, ready, read, st, turned_pieces(w, x, **kw)[skip:])
                later.read_by(at2[kind][n], ready, st[0])

            turned("proj", 7, hnT, skip=EARLY)
            turned("proj", 8, hnT)
            pe.wait_ge(gated, 16)
            for c in range(2):
                turned("mgla", c, hnT)
                turned("gout", c, oT)
            for c in range(2):
                turned("msb", c, hnT)
            turned("sbout", 0, sbT, k_tiles=4, m_tiles=8)
            pe.wait_ge(taken, 32)
            pe.wait_ge(mixed, 1)
            w = [use("wo", n).rearrange("p (k n) -> p k n", k=KT) for n in range(2)]
            pieces = [row_pieces(w[n], mixT) for n in range(2)]
            pieces = [p[TT:] + p[:TT] for p in pieces]

            def turn(t):
                n = P if t else META
                pe.wait_ge(hn_ok, t + 1)
                for half in range(2):
                    if t >= 2:
                        pe.wait_ge(hn_sb, 2 * (t - 2) + half + 1)
                    for k in range(4):
                        last = pe.transpose(psum[:, 4 + 2 * (t % 2) + half, k * P:k * P + n],
                                            hn[0:n, t % 2, (4 * half + k) * P:(4 * half + k + 1) * P], ident[0:n, 0:n])
                    last.then_inc(hn_ps, 1)

            for t in range(TT + 1):
                if t >= 2:
                    pe.wait_ge(post.added, t - 1)
                for n in range(2):
                    rows, width, pairs = pieces[n][t]
                    for i, (lhsT, rhs) in enumerate(pairs):
                        last = pe.matmul(psum[0:rows, WB[t % 2][n], :], lhsT, rhs, start=(i == 0), stop=(i == KT - 1))
                    last.then_inc(wo_ps, 1)
                if t >= 2:
                    turn(t - 2)
            later.read_by(at2["wo"][0], wo_ps, 9)
            later.read_by(at2["wo"][1], wo_ps, 10)
            turn(TT - 1)
            pe.wait_ge(hn_sb, 6)
            pe.wait_ge(post.added, TT)
            wu = use("up", 0).rearrange("p (k n) -> p k n", k=KT)
            for m in range(2):
                for k in range(KT):
                    pe.matmul(psum[:, FFN_BANKS[3 * m], 0:UP_HALF], wu[:, k, m * P:(m + 1) * P],
                              hnT[:, k, META - 2:META - 2 + UP_HALF], start=(k == 0), stop=(k == KT - 1))
            turn(TT)

        @block.scalar
        def _(act):
            def gate(n, dst, func):
                act.wait_ge(ready, n + 1)
                src = g["gr"][:, n, :] if n < EARLY else psum[:, BANKS[n % 4], 0:HALF]
                act.activation(dst, src, func).then_inc(gate_ok, 1)

            half = lambda x, n: x[:, n // 2, (n % 2) * HALF:(n % 2 + 1) * HALF]
            for n in range(16):
                if n >= 2:
                    act.wait_ge(gated, n - 1)
                gate(GR + n, tmp[:, n % 2, :], ACT.Silu)
            for c in range(2):
                if c:
                    act.wait_ge(taken, 8)
                for n in range(8):
                    gate(GLA + 16 * c + n, half(sg, n), ACT.Sigmoid)
            act.wait_ge(taken, 16)
            for n in range(16):
                gate(SBG + n, half(sg, n), ACT.Sigmoid)

            def second_half(t):
                rows, n = post.rows(t)
                act.wait_ge(post.added, t + 1)
                act.wait_ge(post.sq, 2 * t + 2)
                if t:
                    act.wait_ge(sq2, t)
                act.activation(squares[0:n, :], rows, ACT.Square, accum_out=ss[0:n, t:t + 1]).then_inc(sq2, 1)
                act.wait_ge(var2, t + 1)
                act.activation(rstd[0:n, t:t + 1], ss[0:n, t:t + 1], ACT.Sqrt).then_inc(root2, 1)

            def take(t):
                n, c = (P, META + (t - 1) * P) if t else (META, 0)
                for i in range(2):
                    act.wait_ge(hn_ps, 2 * t + i + 1)
                    for k in range(4):
                        last = act.activation(hnT[:, 4 * i + k, c:c + n], psum[:, 4 + 2 * (t % 2) + i, k * P:k * P + n],
                                              ACT.Copy, scale=col(g, "norm_ffn_pre_2")[:, 4 * i + k:4 * i + k + 1])
                    last.then_inc(hn_sb, 1)

            for t in range(TT + 2):
                if t <= TT:
                    act.wait_ge(wo_ps, 2 * t + 2)
                    if t:
                        act.wait_ge(sq2, t)
                    post.act(act, t, WB[t % 2], squares)
                    second_half(t)
                if t >= 1:
                    take(t - 1)

        @block.vector
        def _(dve):
            step = Steps(dve, dstep)
            half = lambda x, n: x[:, n // 2, (n % 2) * HALF:(n % 2 + 1) * HALF]
            bank = lambda n: psum[:, BANKS[n % 4], 0:HALF]
            for n in range(16):
                dve.wait_ge(gate_ok, n + 1)
                dve.scalar_tensor_tensor(out=half(oT, n), in0=tmp[:, n % 2, :], scalar=col(g, "gla_head_norm_2")[:, (n // 2) % 2:(n // 2) % 2 + 1],
                                         in1=half(oT, n), op0=ALU.mult, op1=ALU.mult).then_inc(gated, 1)
            for c in range(2):
                for n in range(8):
                    dve.wait_ge(gate_ok, 16 + 8 * c + n + 1)
                    dve.wait_ge(ready, GLA + 16 * c + 8 + n + 1)
                    dve.tensor_tensor(half(mixT, 8 * c + n), half(sg, n), bank(n), ALU.mult).then_inc(taken, 1)
            dve.wait_ge(taken, 16)
            for n in range(16):
                dve.wait_ge(gate_ok, 32 + n + 1)
                dve.wait_ge(ready, SBO + n + 1)
                dve.tensor_tensor(half(sg, n), half(sg, n), bank(n), ALU.mult).then_inc(taken, 1)
                dve.wait_ge(taken, 16 + n + 1)
                step(dve.tensor_tensor(half(mixT, n), half(mixT, n), half(sg, n), ALU.add))
            dve.engine_nop().then_inc(mixed, 1)
            dve.wait_ge(loads, 16)

            def rows_out(t):
                rows, n = post.rows(t)
                dve.wait_ge(sq2, t + 1)
                dve.tensor_scalar(ss[0:n, t:t + 1], ss[0:n, t:t + 1], 1.0 / D, EPS, ALU.mult, ALU.add).then_inc(var2, 1)
                dve.wait_ge(root2, t + 1)
                step(dve.reciprocal(rstd[0:n, t:t + 1], rstd[0:n, t:t + 1]))
                if t >= 2:
                    dve.wait_ge(hn_ps, 2 * (t - 1))
                dve.tensor_scalar(hn[0:n, t % 2, :], rows, rstd[0:n, t:t + 1], None, ALU.mult).then_inc(hn_ok, 1)

            for t in range(TT + 1):
                post.dve(dve, step, t, WB[t % 2], gain, part)
                dve.wait_ge(post.added, t + 1)
                rows_out(t)

        @block.sync
        def _(sp):
            sp.dma_start(gain, a["norm_mix_post_2"].to_broadcast([P, D])).then_inc(loads, 16)
            later.load_until(sp, at2["wo"][1] + 1 + SLOTS)
    later.new_phase()


def feed_forward(g):
    nc, a, psum, arena, spare, small = g["nc"], g["a"], g["psum"], g["arena"], g["spare"], g["small"]
    hnT, later, at2, res = g["hnT"], g["later"], g["at2"], g["res"]
    b = g["base"] + KT * L2
    prodT = arena[:, b:b + FM * SEQ].rearrange("p (m n) -> p m n", m=FM)
    UP = SEQ + 2
    up = spare[:, 0:2 * UP].rearrange("p (i n) -> p i n", i=2)
    y = spare[:, 1028:1028 + 1024].rearrange("p (i n) -> p i n", i=2)
    gain, part, squares = spare[:, 2052:2052 + D], spare[:, 3076:3076 + D], spare[:, 4100:4100 + D]
    BANKS = FFN_BANKS
    convw = lambda j, m: g["convw2"][:, j * FM + m:j * FM + m + 1]
    with ExitStack() as cx:
        sem, dma_sem = g["semaphores"](cx)
        loads, stored = dma_sem("ffn_gain_loaded"), dma_sem("output_stored")
        ready, taken, dstep = sem("ffn_in_psum"), sem("ffn_taken"), sem("ffn_dve_step")
        up_ok, conv_ok, act_ok, prod_ok = sem("up_ready"), sem("ffn_conv_ready"), sem("gelu_ready"), sem("product_ready")
        chunk_read, acc = sem("down_chunk_read"), sem("down_in_psum")
        post = PostNorm(g, sem, 420)
        block = cx.enter_context(nc.Block())

        @block.tensor
        def _(pe):
            n = 0
            chunks = len(at2["up"])
            for c in range(chunks):
                tiles = min(4, FM - 4 * c)
                wu = later.use(pe, at2["up"][c])[:, 0:KT * tiles * P].rearrange("p (k n) -> p k n", k=KT)
                wg = later.use(pe, at2["gate"][c])[:, 0:KT * tiles * P].rearrange("p (k n) -> p k n", k=KT)
                for m in range(tiles):
                    for w, lo, width in ((wu, META - 2, UP // 2), (wu, META - 2 + UP // 2, UP // 2), (wg, META, SEQ)):
                        if n >= 6:
                            pe.wait_ge(taken if n % 3 < 2 else prod_ok, 2 * ((n - 6) // 3) + n % 3 + 1 if n % 3 < 2 else (n - 6) // 3 + 1)
                        if n in (0, 3):
                            if n:
                                pe.wait_ge(ready, n)
                            last = pe.nop()
                        else:
                            for k in range(KT):
                                last = pe.matmul(psum[:, BANKS[n % 6], 0:width], w[:, k, m * P:(m + 1) * P], hnT[:, k, lo:lo + width],
                                                 start=(k == 0), stop=(k == KT - 1))
                        last.then_inc(ready, 1)
                        n += 1
                later.read_by(at2["up"][c], ready, n - 1)
                later.read_by(at2["gate"][c], ready, n)
            pe.wait_ge(prod_ok, FM)
            for c in range(len(at2["down"])):
                tiles = min(4, FM - 4 * c)
                w = later.use(pe, at2["down"][c])[:, 0:tiles * D].rearrange("p (k n) -> p k n", k=tiles)
                final = c == len(at2["down"]) - 1
                order = ([(t, k) for t in range(TT) for k in range(tiles)] if final else
                         [(t, k) for k in range(tiles) for t in range(TT)])
                for t, k in order:
                    for i in range(2):
                        kk = 4 * c + k
                        last = pe.matmul(psum[:, 2 * t + i, :], prodT[:, kk, t * P:(t + 1) * P], w[:, k, 512 * i:512 * i + 512],
                                         start=(kk == 0), stop=(kk == FM - 1))
                    if final and k == tiles - 1:
                        last.then_inc(acc, 1)
                if not final:
                    last.then_inc(chunk_read, 1)
                    later.read_by(at2["down"][c], chunk_read, c + 1)

        @block.scalar
        def _(act):
            for m in range(FM):
                if m >= 2:
                    act.wait_ge(conv_ok, m - 1)
                for i in range(2):
                    act.wait_ge(ready, 3 * m + i + 1)
                    act.activation(up[:, m % 2, i * (UP // 2):(i + 1) * (UP // 2)], psum[:, BANKS[(3 * m + i) % 6], 0:UP // 2],
                                   ACT.Copy).then_inc(taken, 1)
                if m:
                    act.wait_ge(conv_ok, m)
                    act.activation(y[:, (m - 1) % 2, :], y[:, (m - 1) % 2, :], ACT.Gelu_apprx_tanh).then_inc(act_ok, 1)
            act.wait_ge(conv_ok, FM)
            act.activation(y[:, (FM - 1) % 2, :], y[:, (FM - 1) % 2, :], ACT.Gelu_apprx_tanh).then_inc(act_ok, 1)
            for t in range(TT):
                act.wait_ge(acc, t + 1)
                post.act(act, t, (2 * t, 2 * t + 1), squares)

        @block.vector
        def _(dve):
            step = Steps(dve, dstep)

            def conv(m):
                dve.wait_ge(taken, 2 * m + 2)
                src, dst = up[:, m % 2, :], y[:, m % 2, :]
                if m >= 2:
                    dve.wait_ge(prod_ok, m - 1)
                step(dve.tensor_scalar(dst, src[:, 0:SEQ], convw(0, m), col(g, "conv_b_2")[:, m:m + 1], ALU.mult, ALU.add))
                step(dve.scalar_tensor_tensor(out=dst, in0=src[:, 1:SEQ + 1], scalar=convw(1, m), in1=dst, op0=ALU.mult, op1=ALU.add))
                dve.scalar_tensor_tensor(out=dst, in0=src[:, 2:SEQ + 2], scalar=convw(2, m), in1=dst, op0=ALU.mult,
                                         op1=ALU.add).then_inc(conv_ok, 1)

            def product(m):
                dve.wait_ge(act_ok, m + 1)
                dve.wait_ge(ready, 3 * m + 3)
                dve.tensor_tensor(prodT[:, m, :], y[:, m % 2, :], psum[:, BANKS[(3 * m + 2) % 6], :], ALU.mult).then_inc(prod_ok, 1)

            for m in range(FM):
                conv(m)
                if m:
                    product(m - 1)
            product(FM - 1)
            dve.wait_ge(loads, 16)
            for t in range(TT):
                if t:
                    dve.wait_ge(post.added, t)
                post.dve(dve, step, t, (2 * t, 2 * t + 1), gain, part)

        @block.sync
        def _(sp):
            sp.dma_start(gain, a["norm_ffn_post_2"].to_broadcast([P, D])).then_inc(loads, 16)
            later.load_until(sp, len(later.chunks))
            for t in range(TT):
                sp.wait_ge(post.added, t + 1)
                sp.dma_start(g["out"][0, t * P:(t + 1) * P, :], res[:, t, :]).then_inc(stored, 16)
            sp.wait_ge(stored, 16 * TT)
    later.new_phase()


def second_block(g):
    stick_breaking(g)
    gated_linear(g)
    mix_and_project(g)
    feed_forward(g)


_INS = ["x", "c", "w_mod", "b_mod", "g_norm1", "w_in", "conv_w", "conv_b", "conv_ln_g", "conv_ln_b", "w_out", "g_norm2",
        "w_router_group", "b_router_group", "w_router_expert", "b_router_expert", "w_exp_gate", "w_exp_up", "w_exp_down",
        "g_final", "meta_tokens_2", "norm_mix_pre_2", "w_in_2", "w_gk_up_2", "b_gk_2", "gla_head_norm_2", "w_sb_out_2",
        "w_gla_out_2", "w_o_2", "norm_mix_post_2", "norm_ffn_pre_2", "w_ffn_up_2", "w_ffn_gate_2", "conv_w_2", "conv_b_2",
        "w_ffn_down_2", "norm_ffn_post_2"]


def kernel(**inputs):
    import numpy as _np
    import concourse.bacc as _bacc
    from concourse import mybir as _mybir
    from concourse.bass_utils import run_bass_kernel_spmd as _run

    nc = _bacc.Bacc("TRN2", target_bir_lowering=False, num_devices=1)
    arrays, args = {}, {}
    for name in _INS:
        x = _np.ascontiguousarray(inputs[name])
        arrays[f"in_{name}_dram"] = x
        args[name] = nc.dram_tensor(f"in_{name}_dram", x.shape, _mybir.dt.from_np(x.dtype), kind="ExternalInput").ap()
    out = nc.dram_tensor("out_0_dram", (1, SEQ, D), _mybir.dt.float32, kind="ExternalOutput").ap()
    build_program(nc, args, out)
    r = _run(nc, [arrays], core_ids=[0])
    return r.results[0]["out_0_dram"]
```
